# Optimizing a Trainium2 kernel written in Bass

```python
import jax, jax.numpy as jnp
from jax import lax
import numpy as np

D_MODEL = 1024
BATCH = 1
SEQ = 512
DEPTH = 2

CHUNK = 64
N_MIXERS = 2
N_A_LAYERS = (DEPTH + 1) // 2
N_B_LAYERS = DEPTH // 2

SGU_CHUNK = 2 * CHUNK
SGU_HALF = D_MODEL
SGU_GROUPS = 16
SGU_GROUP_DIM = SGU_HALF // SGU_GROUPS

RWKV_HEAD_DIM = 64
RWKV_HEADS = D_MODEL // RWKV_HEAD_DIM
DECAY_LORA = 64
AAA_LORA = 64
GATE_LORA = 160
GN_EPS = 64e-5
N_SHIFT_MIX = 6

FFN_DIM = 2816
CONV_WIDTH = 3
RMS_EPS = 1e-6


def rms_norm(x, g):
    xf = x.astype(jnp.float32)
    y = xf * lax.rsqrt(jnp.mean(xf * xf, axis=-1, keepdims=True) + RMS_EPS)
    return (y * g.astype(jnp.float32)).astype(x.dtype)

def sgu_mixer(h, w_in, b_in, g_v, w_s, b_s, w_out):
    B, S, _ = h.shape
    z = jax.nn.gelu(h @ w_in + b_in, approximate=False)
    u, v = jnp.split(z, 2, axis=-1)
    v = rms_norm(v, g_v)
    n_blk = S // SGU_CHUNK
    v = v.reshape(B, n_blk, SGU_CHUNK, SGU_GROUPS, SGU_GROUP_DIM)
    causal = jnp.tril(jnp.ones((SGU_CHUNK, SGU_CHUNK), dtype=bool))
    w_causal = jnp.where(causal[None], w_s, 0)
    v = jnp.einsum('gts,bnsgc->bntgc', w_causal, v) + b_s.T[None, None, :, :, None]
    y = u * v.reshape(B, S, SGU_HALF)
    return y @ w_out

def token_shift(x):
    return jnp.pad(x, ((0, 0), (1, 0), (0, 0)))[:, :-1]

def wkv7_scan(r, w, k, v, a, b):
    B, S, H, N = r.shape

    def step(state, inp):
        r_t, w_t, k_t, v_t, a_t, b_t = inp
        sa = jnp.einsum('bhvk,bhk->bhv', state, a_t)
        state = (state * w_t[:, :, None, :]
                 + sa[..., None] * b_t[:, :, None, :]
                 + v_t[..., None] * k_t[:, :, None, :])
        y_t = jnp.einsum('bhvk,bhk->bhv', state, r_t)
        return state, y_t

    xs = tuple(jnp.swapaxes(t, 0, 1) for t in (r, w, k, v, a, b))
    s0 = jnp.zeros((B, H, N, N), jnp.float32)
    _, ys = lax.scan(step, s0, xs)
    return jnp.swapaxes(ys, 0, 1)

def rwkv7_mixer(h, mu, w_r, w_k, w_v, w_o, w0, w1, w2, a0, a1, a2,
                g1, g2, k_k, k_a, r_k, ln_w, ln_b):
    B, S, D = h.shape
    H, N = RWKV_HEADS, RWKV_HEAD_DIM
    f32 = jnp.float32
    xx = token_shift(h) - h
    xr = h + xx * mu[0]
    xw = h + xx * mu[1]
    xk = h + xx * mu[2]
    xv = h + xx * mu[3]
    xa = h + xx * mu[4]
    xg = h + xx * mu[5]
    r = xr @ w_r
    k = xk @ w_k
    v = xv @ w_v
    w = -jax.nn.softplus(-(w0 + jnp.tanh(xw @ w1) @ w2)) - 0.5
    a = jax.nn.sigmoid(a0 + (xa @ a1) @ a2)
    g = jax.nn.sigmoid(xg @ g1) @ g2

    def heads(t):
        return t.reshape(B, S, H, N).astype(f32)

    kk = heads(k * k_k)
    kk = kk * lax.rsqrt(jnp.maximum(jnp.sum(kk * kk, -1, keepdims=True), 1e-24))
    k = k * (1 + (a - 1) * k_a)
    r_h, k_h, v_h, a_h = heads(r), heads(k), heads(v), heads(a)
    decay = jnp.exp(-jnp.exp(heads(w)))
    y = wkv7_scan(r_h, decay, k_h, v_h, -kk, kk * a_h)
    mean = jnp.mean(y, -1, keepdims=True)
    var = jnp.mean(jnp.square(y - mean), -1, keepdims=True)
    y = ((y - mean) * lax.rsqrt(var + GN_EPS)).reshape(B, S, D)
    y = y * ln_w.astype(f32) + ln_b.astype(f32)
    bonus = jnp.sum(r_h * k_h * r_k.astype(f32), -1, keepdims=True) * v_h
    y = (y + bonus.reshape(B, S, D)).astype(h.dtype)
    return (y * g) @ w_o

def conv_ffn(h, w_up, conv_w, conv_b, w_down):
    S = h.shape[1]
    z = h @ w_up
    zp = jnp.pad(z, ((0, 0), (CONV_WIDTH - 1, 0), (0, 0)))
    z = sum(zp[:, j:j + S] * conv_w[j] for j in range(CONV_WIDTH)) + conv_b
    gate, val = jnp.split(z, 2, axis=-1)
    return (jax.nn.silu(gate) * val) @ w_down

def first_inputs(seed: int = 0) -> dict:
    key = jax.random.key(seed)
    ks = iter(jax.random.split(key, 40))
    f32 = jnp.float32

    def nrm(shape, scale):
        return jax.random.normal(next(ks), shape, f32) * scale

    def gain(shape):
        return 1.0 + 0.05 * jax.random.normal(next(ks), shape, f32)

    D, NA, NB = D_MODEL, N_A_LAYERS, N_B_LAYERS
    H2, F2 = 2 * SGU_HALF, 2 * FFN_DIM
    return {
        "x": nrm((BATCH, SEQ, D), 1.0),
        "norm_mix_g": gain((DEPTH, D)),
        "norm_ffn_g": gain((DEPTH, D)),
        "norm_final_g": gain((D,)),
        "sgu_w_in": nrm((NA, D, H2), D ** -0.5),
        "sgu_b_in": nrm((NA, H2), 0.02),
        "sgu_g_v": gain((NA, SGU_HALF)),
        "sgu_w_s": nrm((NA, SGU_GROUPS, SGU_CHUNK, SGU_CHUNK), 0.5 * SGU_CHUNK ** -0.5),
        "sgu_b_s": gain((NA, SGU_GROUPS, SGU_CHUNK)),
        "sgu_w_out": nrm((NA, SGU_HALF, D), SGU_HALF ** -0.5),
        "rwkv_mu": jax.random.uniform(next(ks), (NB, N_SHIFT_MIX, D), f32),
        "rwkv_w_r": nrm((NB, D, D), D ** -0.5),
        "rwkv_w_k": nrm((NB, D, D), D ** -0.5),
        "rwkv_w_v": nrm((NB, D, D), D ** -0.5),
        "rwkv_w_o": nrm((NB, D, D), D ** -0.5),
        "rwkv_w0": jax.random.uniform(next(ks), (NB, D), f32, minval=-6.0, maxval=-1.0),
        "rwkv_w1": nrm((NB, D, DECAY_LORA), 0.1 * D ** -0.5),
        "rwkv_w2": nrm((NB, DECAY_LORA, D), 0.1 * DECAY_LORA ** -0.5),
        "rwkv_a0": nrm((NB, D), 0.1),
        "rwkv_a1": nrm((NB, D, AAA_LORA), 0.1 * D ** -0.5),
        "rwkv_a2": nrm((NB, AAA_LORA, D), 0.1 * AAA_LORA ** -0.5),
        "rwkv_g1": nrm((NB, D, GATE_LORA), D ** -0.5),
        "rwkv_g2": nrm((NB, GATE_LORA, D), GATE_LORA ** -0.5),
        "rwkv_k_k": 0.85 + 0.05 * jax.random.normal(next(ks), (NB, D), f32),
        "rwkv_k_a": gain((NB, D)),
        "rwkv_r_k": nrm((NB, RWKV_HEADS, RWKV_HEAD_DIM), 0.1),
        "rwkv_ln_w": gain((NB, D)),
        "rwkv_ln_b": nrm((NB, D), 0.02),
        "ffn_w_up": nrm((DEPTH, D, F2), D ** -0.5),
        "ffn_conv_w": nrm((DEPTH, CONV_WIDTH, F2), CONV_WIDTH ** -0.5),
        "ffn_conv_b": nrm((DEPTH, F2), 0.02),
        "ffn_w_down": nrm((DEPTH, FFN_DIM, D), FFN_DIM ** -0.5),
    }

def first_block(x, norm_mix_g, norm_ffn_g, norm_final_g,
              sgu_w_in, sgu_b_in, sgu_g_v, sgu_w_s, sgu_b_s, sgu_w_out,
              rwkv_mu, rwkv_w_r, rwkv_w_k, rwkv_w_v, rwkv_w_o,
              rwkv_w0, rwkv_w1, rwkv_w2, rwkv_a0, rwkv_a1, rwkv_a2,
              rwkv_g1, rwkv_g2, rwkv_k_k, rwkv_k_a, rwkv_r_k, rwkv_ln_w, rwkv_ln_b,
              ffn_w_up, ffn_conv_w, ffn_conv_b, ffn_w_down):
    h = x
    for i in range(DEPTH):
        hn = rms_norm(h, norm_mix_g[i])
        j = i // N_MIXERS
        if i % N_MIXERS == 0:
            h = h + sgu_mixer(hn, sgu_w_in[j], sgu_b_in[j], sgu_g_v[j],
                              sgu_w_s[j], sgu_b_s[j], sgu_w_out[j])
        else:
            h = h + rwkv7_mixer(hn, rwkv_mu[j], rwkv_w_r[j], rwkv_w_k[j], rwkv_w_v[j], rwkv_w_o[j],
                                rwkv_w0[j], rwkv_w1[j], rwkv_w2[j],
                                rwkv_a0[j], rwkv_a1[j], rwkv_a2[j],
                                rwkv_g1[j], rwkv_g2[j], rwkv_k_k[j], rwkv_k_a[j], rwkv_r_k[j],
                                rwkv_ln_w[j], rwkv_ln_b[j])
        h = h + conv_ffn(rms_norm(h, norm_ffn_g[i]), ffn_w_up[i], ffn_conv_w[i],
                         ffn_conv_b[i], ffn_w_down[i])
    return rms_norm(h, norm_final_g)


DEPTH_2 = 1

GRID_W = 64
WIN_H_MAX = 8
WIN_W = 16
ATTN_HEADS = 8
ATTN_HEAD_DIM = 64
ATTN_WIDTH = ATTN_HEADS * ATTN_HEAD_DIM
DN_HEADS = 4
DN_HEAD_DIM = 128
DN_WIDTH = DN_HEADS * DN_HEAD_DIM
DN_CONV = 5
DN_CHUNK = 64
D_MIX = ATTN_WIDTH + DN_WIDTH
IN_COLS = 3 * ATTN_WIDTH + 4 * DN_WIDTH + 4 * DN_HEADS
N_GROUPS = 8
EXPERTS_PER_GROUP = 8
N_EXPERTS = N_GROUPS * EXPERTS_PER_GROUP
TOP_K_IN_GROUP = 2
D_EXPERT = D_MODEL // 4
MOE_BLOCK = 256
EPS = 1e-6


def rms_norm_2(x, g):
    xf = x.astype(jnp.float32)
    y = xf * lax.rsqrt(jnp.mean(xf * xf, axis=-1, keepdims=True) + EPS)
    return (y * g.astype(jnp.float32)).astype(x.dtype)

def l2_norm(x):
    xf = x.astype(jnp.float32)
    return xf * lax.rsqrt(jnp.sum(xf * xf, axis=-1, keepdims=True) + EPS)

def neighbourhood_attention(q, k, v, rpb):
    b_, s_, h_, dh = q.shape
    rows = s_ // GRID_W
    kh = min(WIN_H_MAX, rows)
    to_grid = lambda t: t.reshape(b_, rows, GRID_W, h_, dh).transpose(1, 0, 3, 2, 4)
    qg, kg, vg = to_grid(q), to_grid(k), to_grid(v)
    cols = jnp.arange(GRID_W)
    col_start = jnp.clip(cols - WIN_W // 2, 0, GRID_W - WIN_W)
    col_idx = col_start[:, None] + jnp.arange(WIN_W)[None, :]
    col_off = col_idx - cols[:, None] + (WIN_W - 1)
    scale = dh ** -0.5

    def row_block(args):
        r, q_row = args
        r0 = jnp.clip(r - kh // 2, 0, rows - kh)
        k_band = lax.dynamic_slice_in_dim(kg, r0, kh, axis=0)
        v_band = lax.dynamic_slice_in_dim(vg, r0, kh, axis=0)
        k_win = k_band[:, :, :, col_idx]
        v_win = v_band[:, :, :, col_idx]
        row_off = r0 + jnp.arange(kh) - r + (WIN_H_MAX - 1)
        bias = rpb[:, row_off[None, :, None], col_off[:, None, :]]
        logits = jnp.einsum('bhqd,rbhqcd->bhqrc', q_row, k_win).astype(jnp.float32) * scale
        logits = logits + bias.astype(jnp.float32)[None]
        p = jax.nn.softmax(logits.reshape(b_, h_, GRID_W, kh * WIN_W), axis=-1)
        p = p.reshape(b_, h_, GRID_W, kh, WIN_W).astype(v.dtype)
        return jnp.einsum('bhqrc,rbhqce->bqhe', p, v_win)

    out = lax.map(row_block, (jnp.arange(rows), qg))
    return out.transpose(1, 0, 2, 3, 4).reshape(b_, s_, h_ * dh)

def gated_delta_rule(q, k, v, g, beta):
    f32 = jnp.float32
    bn, hn, t_, dk = q.shape
    dv = v.shape[-1]
    c = DN_CHUNK
    nc = t_ // c
    q = q.astype(f32).reshape(bn, hn, nc, c, dk)
    k = k.astype(f32).reshape(bn, hn, nc, c, dk)
    v = v.astype(f32).reshape(bn, hn, nc, c, dv)
    beta = beta.astype(f32).reshape(bn, hn, nc, c)
    gc = jnp.cumsum(g.astype(f32).reshape(bn, hn, nc, c), axis=-1)
    incl = jnp.tril(jnp.ones((c, c), bool))
    strict = jnp.tril(jnp.ones((c, c), bool), -1)
    diff = gc[..., :, None] - gc[..., None, :]
    decay = jnp.where(incl, jnp.exp(jnp.where(incl, diff, 0.0)), 0.0)
    kb = k * beta[..., None]
    lower = jnp.where(strict, jnp.einsum('bhnid,bhnjd->bhnij', kb, k) * decay, 0.0)
    a_mat = jnp.eye(c, dtype=f32) + lower
    rhs = jnp.concatenate([v * beta[..., None], kb * jnp.exp(gc)[..., None]], axis=-1)
    sol = lax.linalg.triangular_solve(a_mat, rhs, left_side=True, lower=True, unit_diagonal=True)
    u, w = sol[..., :dv], sol[..., dv:]
    qk = jnp.einsum('bhnid,bhnjd->bhnij', q, k) * decay

    def step(state, inp):
        q_c, k_c, u_c, w_c, g_c, qk_c = inp
        v_new = u_c - jnp.einsum('bhck,bhkv->bhcv', w_c, state)
        o_c = (jnp.einsum('bhck,bhkv->bhcv', q_c * jnp.exp(g_c)[..., None], state)
               + jnp.einsum('bhij,bhjv->bhiv', qk_c, v_new))
        g_last = g_c[..., -1:]
        state = (state * jnp.exp(g_last)[..., None]
                 + jnp.einsum('bhck,bhcv->bhkv', k_c * jnp.exp(g_last - g_c)[..., None], v_new))
        return state, o_c

    xs = tuple(jnp.moveaxis(t, 2, 0) for t in (q, k, u, w, gc, qk))
    state0 = jnp.zeros((bn, hn, dk, dv), f32)
    _, o = lax.scan(step, state0, xs)
    return jnp.moveaxis(o, 0, 2).reshape(bn, hn, t_, dv)

def bidirectional_gated_deltanet(qkv_raw, z, a, b, conv_w, a_log, dt_bias, out_norm_g):
    b_, s_, _ = qkv_raw.shape
    qkv = lax.conv_general_dilated(qkv_raw, conv_w[:, None, :].astype(qkv_raw.dtype),
                                   window_strides=(1,), padding=[(DN_CONV // 2, DN_CONV // 2)],
                                   dimension_numbers=('NWC', 'WIO', 'NWC'),
                                   feature_group_count=3 * DN_WIDTH)
    qkv = jax.nn.silu(qkv)
    q, k, v = jnp.split(qkv.reshape(b_, s_, 3, DN_HEADS, DN_HEAD_DIM), 3, axis=2)
    q = l2_norm(q[:, :, 0]) * (DN_HEAD_DIM ** -0.5)
    k = l2_norm(k[:, :, 0])
    v = v[:, :, 0].astype(jnp.float32)
    g = -jnp.exp(a_log.astype(jnp.float32)) * jax.nn.softplus(a.astype(jnp.float32) + dt_bias.astype(jnp.float32))
    beta = jax.nn.sigmoid(b.astype(jnp.float32))
    bht = lambda t: t.transpose(0, 2, 1, 3)
    both = lambda t: jnp.concatenate([t, jnp.flip(t, axis=2)], axis=1)
    q2, k2, v2 = both(bht(q)), both(bht(k)), both(bht(v))
    g2 = jnp.concatenate([g[:, :, 0].transpose(0, 2, 1), jnp.flip(g[:, :, 1].transpose(0, 2, 1), axis=-1)], axis=1)
    beta2 = jnp.concatenate([beta[:, :, 0].transpose(0, 2, 1), jnp.flip(beta[:, :, 1].transpose(0, 2, 1), axis=-1)], axis=1)
    o2 = gated_delta_rule(q2, k2, v2, g2, beta2)
    o = o2[:, :DN_HEADS] + jnp.flip(o2[:, DN_HEADS:], axis=2)
    o = o.transpose(0, 2, 1, 3)
    zf = z.reshape(b_, s_, DN_HEADS, DN_HEAD_DIM).astype(jnp.float32)
    o = rms_norm_2(o, out_norm_g) * jax.nn.silu(zf)
    return o.reshape(b_, s_, DN_WIDTH).astype(qkv_raw.dtype)

def hierarchical_moe(h, wg_r, bg_r, we_r, be_r, w_gate, w_up, w_down):
    b_, s_, d_ = h.shape
    n = b_ * s_
    hf = h.reshape(n, d_)
    group_logits = (hf @ wg_r + bg_r).astype(jnp.float32)
    group_prob = jax.nn.softmax(group_logits, axis=-1)
    gsel = jnp.argmax(group_logits, axis=-1)
    gp = jnp.take_along_axis(group_prob, gsel[:, None], axis=-1)
    exp_logits = (hf @ we_r + be_r).astype(jnp.float32).reshape(n, N_GROUPS, EXPERTS_PER_GROUP)
    in_group = jnp.take_along_axis(exp_logits, gsel[:, None, None], axis=1)[:, 0]
    top_val, top_idx = lax.top_k(in_group, TOP_K_IN_GROUP)
    gates = gp * jax.nn.softmax(top_val, axis=-1)
    eid = (gsel[:, None] * EXPERTS_PER_GROUP + top_idx).reshape(-1).astype(jnp.int32)
    gate_flat = gates.reshape(-1)
    tok_flat = jnp.repeat(jnp.arange(n, dtype=jnp.int32), TOP_K_IN_GROUP)
    nk = n * TOP_K_IN_GROUP
    p_rows = -(-nk // MOE_BLOCK) * MOE_BLOCK + N_EXPERTS * MOE_BLOCK
    nb = p_rows // MOE_BLOCK
    order = jnp.argsort(eid)
    e_sorted = eid[order]
    counts = jnp.bincount(eid, length=N_EXPERTS)
    starts = jnp.cumsum(counts) - counts
    padded = -(-counts // MOE_BLOCK) * MOE_BLOCK
    pends = jnp.cumsum(padded)
    pstarts = pends - padded
    dest = pstarts[e_sorted] + (jnp.arange(nk) - starts[e_sorted])
    buf_tok = jnp.full((p_rows,), n, jnp.int32).at[dest].set(tok_flat[order])
    buf_gate = jnp.zeros((p_rows,), jnp.float32).at[dest].set(gate_flat[order])
    block_expert = jnp.clip(jnp.searchsorted(pends, jnp.arange(nb) * MOE_BLOCK, side='right'),
                            0, N_EXPERTS - 1).astype(jnp.int32)
    h_pad = jnp.concatenate([hf, jnp.zeros((1, d_), hf.dtype)], axis=0)

    def expert_block(args):
        tok, e = args
        xb = h_pad[tok]
        hid = jax.nn.silu(xb @ w_gate[e]) * (xb @ w_up[e])
        return hid @ w_down[e]

    out = lax.map(expert_block, (buf_tok.reshape(nb, MOE_BLOCK), block_expert))
    out = (out.reshape(p_rows, d_).astype(jnp.float32) * buf_gate[:, None]).astype(h.dtype)
    y = jnp.zeros((n + 1, d_), h.dtype).at[buf_tok].add(out)[:n]
    return y.reshape(b_, s_, d_)

def hybrid_layer(x, ln1_g, w_in, q_norm_g, k_norm_g, rpb, attn_out_g, conv_w, a_log, dt_bias,
                 dn_out_g, w_out, ln2_g, wg_r, bg_r, we_r, be_r, w_gate, w_up, w_down):
    b_, s_, _ = x.shape
    h = rms_norm_2(x, ln1_g)
    proj = h @ w_in
    a3 = 3 * ATTN_WIDTH
    aq, ak, av, dqkv, dz, dab = jnp.split(
        proj, [ATTN_WIDTH, 2 * ATTN_WIDTH, a3, a3 + 3 * DN_WIDTH, a3 + 4 * DN_WIDTH], axis=-1)
    hs = lambda t: t.reshape(b_, s_, ATTN_HEADS, ATTN_HEAD_DIM)
    aq = rms_norm_2(hs(aq), q_norm_g)
    ak = rms_norm_2(hs(ak), k_norm_g)
    attn = rms_norm_2(neighbourhood_attention(aq, ak, hs(av), rpb), attn_out_g)
    dab = dab.reshape(b_, s_, 2, 2, DN_HEADS)
    dn = bidirectional_gated_deltanet(dqkv, dz, dab[:, :, 0], dab[:, :, 1], conv_w, a_log,
                                      dt_bias, dn_out_g)
    x = x + jnp.concatenate([attn, dn], axis=-1) @ w_out
    x = x + hierarchical_moe(rms_norm_2(x, ln2_g), wg_r, bg_r, we_r, be_r, w_gate, w_up, w_down)
    return x

def second_inputs(seed: int = 0) -> dict:
    key = jax.random.key(seed)
    ks = jax.random.split(key, 24)
    f32 = jnp.float32
    nrm = lambda k, shape, s: jax.random.normal(k, shape, f32) * s
    gain = lambda k, shape: 1.0 + 0.01 * jax.random.normal(k, shape, f32)
    L = DEPTH_2
    dt = jnp.exp(jax.random.uniform(ks[9], (L, 2, DN_HEADS), f32, np.log(1e-3), np.log(1e-1)))
    return {
        'x': nrm(ks[0], (BATCH, SEQ, D_MODEL), 1.0),
        'ln1_g': gain(ks[1], (L, D_MODEL)),
        'w_in': nrm(ks[2], (L, D_MODEL, IN_COLS), D_MODEL ** -0.5),
        'attn_q_norm_g': gain(ks[3], (L, ATTN_HEAD_DIM)),
        'attn_k_norm_g': gain(ks[4], (L, ATTN_HEAD_DIM)),
        'attn_rpb': nrm(ks[5], (L, ATTN_HEADS, 2 * WIN_H_MAX - 1, 2 * WIN_W - 1), 0.1),
        'attn_out_norm_g': gain(ks[6], (L, ATTN_WIDTH)),
        'dn_conv_w': nrm(ks[7], (L, DN_CONV, 3 * DN_WIDTH), DN_CONV ** -0.5),
        'dn_a_log': jnp.log(jax.random.uniform(ks[8], (L, 2, DN_HEADS), f32, 1.0, 16.0)),
        'dn_dt_bias': dt + jnp.log(-jnp.expm1(-dt)),
        'dn_out_norm_g': gain(ks[10], (L, DN_HEAD_DIM)),
        'w_out': nrm(ks[11], (L, D_MIX, D_MODEL), D_MIX ** -0.5),
        'ln2_g': gain(ks[12], (L, D_MODEL)),
        'router_group_w': nrm(ks[13], (L, D_MODEL, N_GROUPS), D_MODEL ** -0.5),
        'router_group_b': nrm(ks[14], (L, N_GROUPS), 0.01),
        'router_expert_w': nrm(ks[15], (L, D_MODEL, N_EXPERTS), D_MODEL ** -0.5),
        'router_expert_b': nrm(ks[16], (L, N_EXPERTS), 0.01),
        'expert_w_gate': nrm(ks[17], (L, N_EXPERTS, D_MODEL, D_EXPERT), D_MODEL ** -0.5),
        'expert_w_up': nrm(ks[18], (L, N_EXPERTS, D_MODEL, D_EXPERT), D_MODEL ** -0.5),
        'expert_w_down': nrm(ks[19], (L, N_EXPERTS, D_EXPERT, D_MODEL), D_EXPERT ** -0.5),
    }

def second_block(x, ln1_g, w_in, attn_q_norm_g, attn_k_norm_g, attn_rpb, attn_out_norm_g, dn_conv_w,
              dn_a_log, dn_dt_bias, dn_out_norm_g, w_out, ln2_g, router_group_w, router_group_b,
              router_expert_w, router_expert_b, expert_w_gate, expert_w_up, expert_w_down):
    for l in range(DEPTH_2):
        x = hybrid_layer(x, ln1_g[l], w_in[l], attn_q_norm_g[l], attn_k_norm_g[l], attn_rpb[l],
                         attn_out_norm_g[l], dn_conv_w[l], dn_a_log[l], dn_dt_bias[l],
                         dn_out_norm_g[l], w_out[l], ln2_g[l], router_group_w[l], router_group_b[l],
                         router_expert_w[l], router_expert_b[l], expert_w_gate[l], expert_w_up[l],
                         expert_w_down[l])
    return x


def setup_inputs(seed=0):
    out = dict(first_inputs(seed))
    for name, value in second_inputs(seed + 1).items():
        if name != "x":
            out[name + "_2"] = value
    return out


def reference(
    x, norm_mix_g, norm_ffn_g, norm_final_g, sgu_w_in, sgu_b_in, sgu_g_v, sgu_w_s, sgu_b_s,
    sgu_w_out, rwkv_mu, rwkv_w_r, rwkv_w_k, rwkv_w_v, rwkv_w_o, rwkv_w0, rwkv_w1, rwkv_w2,
    rwkv_a0, rwkv_a1, rwkv_a2, rwkv_g1, rwkv_g2, rwkv_k_k, rwkv_k_a, rwkv_r_k, rwkv_ln_w,
    rwkv_ln_b, ffn_w_up, ffn_conv_w, ffn_conv_b, ffn_w_down, ln1_g_2, w_in_2, attn_q_norm_g_2,
    attn_k_norm_g_2, attn_rpb_2, attn_out_norm_g_2, dn_conv_w_2, dn_a_log_2, dn_dt_bias_2,
    dn_out_norm_g_2, w_out_2, ln2_g_2, router_group_w_2, router_group_b_2, router_expert_w_2,
    router_expert_b_2, expert_w_gate_2, expert_w_up_2, expert_w_down_2,
):
    x = first_block(
        x, norm_mix_g, norm_ffn_g, norm_final_g, sgu_w_in, sgu_b_in, sgu_g_v, sgu_w_s, sgu_b_s,
        sgu_w_out, rwkv_mu, rwkv_w_r, rwkv_w_k, rwkv_w_v, rwkv_w_o, rwkv_w0, rwkv_w1, rwkv_w2,
        rwkv_a0, rwkv_a1, rwkv_a2, rwkv_g1, rwkv_g2, rwkv_k_k, rwkv_k_a, rwkv_r_k, rwkv_ln_w,
        rwkv_ln_b, ffn_w_up, ffn_conv_w, ffn_conv_b, ffn_w_down,
    )
    return second_block(
        x, ln1_g_2, w_in_2, attn_q_norm_g_2, attn_k_norm_g_2, attn_rpb_2, attn_out_norm_g_2,
        dn_conv_w_2, dn_a_log_2, dn_dt_bias_2, dn_out_norm_g_2, w_out_2, ln2_g_2,
        router_group_w_2, router_group_b_2, router_expert_w_2, router_expert_b_2,
        expert_w_gate_2, expert_w_up_2, expert_w_down_2,
    )


_drawn_inputs = setup_inputs


def setup_inputs(seed=0):
    import zlib

    import numpy as np

    out = dict(_drawn_inputs(seed))
    spreads = {}
    factors = {'sgu_g_v': 3.198,
     'rwkv_w1': 8.0,
     'rwkv_w2': 8.0,
     'rwkv_a1': 8.0,
     'rwkv_a2': 8.0,
     'rwkv_ln_b': 2.775,
     'ln1_g_2': 3.812,
     'attn_q_norm_g_2': 7.062,
     'attn_k_norm_g_2': 7.128,
     'attn_out_norm_g_2': 15.359,
     'dn_out_norm_g_2': 7.665,
     'ln2_g_2': 4.716,
     'router_group_b_2': 22.301,
     'router_expert_b_2': 16.935}
    for name, (base, spread) in spreads.items():
        noise = np.random.default_rng([zlib.crc32(name.encode()), seed]).standard_normal(out[name].shape)
        drawn = base * np.exp(spread * noise) if base else spread * noise
        out[name] = __import__('jax').numpy.asarray(drawn.astype(out[name].dtype))
    for name, factor in factors.items():
        out[name] = (out[name] * factor).astype(out[name].dtype)
    return out
```

```python
from contextlib import ExitStack, contextmanager

import numpy as np

import concourse.bass as bass
from concourse import mybir

F32 = mybir.dt.float32
F32R = mybir.dt.float32r
I32 = mybir.dt.int32
ALU = mybir.AluOpType
ACT = mybir.ActivationFunctionType
AX = mybir.AxisListType
MUL, ADD, SUB, MAX, MIN = ALU.mult, ALU.add, ALU.subtract, ALU.max, ALU.min

S = 512
D = 1024
KT = 8
FF = 2816
FT = FF // 128
NOV = 16
NP = (64 + NOV) // 2
ROWS = NP * 128
NOWHERE = 1 << 20


class Engine:

    def __init__(self, sem):
        self.sem, self.n, self.list, self.met, self.sent = sem, 0, [], {}, []

    def wait(self, *tokens):
        for t in tokens:
            if not t:
                continue
            if isinstance(t, list):
                self.wait(*t)
                continue
            sem, value = t
            if self.met.get(sem.num, 0) < value:
                self.met[sem.num] = value
                self.list.append(lambda e, s=sem, v=value: e.wait_ge(s, v))

    def put(self, f, w=(), inc=True):
        self.wait(*w)
        if not inc:
            self.list.append(f)
            return None
        self.n += 1
        self.list.append(lambda e, f=f: f(e).then_inc(self.sem, 1))
        return (self.sem, self.n)

    def now(self):
        return (self.sem, self.n) if self.n else None


class Banks:

    def __init__(self, ids, free):
        self.ids, self.free, self.i = ids, free, -1

    def take(self):
        self.i = (self.i + 1) % len(self.ids)
        b = self.ids[self.i]
        return b, None, self.free[b]


class Slots:

    def __init__(self, bufs):
        self.bufs, self.free, self.i = bufs, [[] for _ in bufs], -1

    def take(self):
        self.i = (self.i + 1) % len(self.bufs)
        return self.i, self.bufs[self.i], self.free[self.i]


PARAMS = {}


def param_columns():
    if PARAMS:
        return PARAMS
    at = 0
    for name, n in (("mixg", 16), ("ffng", 16), ("fing", 8), ("ln1", 8), ("ln2", 8), ("bu", 8),
                    ("mu", 48), ("w0", 8), ("a0", 8), ("kk", 8), ("ka", 8), ("rk", 8), ("lnw", 8), ("lnb", 8),
                    ("cw", 2 * 3 * 44), ("cb", 2 * 44), ("dncw", 5 * 12), ("qg", 1), ("kg", 1), ("aog", 4), ("dng", 1),
                    ("eps", 1), ("gneps", 1), ("zero", 1), ("one", 1)):
        PARAMS[name] = at
        at += n
    PARAMS["n"] = at
    return PARAMS


CONSTS = {}


def const_columns():
    if CONSTS:
        return CONSTS
    at = 0
    for name, n in (("ident", 128), ("ones", 128), ("blk", 128), ("i2", 64), ("up", 384), ("lo", 384),
                    ("incu", 64), ("stru", 64), ("incl", 64), ("strl", 64), ("cumf", 128), ("cumb", 128),
                    ("half", 256), ("tri", 128), ("iota8", 8), ("iota64", 64), ("iota16", NOV), ("slot64", 64), ("slot16", NOV), ("gidx", 1)):
        CONSTS[name] = at
        at += n
    CONSTS["n"] = at
    return CONSTS


def constants():
    c = const_columns()
    out = np.zeros((128, c["n"]), np.float32)

    def put(name, a):
        out[:, c[name]:c[name] + a.shape[1]] = a

    p = np.arange(128)[:, None]
    j = np.arange(64)[None, :]
    q = p % 64
    t = np.arange(128)[None, :]
    put("ident", np.eye(128))
    put("ones", np.ones((128, 128)))
    put("blk", (p // 64 == t // 64) * 1.0)
    put("i2", (q == j) * 1.0)
    for l in range(6):
        b = 2 << l
        same = (q // b == j // b)
        up = same & (q % b < b // 2) & (j % b >= b // 2)
        lo = same & (q % b >= b // 2) & (j % b < b // 2)
        out[:, c["up"] + 64 * l:c["up"] + 64 * l + 64] = up
        out[:, c["lo"] + 64 * l:c["lo"] + 64 * l + 64] = lo
    put("incu", (q <= j) * 1.0)
    put("stru", (q < j) * 1.0)
    put("incl", (q >= j) * 1.0)
    put("strl", (q > j) * 1.0)
    put("cumf", ((p // 64 == t // 64) & (p <= t)) * 1.0)
    put("cumb", ((p // 64 == t // 64) & (p >= t)) * 1.0)
    put("half", np.concatenate([np.repeat(p < 64, 128, 1), np.repeat(p >= 64, 128, 1)], 1) * 1.0)
    put("tri", (p < t) * 1.0)
    put("iota8", np.repeat(np.arange(8)[None], 128, 0))
    put("iota64", np.repeat(np.arange(64)[None], 128, 0))
    put("iota16", np.repeat(np.arange(NOV)[None], 128, 0))
    b = np.arange(2 * NP)[None]
    slot = np.repeat(b % 2 * 64 * NP + b // 2, 128, 0)
    put("slot64", slot[:, 0:64])
    put("slot16", slot[:, 64:])
    put("gidx", p * 1.0)
    return out


class Program:
    def __init__(self, nc, ctx, A):
        self.nc, self.ctx, self.A = nc, ctx, A
        self.nsem = 0
        self.pe, self.dve, self.act, self.pool, self.sp = (Engine(self.sem(x)) for x in ("s_pe", "s_dve", "s_act", "s_pool", "s_sp"))
        self.counts = {}
        self.stores = []
        self.ps = ctx.enter_context(nc.psum_tensor("ps", [128, 8, 512], F32))
        self.at = 16512 - 16512 % 32 + 32
        self.end = 229344

    def sem(self, name):
        return self.ctx.enter_context(self.nc.semaphore(name))

    def place(self, name, shape, dt, offset):
        n = 4
        for x in shape[1:]:
            n *= x
        n += -n % 32
        assert offset + n <= self.end, (name, offset, n)
        return self.nc.alloc_sbuf_tensor_at(name, shape, dt, offset=offset), offset + n

    def keep(self, name, shape, dt=F32):
        t, self.at = self.place(name, shape, dt, self.at)
        return t

    def dma(self, eng, out, in_, sem, w=(), store=False):
        eng.wait(*w)
        t = self.counted_up(eng, sem)
        eng.list.append(lambda e: e.dma_start(out, in_(e) if callable(in_) else in_).then_inc(sem, 16))
        if store:
            self.stores.append(t)
        return t

    def counted_up(self, eng, sem, within=False):
        self.counts[sem.num] = self.counts.get(sem.num, 0) + 16
        if not within:
            eng.sent.append(sem)
        return (sem, self.counts[sem.num])

    def counted(self, at, most, w):
        regs = {}
        for x in (self.pe, self.dve, self.act, self.pool, self.sp):
            x.wait(*w)
            x.list.append(lambda e, x=x: regs.update({x: e.value_load(at, min_val=0, max_val=most)}))
        return regs

    @contextmanager
    def when(self, regs, n):
        engines = (self.pe, self.dve, self.act, self.pool, self.sp)
        before = [(x, x.list, x.n, dict(x.met), len(x.sent)) for x in engines]
        now = [x.now() for x in engines[:4]]
        counts = dict(self.counts)
        for x in engines:
            x.list = []
        yield
        for x, outer, first, met, sent in before:
            inner, x.list, x.met = x.list, outer, met
            owed = [(x.sem, x.n - first)] if x.n > first else []
            for sem in {s.num: s for s in x.sent[sent:]}.values():
                owed.append((sem, 16 * sum(s.num == sem.num for s in x.sent[sent:])))

            quiet = [(s, first if s is x.sem else counts.get(s.num, 0)) for s, _ in owed] + (now if len(x.sent) > sent else [])

            def both(e, x=x, inner=inner, owed=owed, quiet=quiet):
                with e.If(regs[x] > n):
                    for f in inner:
                        f(e)
                with e.Else():
                    for sem, value in quiet:
                        e.wait_ge(sem, value)
                    for sem, value in owed:
                        e.sem_inc(sem, value)

            x.list.append(both)

    def mm(self, out, l, r, start, stop, w=(), inc=False, skip=False):
        return self.pe.put(lambda e: e.matmul(out, l, r, start=start, stop=stop, skip_group_check=skip), w, inc)

    def tr(self, out, in_, ident, w=(), inc=False):
        return self.pe.put(lambda e: e.transpose(out, in_, ident), w, inc)

    def a(self, out, in_, func, w=(), bias=0.0, scale=1.0, accum=None):
        if accum is not None:
            return self.act.put(lambda e: e.activation(out, in_, func, bias=bias, scale=scale, accum_out=accum), w)
        return self.act.put(lambda e: e.activation(out, in_, func, bias=bias, scale=scale), w)

    def tt(self, eng, out, in0, in1, op, w=()):
        return eng.put(lambda e: e.tensor_tensor(out, in0, in1, op), w)

    def ts(self, eng, out, in0, s1, s2, op0, op1=None, w=()):
        if op1 is None:
            return eng.put(lambda e: e.tensor_scalar(out, in0, s1, None, op0), w)
        return eng.put(lambda e: e.tensor_scalar(out, in0, s1, s2, op0, op1), w)

    def stt(self, out, in0, s, in1, op0, op1, w=()):
        return self.dve.put(lambda e: e.scalar_tensor_tensor(out, in0, s, in1, op0, op1), w)

    def cp(self, eng, out, in_, w=()):
        return eng.put(lambda e: e.tensor_copy(out, in_), w)

    def red(self, out, in_, op, w=(), axis=AX.X):
        return self.dve.put(lambda e: e.tensor_reduce(out, in_, axis, op), w)

    def recip(self, out, in_, w=()):
        return self.dve.put(lambda e: e.reciprocal(out, in_), w)

    def rsqrt(self, out, in_, w=(), bias=0.0, scale=1.0):
        t = self.a(out, in_, ACT.Ln, w, bias=bias, scale=scale)
        return t, self.a(out, out, ACT.Exp, [t], scale=-0.5)

    def rsqrts(self, todo, bias=0.0, scale=1.0):
        first = [self.a(out, in_, ACT.Ln, w, bias=bias, scale=scale) for out, in_, w in todo]
        return first, [self.a(out, out, ACT.Exp, [t], scale=-0.5) for (out, _, _), t in zip(todo, first)]

    def memset(self, eng, out, v, w=()):
        return eng.put(lambda e: e.memset(out, v), w)

    def barrier(self):
        now = [x.now() for x in (self.pe, self.dve, self.act, self.pool)]
        for x in (self.pe, self.dve, self.act, self.pool, self.sp):
            x.wait(*now)

    def run(self):
        block = self.ctx.enter_context(self.nc.Block())

        @block.tensor
        def _(e):
            for f in self.pe.list:
                f(e)

        @block.vector
        def _(e):
            for f in self.dve.list:
                f(e)

        @block.scalar
        def _(e):
            for f in self.act.list:
                f(e)

        @block.gpsimd
        def _(e):
            for f in self.pool.list:
                f(e)

        @block.sync
        def _(e):
            for f in self.sp.list:
                f(e)
            last = {}
            for sem, v in self.stores:
                last[sem.num] = (sem, max(v, last.get(sem.num, (sem, 0))[1]))
            for sem, v in last.values():
                e.wait_ge(sem, v)


class Stream:

    def __init__(self, P, name, raws, highs, lows, items, ahead=1, share=None):
        self.P, self.items, self.ahead, self.share = P, items, ahead, share
        self.raws, self.highs, self.lows = raws, highs, lows
        self.rfree = [[] for _ in raws]
        self.sfree = [[] for _ in highs]
        self.sems = [P.sem(f"{name}{i}") for i in range(len(raws))]
        self.loaded, self.cut, self.i, self.ns = {}, {}, 0, 0
        self.nl = 0

    def load(self, upto):
        while self.nl < min(upto, len(self.items)):
            i = self.nl
            r = i % len(self.raws)
            src, n = self.items[i][:2]
            self.loaded[i] = self.P.dma(self.P.sp, self.raws[r][:, 0:n], src, self.sems[r], self.rfree[r])
            self.nl += 1

    def split(self, i):
        if i in self.cut or i >= len(self.items):
            return
        P = self.P
        n = self.items[i][1]
        r = i % len(self.raws)
        if self.items[i][2] == "raw":
            self.cut[i] = (self.raws[r], None, [self.loaded[i]], r)
            return
        s = self.ns % len(self.highs)
        self.ns += 1
        h, l, raw = self.highs[s], self.lows[s], self.raws[r]
        t1 = P.a(h[:, 0:n], raw[:, 0:n], ACT.Copy, [self.loaded[i], self.sfree[s]])
        m = self.share or n
        w = [self.loaded[i], t1, self.sfree[s]]
        t2 = [P.tt(P.dve, l[:, 0:m], raw[:, 0:m], h[:, 0:m].bitcast(F32), SUB, w)]
        if m < n:
            t2.append(P.tt(P.pool, l[:, m:n], raw[:, m:n], h[:, m:n].bitcast(F32), SUB, w))
        self.rfree[r] = [t1, t2]
        self.cut[i] = (h, l, [t1, t2], s)

    def next(self):
        i = self.i
        self.i += 1
        upto = i + 1
        while upto < min(i + len(self.raws), len(self.items)) and self.items[upto][2] != "late":
            upto += 1
        self.load(upto)
        self.split(i)
        for q in range(i + 1, min(i + 1 + self.ahead, len(self.items))):
            if self.items[q][2] != "split":
                break
            self.split(q)
        h, l, t, s = self.cut[i]

        def done(token):
            if self.items[i][2] == "raw":
                self.rfree[s] = [token]
            else:
                self.sfree[s] = [token]

        return h, l, t, done


class Ring:

    def __init__(self, P, name, slots, items, free, alone):
        self.P, self.slots, self.items, self.alone = P, slots, items, alone
        self.free = [free for _ in slots]
        self.sems = [P.sem(f"{name}{i}") for i in range(len(slots))]
        self.loaded, self.i, self.nl = {}, 0, 0

    def load(self, upto):
        while self.nl < min(upto, len(self.items)):
            i, r = self.nl, self.nl % len(self.slots)
            src, k = self.items[i]
            self.loaded[i] = self.P.dma(self.P.sp, self.slots[r][:, :].rearrange("p (k n) -> p k n", k=k), src,
                                        self.sems[r], self.free[r])
            self.nl += 1

    def next(self):
        i = self.i
        self.i += 1
        assert i < self.nl

        def done(token):
            self.free[i % len(self.slots)] = [token]
            self.load(min(i + 1 + len(self.slots), self.alone))

        return self.slots[i % len(self.slots)], self.loaded[i], done


def build(nc, A, out):
    with ExitStack() as ctx:
        P = Program(nc, ctx, A)
        c, pc = const_columns(), param_columns()
        pe, dve, act, pool, sp = P.pe, P.dve, P.act, P.pool, P.sp
        ps = P.ps
        CST = P.keep("cst", [128, c["n"]])
        PRM = P.keep("prm", [128, pc["n"]])
        PRM_END = P.at
        H = P.keep("H", [128, KT, S])
        TMPS = [P.keep(f"tmp{i}", [128, S]) for i in range(6)]
        ring0 = P.at
        RAW = [P.keep(f"raw{i}", [128, 2048]) for i in range(2)]
        WH = [P.keep(f"wh{i}", [128, 2048], F32R) for i in range(2)]
        WL = [P.keep(f"wl{i}", [128, 2048], F32R) for i in range(2)]
        cut0 = P.at - 32768
        xs0 = P.at
        XH = P.keep("xh", [128, KT, S], F32R)
        XL = P.keep("xl", [128, KT, S], F32R)
        base = P.at

        def cst(name, n, k=0):
            return CST[:, c[name] + k:c[name] + k + n]

        def prm(name, k=0):
            return PRM[:, pc[name] + k:pc[name] + k + 1]

        ident, ones, blk = cst("ident", 128), cst("ones", 128), cst("blk", 128)
        tmp = Slots([t[:, :] for t in TMPS])
        bfree = {b: [] for b in range(8)}
        bank = Banks(list(range(8)), bfree)

        items = []

        def feed(name, n, kind="split"):
            for i in range(A[name].shape[0]):
                items.append((A[name][i], n, kind))

        feed("sgu_u", 2048)
        feed("sgu_v", 2048)
        feed("sgu_o", 2048)
        for l in range(2):
            feed(f"up{l}", 2048)
            feed(f"down{l}", 1408)
            if l == 0:
                feed("lora1", 1024)
                feed("rwkv_rkv", 2048)
                feed("lora2", 2048, "raw")
                items.append((A["rwkv_o"][0], 2048, "late"))
                for i in range(1, 4):
                    items.append((A["rwkv_o"][i], 2048, "split"))
        feed("in2_qk", 2048)
        feed("in2_v", 2048)
        feed("in2_dn", 2048)
        feed("in2_ab", 128)
        items.append((A["out2"][0], 2048, "late"))
        for i in range(1, 4):
            items.append((A["out2"][i], 2048, "split"))
        W = Stream(P, "s_w", RAW, WH, WL, items)

        s_c = P.sem("s_c")
        P.dma(sp, CST[:, :], A["consts"], s_c)
        P.dma(sp, PRM[:, :], A["params"], s_c)
        t_c = P.dma(sp, H[:, :, :], A["x"].rearrange("(k p) t -> p k t", p=128), s_c)
        W.load(2)
        for e in (pe, dve, act, pool):
            e.wait(t_c)

        def split(src, k, t, XH=XH, XL=XL, w=()):
            th = P.a(XH[:, k], src, ACT.Copy, [t, w])
            tl = P.tt(dve, XL[:, k], src, XH[:, k].bitcast(F32), SUB, [t, th, w])
            return [th, tl]

        def rstd_of(total, n, eps, w):
            b, _, free = bank.take()
            t = P.mm(ps[:, b], ones, total, True, True, [w, free], True)
            i, r, free = tmp.take()
            t1, t = P.rsqrt(r, ps[:, b], [t, free], prm(eps), 1.0 / n)
            bank.free[b] = [t1]
            return i, r, t

        def square_sum(tiles, toks):
            ia, acc, free = tmp.take()
            ta = P.a(acc, tiles[0], ACT.Square, [toks[0], free])
            for k in range(1, len(tiles)):
                i, q, free = tmp.take()
                if i == ia:
                    i, q, free = tmp.take()
                t = P.a(q, tiles[k], ACT.Square, [toks[k], free])
                ta = P.tt(dve, acc, acc, q, ADD, [t, ta])
                tmp.free[i] = [ta]
            return ia, acc, ta

        def norm(gain, gk, toks, inplace=False, w=()):
            ia, acc, ta = square_sum([H[:, k] for k in range(KT)], toks)
            ir, r, tr = rstd_of(acc, D, "eps", ta)
            tmp.free[ia] = [pe.now()]
            got = []
            for k in range(KT):
                if inplace:
                    got.append(P.stt(H[:, k], H[:, k], prm(gain, gk + k), r, MUL, MUL, [tr, toks[k]]))
                    tl = got[-1]
                    continue
                i, x, free = tmp.take()
                if i == ir:
                    i, x, free = tmp.take()
                t = P.stt(x, H[:, k], prm(gain, gk + k), r, MUL, MUL, [tr, toks[k], free])
                got.append(split(x, k, t, w=w))
                tmp.free[i] = got[-1]
                tl = t
            tmp.free[ir] = [tl]
            return got

        def products(o, h, l, X, XLo, xt, first, last, inc, w):
            P.mm(o, h, X, first, False, [w, xt])
            P.mm(o, h, XLo, False, False)
            return P.mm(o, l, X, False, last, inc=inc)

        def gemm(nm, evac, xt, mt=2):
            m = 0
            for _ in range(nm // mt):
                h, l, tw, done = W.next()
                hv = h[:, 0:mt * 1024].rearrange("p (m k j) -> p m k j", m=mt, j=128)
                lv = l[:, 0:mt * 1024].rearrange("p (m k j) -> p m k j", m=mt, j=128)
                for q in range(mt):
                    b, _, free = bank.take()
                    for k in range(KT):
                        t = products(ps[:, b], hv[:, q, k], lv[:, q, k], XH[:, k], XL[:, k], xt[k],
                                     k == 0, k == KT - 1, k == KT - 1, [tw, free])
                    bank.free[b] = evac(m, ps[:, b], t)
                    m += 1
                done(t)

        def gemm_tok(chunks, cols, evac, xt):
            for ch in range(chunks):
                h, l, tw, done = W.next()
                hv = h[:, 0:KT * cols].rearrange("p (k j) -> p k j", k=KT)
                lv = l[:, 0:KT * cols].rearrange("p (k j) -> p k j", k=KT)
                for n in range(4):
                    b, _, free = bank.take()
                    o = ps[:, b, 0:cols]
                    for k in range(KT):
                        xh, xl = XH[:, k, 128 * n:128 * n + 128], XL[:, k, 128 * n:128 * n + 128]
                        P.mm(o, xh, hv[:, k], k == 0, False, [tw, free, xt[k]])
                        P.mm(o, xl, hv[:, k], False, False)
                        t = P.mm(o, xh, lv[:, k], False, k == KT - 1, inc=k == KT - 1)
                    bank.free[b] = evac(ch, n, o, t)
                done(t)

        def residual(toks):
            def evac(m, o, t):
                toks[m] = P.tt(dve, H[:, m], o, H[:, m], ADD, [t, toks[m]])
                return [toks[m]]
            return evac

        at = base
        U, at = P.place("U", [128, KT, S], F32, at)
        V, at = P.place("V", [128, 4, D], F32, at)
        WS, at = P.place("WS", [128, 16, 128], F32, at)
        ROWB, at = P.place("ROWB", [128, 2, D], F32, at)
        BS, at = P.place("BS", [16, 128], F32, at)
        SEL, at = P.place("SEL", [16, D], F32, at)
        SS, at = P.place("SS", [128, 4, 4], F32, at)
        RS, at = P.place("RS", [128, 4], F32, at)
        s_g = P.sem("s_g")
        P.dma(sp, SEL[:, :], A["sel"], s_g)
        P.dma(sp, WS[:, :, :], A["sgu_ws"], s_g)
        P.dma(sp, ROWB[:, :, :], A["sgu_rows"], s_g)
        t_g = P.dma(sp, BS[:, :], A["sgu_bs"], s_g)
        t_ws = pool.put(lambda e: e.affine_select(out=WS[:, :, :], in_=WS[:, :, :], compare_op=ALU.is_ge, fill=0.0, base=0,
                                                  pattern=[[0, 16], [1, 128]], channel_multiplier=-1), [t_g])
        xt = norm("mixg", 0, [t_c] * KT)
        ut = [None] * KT

        def evac_u(m, o, t):
            ut[m] = P.a(U[:, m], o, ACT.Gelu, [t], bias=prm("bu", m))
            return [ut[m]]

        gemm(KT, evac_u, xt)
        vt = [[None] * 4 for _ in range(4)]

        def evac_v(ch, n, o, t):
            v = V[:, n, 256 * ch:256 * ch + 256]
            t1 = P.tt(dve, v, o, ROWB[:, 0, 256 * ch:256 * ch + 256], ADD, [t, t_g])
            vt[n][ch] = P.a(v, v, ACT.Gelu, [t1])
            return [t1]

        gemm_tok(4, 256, evac_v, xt)
        st = []
        for n in range(4):
            for ch in range(4):
                i, q, free = tmp.take()
                t = P.a(q[:, 0:256], V[:, n, 256 * ch:256 * ch + 256], ACT.Square, [vt[n][ch], free], accum=SS[:, n, ch:ch + 1])
                tmp.free[i] = [t]
                st.append(t)
        t = P.red(RS[:, :], SS[:, :, :], ADD, st)
        t = P.a(RS[:, :], RS[:, :], ACT.Sqrt, [t], bias=prm("eps"), scale=1.0 / D)
        t = P.recip(RS[:, :], RS[:, :], [t])
        vn = [P.stt(V[:, n], V[:, n], RS[:, n:n + 1], ROWB[:, 1], MUL, MUL, [t, vt[n]]) for n in range(4)]
        xt2 = []
        for m in range(KT):
            b, _, free = bank.take()
            P.mm(ps[:, b].rearrange("p (n t) -> p n t", n=4), SEL[:, 128 * m:128 * m + 128],
                 BS[:, :].rearrange("p (a t) -> p a t", a=1).to_broadcast([16, 4, 128]), True, False, [free, t_g], skip=True)
            for n in range(4):
                for g in range(2):
                    f = 128 * m + 64 * g
                    t = P.mm(ps[64 * g:64 * g + 64, b, 128 * n:128 * n + 128], V[:, n, f:f + 64], WS[:, 2 * m + g, :],
                             False, n == 3, [vn[n], t_ws], inc=(n == 3 and g == 1), skip=True)
            i, y, free = tmp.take()
            t = P.tt(dve, y, ps[:, b], U[:, m], MUL, [t, ut[m], free])
            bank.free[b] = [t]
            xt2.append(split(y, m, t, w=[pe.now()]))
            tmp.free[i] = xt2[-1]
        ht = [t_c] * KT
        gemm(KT, residual(ht), xt2)

        def ffn(l, ht):
            xt = norm("ffng", 8 * l, ht, w=[pe.now()])
            HH, at = P.place(f"HH{l}", [128, FT, S], F32R, base)
            HL, at = P.place(f"HL{l}", [128, FT, S], F32R, at)
            hid = []
            half = {}

            def evac(m, o, t):
                f = m // 2 + (m % 2) * FT
                w = [prm("cw", (3 * l + j) * 44 + f) for j in range(3)]
                i, z, free = tmp.take()
                t1 = P.a(z, o, ACT.Identity, [t, free], bias=prm("cb", 44 * l + f), scale=w[2])
                t2 = P.stt(z[:, 1:S], o[:, 0:S - 1], w[1], z[:, 1:S], MUL, ADD, [t1])
                t3 = P.stt(z[:, 2:S], o[:, 0:S - 2], w[0], z[:, 2:S], MUL, ADD, [t2])
                if m % 2 == 0:
                    half[0] = (i, z, P.a(z, z, ACT.Silu, [t3]))
                    return [t3]
                ig, g, tg = half[0]
                t4 = P.tt(dve, z, z, g, MUL, [t3, tg])
                tmp.free[ig] = [t4]
                hid.append(split(z, m // 2, t4, HH, HL))
                tmp.free[i] = hid[-1]
                return [t3]

            gemm(2 * FT, evac, xt)
            for m in range(KT):
                b, _, free = bank.take()
                for part in range(2):
                    h, lo, tw, done = W.next()
                    for j in range(11):
                        k = 11 * part + j
                        t = products(ps[:, b], h[:, 128 * j:128 * j + 128], lo[:, 128 * j:128 * j + 128],
                                     HH[:, k], HL[:, k], hid[k], k == 0, k == FT - 1, j == 10, [tw, free])
                    done(t)
                ht[m] = P.tt(dve, H[:, m], ps[:, b], H[:, m], ADD, [t, ht[m]])
                bank.free[b] = [ht[m]]
            return ht

        P.barrier()
        ht = ffn(0, ht)

        def inverse(MT, T, TT, Z, n0, nb, masks, ready, banks, want, mbs, tri):
            sl = slice(n0, n0 + nb)
            w = nb * 64

            def level(l):
                return cst(masks, 64, 64 * l).rearrange("p (a j) -> p a j", a=1).to_broadcast([128, nb, 64])

            eye = cst("i2", 64)
            eyes = eye.rearrange("p (a j) -> p a j", a=1).to_broadcast([128, nb, 64])
            im, mb, free = mbs.take()
            M = mb[:, 0:w].rearrange("p (a j) -> p a j", j=64)
            tm = P.tt(dve, M, MT[:, sl], level(0), MUL, [ready, free])
            b, _, free = banks.take()
            o = ps[:, b, 0:w].rearrange("p (a j) -> p a j", j=64)
            for a in range(nb):
                for h in (0, 64):
                    t = P.mm(o[h:h + 64, a], M[h:h + 64, a], eye[h:h + 64], True, True, [tm, free], a == nb - 1 and h > 0)
            tT = P.tt(dve, T[:, sl], o, eyes, ADD, [t, tri])
            tTT = P.tt(dve, TT[:, sl], M, eyes, ADD, [tm, tri])
            banks.free[b] = [tT]
            mbs.free[im] = [tTT, t]
            yield
            for l in range(1, 6):
                im, mb, free = mbs.take()
                M = mb[:, 0:w].rearrange("p (a j) -> p a j", j=64)
                tm = P.tt(dve, M, MT[:, sl], level(l), MUL, [ready, free])
                b, _, free = banks.take()
                o = ps[:, b, 0:w].rearrange("p (a j) -> p a j", j=64)
                for a in range(nb):
                    for h in (0, 64):
                        t = P.mm(o[h:h + 64, a], M[h:h + 64, a], T[h:h + 64, n0 + a], True, True, [tm, tT, free],
                                 a == nb - 1 and h > 0)
                mbs.free[im] = [t]
                tz = P.a(Z[:, sl], o, ACT.Copy, [t, tri])
                banks.free[b] = [tz]
                yield
                last = l == 5
                got = {}
                for name, left, right in (("T", TT, Z), ("TT", Z, TT)):
                    if last and name != want:
                        continue
                    b, _, free = banks.take()
                    o = ps[:, b, 0:w].rearrange("p (a j) -> p a j", j=64)
                    for a in range(nb):
                        for h in (0, 64):
                            t = P.mm(o[h:h + 64, a], left[h:h + 64, n0 + a], right[h:h + 64, n0 + a], True, True,
                                     [tz, tTT, free], a == nb - 1 and h > 0)
                    got[name] = (b, o, t)
                both = [x[2] for x in got.values()]
                for name, (b, o, t) in got.items():
                    X = T if name == "T" else TT
                    t = P.tt(dve, X[:, sl], o, X[:, sl], ADD, both)
                    banks.free[b] = [t]
                    if name == "T":
                        tT = t
                    else:
                        tTT = t
                yield
            tri[:] = [tT if want == "T" else tTT]

        P.barrier()
        s_h = P.sem("s_h")
        hs = nc.dram_tensor("hs", [128, KT, S], F32, kind="Internal").ap()
        t_sp = P.dma(sp, hs, H[:, :, :], s_h, [ht], store=True)
        AR, at = P.place("AR", [128, 2, KT, S], F32, base)
        KB, at = P.place("KB", [128, KT, S], F32, at)
        LW, at = P.place("LW", [128, KT, S], F32, at)
        OMM, at = P.place("OMM", [128, 48], F32, at)
        PC, at = P.place("PC", [128, KT, 8], F32, at)
        q0 = at
        VF, at = P.place("VF", [128, KT, S], F32, at)
        HID, at = P.place("HID", [128, 4, S], F32, at)
        SM, _ = P.place("SM", [128, S], F32, ring0)
        G, _ = P.place("G", [128, KT, S], F32, xs0)
        VT, _ = P.place("VT", [128, 4, D], F32, xs0 + 16384)
        B = H
        t_om = P.ts(dve, OMM[:, :], PRM[:, pc["mu"]:pc["mu"] + 48], -1.0, 1.0, MUL, ADD)
        xn = norm("mixg", 8, [[x, t_sp] for x in ht], inplace=True)

        def mix(i):
            w = [pe.now()]
            got = []
            for k in range(KT):
                q, x, free = tmp.take()
                t = P.a(x, H[:, k], ACT.Copy, [xn[k], t_om, free], scale=OMM[:, 8 * i + k:8 * i + k + 1])
                t = P.stt(x[:, 1:S], H[:, k, 0:S - 1], prm("mu", 8 * i + k), x[:, 1:S], MUL, ADD, [t])
                got.append(split(x, k, t, w=w))
                tmp.free[q] = got[-1]
            return got

        hid = [None] * 4

        def into(dst, toks, at=0, func=ACT.Copy):
            def evac(m, o, t):
                toks[at + m] = P.a(dst[:, at + m], o, func, [t])
                return [toks[at + m]]
            return evac

        gemm(1, into(HID, hid, 0, ACT.Tanh), mix(1), 1)
        gemm(1, into(HID, hid, 1), mix(4), 1)
        gemm(2, into(HID, hid, 2, ACT.Sigmoid), mix(5), 1)
        rt, kt, vt = [None] * 8, [None] * 8, [None] * 8
        gemm(KT, into(AR[:, 1], rt), mix(0))
        gemm(KT, into(KB, kt), mix(2))
        gemm(KT, into(VF, vt), mix(3))
        mixed = [pe.now(), act.now(), dve.now()]
        raw0, _, t0, done0 = W.next()
        lt, at_, gt = [None] * 8, [None] * 8, [None] * 8
        for m in range(KT):
            b1, _, free = bank.take()
            P.mm(ps[:, b1], raw0[0:64, 128 * m:128 * m + 128], HID[0:64, 0], True, True, [t0, hid[0], free])
            b2, _, free = bank.take()
            t = P.mm(ps[:, b2], raw0[64:128, 128 * m:128 * m + 128], HID[64:128, 1], True, True, [hid[1], free], True)
            x = P.a(LW[:, m], ps[:, b1], ACT.Sigmoid, [t], bias=prm("w0", m))
            bank.free[b1] = [x]
            lt[m] = P.ts(dve, LW[:, m], LW[:, m], -float(np.exp(np.float64(-0.5))), None, MUL, w=[x])
            at_[m] = P.a(B[:, m], ps[:, b2], ACT.Sigmoid, [t, mixed], bias=prm("a0", m))
            bank.free[b2] = [at_[m]]
        done0(t)
        raw1, _, t1, done1 = W.next()
        for m in range(KT):
            b, _, free = bank.take()
            P.mm(ps[:, b], raw1[:, 128 * m:128 * m + 128], HID[:, 2], True, False, [t1, hid, free])
            t = P.mm(ps[:, b], raw1[0:32, D + 128 * m:D + 128 * m + 128], HID[0:32, 3], False, True, inc=True)
            gt[m] = P.cp(dve, G[:, m], ps[:, b], [t, mixed])
            bank.free[b] = [gt[m]]
        done1(t)
        vn = []
        for n in range(4):
            for half in range(2):
                b, _, free = bank.take()
                for q in range(4):
                    t = P.tr(ps[:, b, 128 * q:128 * q + 128], VF[:, 4 * half + q, 128 * n:128 * n + 128], ident,
                             [vt, free], q == 3)
                bank.free[b] = [P.cp(dve, VT[:, n, 512 * half:512 * half + 512], ps[:, b], [t, mixed])]
                vn += bank.free[b]
        t_sm = P.memset(pool, SM[:, :], 1.0, [t])
        t_sm = P.memset(pool, SM[:, :].rearrange("p (c t) -> p c t", t=64)[:, :, 0:1], 0.0, [t_sm])
        kk = [None] * 8
        for j0 in range(0, KT, 4):
            todo, xs = [], []
            for j in range(j0, j0 + 4):
                x = AR[:, 0, j]
                tx = P.ts(dve, x, KB[:, j], prm("kk", j), None, MUL, w=[kt[j]])
                i, y, free = tmp.take()
                t = P.a(y, x, ACT.Square, [tx, free])
                b, _, free = bank.take()
                t = P.mm(ps[:, b], blk, y, True, True, [t, free], True)
                t = P.ts(dve, y, ps[:, b], 1e-24, None, MAX, w=[t])
                bank.free[b] = [t]
                todo.append((y, y, [t]))
                xs.append((j, i, x, y, tx))
            for (j, i, x, y, tx), t in zip(xs, P.rsqrts(todo, scale=float(2 ** 20))[1]):
                kk[j] = P.stt(x, x, 1024.0, y, MUL, MUL, [tx, t])
                tmp.free[i] = [kk[j]]
        ready = []
        bv = []
        for j in range(KT):
            r, k, a, lw = AR[:, 1, j], KB[:, j], B[:, j], LW[:, j]
            ic, cum, free = tmp.take()
            t_cum = dve.put(lambda e, cum=cum, lw=lw: e.tensor_tensor_scan(cum, SM[:, :], lw, 0.0, MUL, ADD), [lt[j], t_sm, free])
            i1, x, free = tmp.take()
            t = P.tt(dve, x, cum, lw, SUB, [t_cum, free])
            t_lw = t
            t_e1 = P.a(x, x, ACT.Exp, [t])
            i2, e2, free = tmp.take()
            t_e2 = P.a(e2, cum, ACT.Exp, [t_cum, free])
            t_e3 = P.a(cum, cum, ACT.Exp, [t_e2, t_e1], scale=-1.0)
            i3, y, free = tmp.take()
            t = P.ts(dve, y, a, -1.0, prm("ka", j), ADD, MUL, w=[at_[j], free])
            t_k = P.stt(k, y, 1.0, k, ADD, MUL, [t, kk[j]])
            t = P.stt(y, r, prm("rk", j), k, MUL, MUL, [rt[j], t_k])
            b, _, free = bank.take()
            t = P.mm(ps[:, b], blk, y, True, True, [t, free], True)
            tmp.free[i3] = [t]
            t_bv = P.tt(dve, lw, ps[:, b], VF[:, j], MUL, [t, t_lw, vt[j]])
            bank.free[b] = [t_bv]
            bv.append(t_bv)
            t1 = P.tt(dve, a, AR[:, 0, j], a, MUL, [t, kk[j]])
            t2 = P.stt(AR[:, 0, j], AR[:, 0, j], -1.0, x, MUL, MUL, [t_e1, t1])
            tmp.free[i1] = [t2]
            t3 = P.tt(dve, r, r, e2, MUL, [t_e2, t])
            t4 = P.cp(pool, PC[:, j], e2.rearrange("p (c t) -> p c t", t=64)[:, :, 63], [t_e2])
            tmp.free[i2] = [t3, t4]
            t5 = P.tt(dve, a, a, cum, MUL, [t_e3, t1])
            t6 = P.tt(dve, k, k, cum, MUL, [t_e3, t_k, t])
            tmp.free[ic] = [t5, t6]
            ready.append([t2, t3, t4, t5, t6])

        P.barrier()
        sets = []
        for q, x in enumerate((q0, cut0)):
            one = {}
            for name, shape in (("TT", [128, 16, 64]), ("RB", [128, 16, 64]), ("RK", [128, 16, 64]),
                                ("AKV", [128, 4, 256]), ("BT", [128, 4, 256]), ("KT", [128, 4, 256])):
                one[name], x = P.place(f"q{name}{q}", shape, F32, x)
            sets.append(one)
        TN, x = P.place("TN", [128, 16, 64], F32, x)
        ZZ, x = P.place("ZZ", [128, 16, 64], F32, x)
        assert x <= cut0 + 32768
        MT, x = P.place("MT", [128, 16, 64], F32, ring0)
        ST, x = P.place("ST", [128, 2, 64], F32, x)
        RH, x = P.place("RH", [128, 2, 2, 64], F32, x)
        UU, x = P.place("UU", [128, 2, 2, 64], F32, x)
        Y1, x = P.place("Y1", [128, 2, 64], F32, x)
        assert x <= ring0 + 8192
        mbs = Slots([TMPS[0][:, :], TMPS[1][:, :]])
        free_banks = Banks([4, 5, 6, 7], bfree)

        def mask(name, n):
            return cst(name, 64).rearrange("p (a j) -> p a j", a=1).to_broadcast([128, n, 64])

        solved = {}

        def solve(q):
            z = sets[q % 2]
            w0 = [pe.now(), dve.now(), act.now()]
            got = []
            for hl in range(4):
                j, r = 2 * q + hl // 2, 64 * (hl % 2)
                o = []
                for left in (B, KB):
                    b, _, free = free_banks.take()
                    for n in range(4):
                        for h in (0, 64):
                            f = 128 * n + h
                            t = P.mm(ps[h:h + 64, b, 128 * n:128 * n + 128].rearrange("p (a j) -> p a j", a=2),
                                     left[r:r + 64, j, f:f + 64], AR[r:r + 64, :, j, f:f + 64], True, True,
                                     [free], n == 3 and h > 0)
                    o.append((b, ps[:, b].rearrange("p (n a j) -> p n a j", n=4, a=2), t))
                it = slice(4 * hl, 4 * hl + 4)
                (b1, o1, t1), (b2, o2, t2) = o
                x1 = P.cp(dve, MT[:, it], o1[:, :, 0], [t1, w0])
                x2 = P.tt(dve, z["RB"][:, it], o1[:, :, 1], mask("incu", 4), MUL, [t1, w0])
                x3 = P.tt(dve, ZZ[:, it], o2[:, :, 0], mask("stru", 4), MUL, [t2, w0])
                x4 = P.tt(dve, z["RK"][:, it], o2[:, :, 1], mask("incu", 4), MUL, [t2, w0])
                free_banks.free[b1] = [x1, x2]
                free_banks.free[b2] = [x3, x4]
                got += [x1, x2, x3, x4]
                yield
            for left, name in ((B, "BT"), (KB, "KT")):
                for jl in range(2):
                    b, _, free = free_banks.take()
                    for n in range(4):
                        t = P.tr(ps[:, b, 128 * n:128 * n + 128], left[:, 2 * q + jl, 128 * n:128 * n + 128], ident,
                                 [free], n == 3)
                    x = P.a(z[name][:, :, 128 * jl:128 * jl + 128], ps[:, b].rearrange("p (n k) -> p n k", n=4), ACT.Copy, [t, w0])
                    free_banks.free[b] = [x]
                    got.append(x)
                yield
            for half in range(2):
                b, _, free = free_banks.take()
                for nl in range(2):
                    n = 2 * half + nl
                    for h in (0, 64):
                        for hl in range(4):
                            jl, par = hl // 2, hl % 2
                            f = 128 * (2 * q + jl) + 64 * par
                            c0 = 256 * nl + 128 * par + 64 * jl
                            t = P.mm(ps[h:h + 64, b, c0:c0 + 64], ZZ[h:h + 64, 4 * hl + n], VT[h:h + 64, n, f:f + 64],
                                     True, True, [free, got], True)
                x = P.a(z["AKV"][:, 2 * half:2 * half + 2], ps[:, b].rearrange("p (n k) -> p n k", n=2), ACT.Copy, [t, w0])
                free_banks.free[b] = [x]
                got.append(x)
            yield
            tris = [[w0, t], [w0, t]]
            gens = [inverse(MT, TN, z["TT"], ZZ, 8 * i, 8, "up", got, free_banks, "TT", mbs, tris[i]) for i in range(2)]
            while gens:
                for g in list(gens):
                    try:
                        next(g)
                        yield
                    except StopIteration:
                        gens.remove(g)
            solved[q] = [got, tris]

        yt = [[] for _ in range(KT)]

        def recur(q):
            z = sets[q % 2]
            w = solved[q]
            ts = P.memset(dve, ST[:, :, :], 0.0, [pe.now(), dve.now()])
            tyl = dve.now()
            for ch in range(8):
                n, p = ch // 2, 64 * (ch % 2)
                P_ = slice(p, p + 64)
                for par in range(2):
                    r = slice(64 * par, 64 * par + 64)
                    for jl in range(2):
                        j = 2 * q + jl
                        f = 64 * ch
                        P.mm(ps[P_, par, 64 * jl:64 * jl + 64], AR[r, 0, j, f:f + 64], ST[r, jl], True, True, [ts, w, bfree[par]])
                        t = P.mm(ps[r, par, 256 + 64 * jl:256 + 64 * jl + 64], ST[r, jl], AR[r, 1, j, f:f + 64], True, True,
                                 inc=par == 1 and jl == 1)
                tr = P.tt(dve, RH[P_], ps[P_, 0:2, 0:128].rearrange("p a (j v) -> p a j v", j=2),
                          z["AKV"][P_, n].rearrange("p (a j v) -> p a j v", a=2, j=2), ADD, [t])
                ty = [P.cp(dve, Y1[64 * par:64 * par + 64], ps[64 * par:64 * par + 64, par, 256:384].rearrange("p (j v) -> p j v", j=2), [t, tyl])
                      for par in range(2)]
                bfree[0], bfree[1] = [tr, ty], [tr, ty]
                yield
                for par in range(2):
                    for jl in range(2):
                        hl = 2 * jl + par
                        t = P.mm(ps[P_, 2, 128 * par + 64 * jl:128 * par + 64 * jl + 64], z["TT"][P_, 4 * hl + n], RH[P_, par, jl],
                                 True, True, [tr, bfree[2]], par == 1 and jl == 1)
                tu = P.a(UU[P_], ps[P_, 2, 0:256].rearrange("p (a j v) -> p a j v", a=2, j=2), ACT.Copy, [t])
                bfree[2] = [tu]
                yield
                for part in range(2):
                    for par in range(2):
                        r = slice(64 * par, 64 * par + 64)
                        for jl in range(2):
                            j, it = 2 * q + jl, 4 * (2 * jl + par) + n
                            k = slice(128 * jl + 64 * par, 128 * jl + 64 * par + 64)
                            f = 128 * j + 64 * par
                            v = VT[P_, n, f:f + 64]
                            if part == 0:
                                o = ps[r, 3, 64 * jl:64 * jl + 64]
                                P.mm(o, z["KT"][P_, n, k], v, True, False, [bfree[3], tu])
                                t = P.mm(o, z["BT"][P_, n, k], UU[P_, par, jl], False, True)
                            else:
                                o = ps[r, 3, 128 + 64 * jl:192 + 64 * jl]
                                P.mm(o, v, z["RK"][P_, it], True, False)
                                t = P.mm(o, UU[P_, par, jl], z["RB"][P_, it], False, True, inc=par == 1 and jl == 1)
                ts = P.tt(dve, ST[:, :, :], ST[:, :, :], ps[:, 3, 0:128].rearrange("p (j v) -> p j v", j=2), ADD, [t])
                ts = P.tt(dve, ST[:, :, :], ST[:, :, :], PC[:, 2 * q:2 * q + 2, ch:ch + 1].to_broadcast([128, 2, 64]), MUL, [ts])
                ty = P.tt(dve, AR[:, 1, 2 * q:2 * q + 2, 64 * ch:64 * ch + 64], ps[:, 3, 128:256].rearrange("p (j v) -> p j v", j=2),
                          Y1[:, :, :], ADD, [t, ty])
                bfree[3] = [ts, ty]
                tyl = ty
                yield
            yt[2 * q] = yt[2 * q + 1] = [ty]

        def drain(*gens):
            gens = list(gens)
            while gens:
                for g in list(gens):
                    try:
                        next(g)
                    except StopIteration:
                        gens.remove(g)

        drain(solve(0))
        for q in range(4):
            if q < 3:
                drain(recur(q), solve(q + 1))
            else:
                drain(recur(q))

        P.barrier()
        t_h = P.dma(sp, H[:, :, :], hs, s_h)
        yx = []
        for j0 in range(0, KT, 4):
            todo, xs = [], []
            for j in range(j0, j0 + 4):
                y = AR[:, 1, j]
                b, _, free = bank.take()
                t = P.mm(ps[:, b], blk, y, True, True, [free, yt[j]], True)
                tc = P.stt(y, ps[:, b], -1.0 / 64, y, MUL, ADD, [t])
                bank.free[b] = [tc]
                i, x, free = tmp.take()
                t = P.a(x, y, ACT.Square, [tc, free])
                b, _, free = bank.take()
                t = P.mm(ps[:, b], blk, x, True, True, [free, t], True)
                todo.append((x, ps[:, b], [t]))
                xs.append((j, i, x, y, b))
            first, second = P.rsqrts(todo, prm("gneps"), 1.0 / 64)
            for (j, i, x, y, b), t1, t in zip(xs, first, second):
                bank.free[b] = [t1]
                t = P.tt(dve, x, x, y, MUL, [t])
                t = P.ts(dve, x, x, prm("lnw", j), prm("lnb", j), MUL, ADD, [t])
                t = P.tt(dve, x, x, LW[:, j], ADD, [t])
                t = P.tt(dve, x, x, G[:, j], MUL, [t])
                yx.append(split(x, j, t))
                tmp.free[i] = yx[-1]
        ht = [t_h] * KT
        gemm(KT, residual(ht), yx)
        P.barrier()
        ht = ffn(1, ht)

        P.barrier()
        ht = norm("fing", 0, ht, inplace=True)
        xt = norm("ln1", 0, ht, w=[pe.now()])
        QK, at = P.place("QK", [128, 8, S], F32, base)
        AV, at = P.place("AV", [128, 4, S], F32, at)
        KQ, at = P.place("KQ", [128, 2, 4, S], F32, at)
        DV, at = P.place("DV", [128, 4, S], F32, at)
        ZG, at = P.place("ZG", [128, 4, S], F32, at)
        AT, at = P.place("AT", [128, 4, S], F32, at)
        AB, at = P.place("AB", [128, 4, 16], F32, at)
        R8, at = P.place("R8", [128, 2, 8], F32, at)
        tail = at
        CM, _ = P.place("CM", [128, 64], F32, tail)
        s_b = P.sem("s_b")
        t_r8 = P.dma(sp, R8[:, :, :], A["rows8"], s_b)
        t_cm = P.dma(sp, CM[:, :], A["colmask"], s_b)
        qt, av, dt_, ab = [None] * 8, [], [None] * 16, []
        gemm(8, into(QK, qt), xt)

        def evac_av(ch, n, o, t):
            av.append(P.a(AV[:, n, 256 * ch:256 * ch + 256], o, ACT.Copy, [t]))
            return [av[-1]]

        gemm_tok(2, 256, evac_av, xt)

        def evac_dn(m, o, t):
            if m >= 12:
                dt_[m] = P.a(ZG[:, m - 12], o, ACT.Silu, [t])
                return [dt_[m]]
            i, z, free = tmp.take()
            w = [prm("dncw", 12 * j + m) for j in range(5)]
            t1 = P.a(z, o, ACT.Copy, [t, free], scale=w[2])
            t1 = P.stt(z[:, 2:S], o[:, 0:S - 2], w[0], z[:, 2:S], MUL, ADD, [t1])
            t1 = P.stt(z[:, 1:S], o[:, 0:S - 1], w[1], z[:, 1:S], MUL, ADD, [t1])
            t1 = P.stt(z[:, 0:S - 1], o[:, 1:S], w[3], z[:, 0:S - 1], MUL, ADD, [t1])
            t1 = P.stt(z[:, 0:S - 2], o[:, 2:S], w[4], z[:, 0:S - 2], MUL, ADD, [t1])
            dst = KQ[:, 1, m] if m < 4 else KQ[:, 0, m - 4] if m < 8 else DV[:, m - 8]
            dt_[m] = P.a(dst, z, ACT.Silu, [t1])
            tmp.free[i] = [dt_[m]]
            return [t1]

        gemm(16, evac_dn, xt)

        def evac_ab(ch, n, o, t):
            ab.append(P.cp(dve, AB[:, n], o, [t]))
            return [ab[-1]]

        gemm_tok(1, 16, evac_ab, xt)
        projected = pe.now()
        BT, _ = P.place("BT", [128, 8, 16, 64], F32, xs0)
        tb = []
        P.dma(sp, BT[0:64, :, 0:15], A["rpb"], s_b, [projected])
        t_bt = P.dma(sp, BT[64:128, :, 1:16], A["rpb"], s_b)
        for p, d in ((0, 0), (64, 1)):
            v = BT[p:p + 64, :, d:d + 15]
            tb.append(P.tt(pool, v, v, CM[p:p + 64, :].rearrange("p (a b j) -> p a b j", a=1, b=1).to_broadcast([64, 8, 15, 64]),
                           ADD, [t_bt, t_cm]))
        for m0 in (0, 4):
            todo, xs = [], []
            for m in range(m0, m0 + 4):
                i, x, free = tmp.take()
                t = P.a(x, QK[:, m], ACT.Square, [qt[m], free])
                b, _, free = bank.take()
                t = P.mm(ps[:, b], blk, x, True, True, [t, free], True)
                todo.append((x, ps[:, b], [t]))
                xs.append((m, i, x, b))
            first, second = P.rsqrts(todo, prm("eps"), 1.0 / 64)
            for (m, i, x, b), t1, t in zip(xs, first, second):
                bank.free[b] = [t1]
                qt[m] = P.stt(QK[:, m], QK[:, m], prm("qg" if m < 4 else "kg"), x, MUL, MUL, [t])
                tmp.free[i] = [qt[m]]
        for m0 in (0, 4):
            todo, xs = [], []
            for m in range(m0, m0 + 4):
                v = KQ[:, 1 - m // 4, m % 4]
                i, x, free = tmp.take()
                t = P.a(x, v, ACT.Square, [dt_[m], free])
                b, _, free = bank.take()
                t = P.mm(ps[:, b], ones, x, True, True, [t, free], True)
                todo.append((x, ps[:, b], [t]))
                xs.append((m, i, x, b, v))
            first, second = P.rsqrts(todo, prm("eps"))
            for (m, i, x, b, v), t1, t in zip(xs, first, second):
                bank.free[b] = [t1]
                dt_[m] = P.stt(v, v, float(128 ** -0.5) if m < 4 else 1.0, x, MUL, MUL, [t])
                tmp.free[i] = [dt_[m]]

        x = tail + 256
        LG, PM, PT = [], [], []
        for i in range(2):
            for lst, name in ((LG, "LG"), (PM, "PM"), (PT, "PT")):
                y, x = P.place(f"{name}{i}", [128, S], F32, x)
                lst.append(y[:, :])
        AO, x = P.place("AO", [128, S], F32, x)
        MX, x = P.place("MX", [128, 32], F32, x)
        SU, x = P.place("SU", [128, 32], F32, x)
        SQ, x = P.place("SQ", [128, 4], F32, x)
        lg, pm, pt = Slots(LG), Slots(PM), Slots(PT)
        at_banks = Banks([0, 1, 2, 3, 4, 5], bfree)
        out_banks = Banks([6, 7], bfree)
        work = [(r, h) for r in range(4) for h in range(8)]
        scored, turned = {}, {}

        def score(i):
            r, h = work[i]
            p = slice(64 * (h % 2), 64 * (h % 2) + 64)
            b, _, free = at_banks.take()
            t = P.mm(ps[:, b], QK[p, h // 2, 128 * r:128 * r + 128], QK[p, 4 + h // 2, :], True, True, [free, qt], True)
            il, l, free = lg.take()
            d = 7 - 2 * r
            t = P.stt(l, ps[:, b], 0.125, BT[:, h, d:d + 8].rearrange("p d j -> p (d j)"), MUL, ADD, [t, tb, free])
            at_banks.free[b] = [t]
            t2 = dve.put(lambda e, l=l, o=MX[:, i:i + 1]: e.tensor_reduce(o, l, AX.X, MAX, negate=True), [t])
            ip, e, free = pm.take()
            t = P.a(e, l, ACT.Exp, [t2, free], bias=MX[:, i:i + 1], accum=SU[:, i:i + 1])
            lg.free[il] = [t]
            scored[i] = (ip, e, t)

        def turn(i):
            ip, e, t = scored[i]
            b, _, free = at_banks.take()
            for k in range(4):
                t1 = P.tr(ps[:, b, 128 * k:128 * k + 128], e[:, 128 * k:128 * k + 128], ident, [t, free], k == 3)
            pm.free[ip] = [t1]
            it, q, free = pt.take()
            if i % 2:
                t1 = P.a(q, ps[:, b], ACT.Copy, [t1, free])
            else:
                t1 = P.cp(dve, q, ps[:, b], [t1, free])
            at_banks.free[b] = [t1]
            turned[i] = (it, q, t1)

        ob = {}
        att = []

        def value(i):
            r, h = work[i]
            if h == 0:
                b, _, free = out_banks.take()
                ob[r] = (b, free)
            b, free = ob[r]
            it, q, t = turned[i]
            for k in range(4):
                t1 = P.mm(ps[:, b, 64 * h:64 * h + 64], q[:, 128 * k:128 * k + 128], AV[:, k, 64 * h:64 * h + 64], k == 0, k == 3,
                          [t, free, av], k == 3)
            pt.free[it] = [t1]
            if h < 7:
                return
            s = SU[:, 8 * r:8 * r + 8]
            t2 = P.recip(s, s, [scored[i][2]])
            t2 = P.tt(dve, AO[:, :].rearrange("p (h d) -> p h d", h=8), ps[:, b].rearrange("p (h d) -> p h d", h=8),
                      s.rearrange("p (h a) -> p h a", a=1).to_broadcast([128, 8, 64]), MUL, [t1, t2, att])
            bfree[b] = [t2]
            i1, x, free = tmp.take()
            t = P.a(x, AO[:, :], ACT.Square, [t2, free], accum=SQ[:, r:r + 1])
            tmp.free[i1] = [t]
            t = P.a(SQ[:, r:r + 1], SQ[:, r:r + 1], ACT.Sqrt, [t], bias=prm("eps"), scale=1.0 / 512)
            t = P.recip(SQ[:, r:r + 1], SQ[:, r:r + 1], [t])
            t = P.ts(dve, AO[:, :], AO[:, :], SQ[:, r:r + 1], None, MUL, w=[t])
            b, _, free = at_banks.take()
            for k in range(4):
                t1 = P.tr(ps[:, b, 128 * k:128 * k + 128], AO[:, 128 * k:128 * k + 128], ident, [t, free], k == 3)
            new = []
            for k in range(4):
                new.append(P.a(AT[:, k, 128 * r:128 * r + 128], ps[:, b, 128 * k:128 * k + 128], ACT.Copy, [t1], scale=prm("aog", k)))
            at_banks.free[b] = new
            att.append(t1)
            atts.append(new)

        atts = []
        for i in range(len(work) + 2):
            if i < len(work):
                score(i)
            if 1 <= i < len(work) + 1:
                turn(i - 1)
            if i >= 2:
                value(i - 2)

        P.barrier()
        x = tail
        ATT, x = P.place("ATT", [128, 32, 64], F32, x)
        OO, x = P.place("OO", [128, 4, S], F32, x)
        names = ("GG", "GC", "EG", "ED", "BE", "NB", "BG", "GL", "SC1", "SC2")
        sc = {}
        for name in names:
            sc[name], x = P.place(f"d{name}", [128, 2, 4, 4], F32, x)
        EH, x = P.place("EH", [128, 2, 32], F32, x)
        GT, x = P.place("GT", [128, 2, 128], F32, x)
        QS, x = P.place("QS", [128, 2, 4, S], F32, xs0)
        WT, x = P.place("WT", [128, 2, 32, 64], F32, x)
        UV, x = P.place("UV", [128, 32, 128], F32, base)
        KK, x = P.place("KKT", [128, 4, 4, 128], F32, x)
        assert x <= base + 24576
        MM, x = P.place("MM", [128, 32, 64], F32, cut0)
        TR, x = P.place("TR", [128, 32, 64], F32, x)
        TX, x = P.place("TX", [128, 32, 64], F32, x)
        ZX, x = P.place("ZX", [128, 32, 64], F32, x)
        KG, x = P.place("KG", [128, 32, 128], F32, ring0)
        SS2, x = P.place("SS2", [128, 2, 8, 128], F32, DVo := base + 16384 + 8192 + 16384)
        VN, x = P.place("VN", [128, 2, 4, 128], F32, cut0)

        def flat(name):
            return sc[name][:, :, :, :].rearrange("p d n h -> p (d n h)")

        def of_ab(k):
            return AB[:, :, 8 * k:8 * k + 8].rearrange("p n (d h) -> p d n h", d=2)

        def row(k):
            return R8[:, k].rearrange("p (d a h) -> p d a h", d=2, a=1).to_broadcast([128, 2, 4, 4])

        full = {k: sc[k][:, :, :, :] for k in names}
        t = P.tt(dve, full["SC1"], of_ab(0), row(0), ADD, [ab, t_r8])
        t1 = P.ts(dve, flat("SC2"), flat("SC1"), -1.0, None, MUL, w=[t])
        t1 = P.tt(dve, flat("SC2"), flat("SC2"), flat("SC1"), MAX, [t1])
        t1 = P.a(flat("SC2"), flat("SC2"), ACT.Exp, [t1], scale=-1.0)
        t1 = P.a(flat("SC2"), flat("SC2"), ACT.Ln, [t1], bias=prm("one"))
        t = P.ts(dve, flat("SC1"), flat("SC1"), 0.0, None, MAX, w=[t1])
        t = P.tt(dve, flat("SC1"), flat("SC1"), flat("SC2"), ADD, [t])
        t1 = P.a(R8[:, 1], R8[:, 1], ACT.Exp, [t_r8])
        t = P.tt(dve, full["GG"], full["SC1"], row(1), MUL, [t, t1])
        t_g = P.ts(dve, flat("GG"), flat("GG"), -1.0, None, MUL, w=[t])
        t_be = P.a(full["BE"], of_ab(1), ACT.Sigmoid, [ab])
        b, _, free = bank.take()
        P.mm(ps[:, b, 0:16], cst("cumf", 128), flat("GG")[:, 0:16], True, True, [t_g, free])
        P.mm(ps[:, b, 16:32], cst("cumb", 128), flat("GG")[:, 16:32], True, True)
        P.mm(ps[:, b, 32:64], blk, flat("GG"), True, True)
        P.mm(ps[:, b, 64:96], cst("half", 128), flat("GG"), True, True)
        t = P.mm(ps[:, b, 96:128], cst("half", 128, 128), flat("GG"), True, True, inc=True)
        t_gc = P.cp(dve, flat("GC"), ps[:, b, 0:32], [t])
        t_gl = P.tt(dve, flat("GL"), ps[:, b, 32:64], flat("GC"), SUB, [t_gc])
        t_eh = P.a(EH[:, :, :].rearrange("p a b -> p (a b)"), ps[:, b, 64:128], ACT.Exp, [t_gl])
        bank.free[b] = [t_gl, t_eh]
        t_e = P.a(flat("EG"), flat("GC"), ACT.Exp, [t_gc])
        t_ed = P.a(flat("ED"), flat("GL"), ACT.Exp, [t_gl])
        t_nb = P.ts(dve, flat("NB"), flat("BE"), -1.0, None, MUL, w=[t_be])
        t_bg = P.tt(dve, flat("BG"), flat("BE"), flat("EG"), MUL, [t_be, t_e])

        def spread(name, d, n, width):
            return sc[name][:, d, n, :].rearrange("p (h a) -> p h a", a=1).to_broadcast([128, 4, width])

        tv, tk = {}, []
        for n in range(4):
            b, _, free = bank.take()
            for h in range(4):
                t = P.tr(ps[:, b, 128 * h:128 * h + 128], DV[:, h, 128 * n:128 * n + 128], ident, [free, dt_], h == 3)
            o = ps[:, b].rearrange("p (h v) -> p h v", h=4)
            for d in range(2):
                i0 = 16 * d + 4 * n
                tv[d, n] = P.tt(dve, UV[:, i0:i0 + 4], o, spread("BE", d, n, 128), MUL, [t, t_be])
            bank.free[b] = [tv[0, n], tv[1, n]]
            b, _, free = bank.take()
            for h in range(4):
                t = P.tr(ps[:, b, 128 * h:128 * h + 128], KQ[:, 0, h, 128 * n:128 * n + 128], ident, [free, dt_], h == 3)
            tk.append(P.a(KK[:, n], ps[:, b].rearrange("p (h v) -> p h v", h=4), ACT.Copy, [t]))
            bank.free[b] = [tk[-1]]
        tkg = {}
        for d in range(2):
            for n in range(4):
                i0 = 16 * d + 4 * n
                tkg[d, n] = P.tt(pool, KG[:, i0:i0 + 4], KK[:, n], spread("BG", d, n, 128), MUL, [tk[n], t_bg])
        tq = []
        for d in range(2):
            for h in range(4):
                b, _, free = bank.take()
                for n in range(4):
                    t = P.mm(ps[:, b, 128 * n:128 * n + 128], sc["EG"][:, d, n, h:h + 1].to_broadcast([128, 128]), ident, True, True,
                             [free, t_e], n == 3)
                tq.append(P.tt(dve, QS[:, d, h], ps[:, b], KQ[:, 1, h], MUL, [t, dt_]))
                bank.free[b] = [tq[-1]]
        tm = {}
        gt_slot = Slots([GT[:, 0], GT[:, 1]])
        for n in range(4):
            bk, _, free = bank.take()
            for h in range(4):
                for p in (0, 64):
                    f = 128 * n + p
                    t_kk = P.mm(ps[p:p + 64, bk, 128 * h:128 * h + 128].rearrange("p (a j) -> p a j", a=2), KQ[:, 0, h, f:f + 64],
                                KQ[:, :, h, f:f + 64], True, True, [free], h == 3 and p > 0)
            o = ps[:, bk].rearrange("p (h a j) -> p h a j", h=4, a=2)
            for d in range(2):
                i0 = 16 * d + 4 * n
                b, _, free = bank.take()
                for h in range(4):
                    ig, g, gfree = gt_slot.take()
                    t = P.ts(dve, g, blk, sc["GC"][:, d, n, h:h + 1], None, MUL, w=[t_gc, gfree])
                    t = P.mm(ps[:, b, 64 * h:64 * h + 64], g, cst("i2", 64), True, True, [free, t], True)
                    gt_slot.free[ig] = [t]
                i1, y, free = tmp.take()
                y1 = y[:, 0:256].rearrange("p (h j) -> p h j", h=4)
                y2 = y[:, 256:512].rearrange("p (h j) -> p h j", h=4)
                t = P.tt(dve, y1, ps[:, b, 0:256].rearrange("p (h j) -> p h j", h=4), spread("GC", d, n, 64), SUB, [t, free])
                bank.free[b] = [t]
                t2 = P.ts(dve, y2, y1, 0.0, None, MIN, w=[t])
                t1 = P.ts(dve, y1, y1, 0.0, None, MAX, w=[t2])
                t1 = P.a(y1, y1, ACT.Exp, [t1], scale=-1.0)
                t2 = P.a(y2, y2, ACT.Exp, [t2])
                t1 = P.tt(dve, y1, y1, o[:, :, 0], MUL, [t1, t_kk])
                tm[d, n] = P.tt(dve, MM[:, i0:i0 + 4], y1, spread("NB", d, n, 64), MUL, [t1, t_nb])
                t2 = P.tt(dve, y2, y2, o[:, :, 1], MUL, [t2, t_kk])
                t3 = P.tt(dve, ATT[:, i0:i0 + 4], y2, mask("incl" if d else "incu", 4), MUL, [t2])
                tmp.free[i1] = [tm[d, n], t3]
                tm["a", d, n] = t3
                bank.free[bk] = [t1, t2]
        tris = [[] for _ in range(4)]
        mbs = Slots([TMPS[i][:, :] for i in range(4)])
        for i in range(4):
            mbs.free[i] = [tm["a", 0, 3], tm["a", 1, 3], tm[1, 3], tm[0, 3]]
        gens = []
        for i in range(4):
            d = i // 2
            n = 2 * (i % 2)
            gens.append(inverse(MM, TR, TX, ZX, 8 * i, 8, "up" if d else "lo", [tm[d, n], tm[d, n + 1]], bank, "T", mbs, tris[i]))
        drain(*gens)
        tu, tw = [], []
        for i0 in range(0, 32, 4):
            d, n = i0 // 16, i0 % 16 // 4
            b, _, free = bank.take()
            for q in range(4):
                for p in (0, 64):
                    t = P.mm(ps[p:p + 64, b, 128 * q:128 * q + 128], TR[p:p + 64, i0 + q], UV[p:p + 64, i0 + q], True, True,
                             [free, tris[i0 // 8], tv[d, n]], q == 3 and p > 0)
            tu.append(P.cp(dve, UV[:, i0:i0 + 4], ps[:, b].rearrange("p (q v) -> p q v", q=4), [t]))
            bank.free[b] = [tu[-1]]
        for i0 in range(0, 32, 8):
            bs = [bank.take() for _ in range(2)]
            d, n = i0 // 16, i0 % 16 // 4
            for q in range(8):
                for a, p in enumerate((0, 64)):
                    t = P.mm(ps[:, bs[a][0], 64 * q:64 * q + 64], KG[p:p + 64, i0 + q], TR[p:p + 64, i0 + q], True, True,
                             [bs[0][2], bs[1][2], tkg[d, n], tkg[d, n + 1]], q == 7 and a == 1)
            for a in range(2):
                tw.append(P.a(WT[:, a, i0:i0 + 8], ps[:, bs[a][0]].rearrange("p (q j) -> p q j", q=8), ACT.Copy, [t, projected]))
                bank.free[bs[a][0]] = [tw[-1]]
        tkd = []
        for d in range(2):
            for n in range(4):
                i0 = 16 * d + 4 * n
                tkd.append(P.tt(pool, KG[:, i0:i0 + 4], KK[:, n], spread("ED", d, n, 128), MUL, [t_ed, pe.now()]))
        P.barrier()
        st = P.memset(dve, SS2[:, 0], 0.0)
        tso = [st, st]
        to = {}
        tpool = None
        for s in range(8):
            geo = []
            for d in range(2):
                ch = s if d == 0 else 7 - s
                geo.append((ch, ch // 2, ch % 2, slice(64 * (ch % 2), 64 * (ch % 2) + 64)))
            for d in range(2):
                ch, n, hf, p = geo[d]
                for h in range(4):
                    it = 16 * d + 4 * n + h
                    P.mm(ps[p, d, 128 * h:128 * h + 128], WT[:, hf, it], SS2[:, 0, 4 * d + h], True, True, [tso[d], bfree[d]])
                for h in range(4):
                    ta = P.mm(ps[:, 4 + d, 64 * h:64 * h + 64], SS2[:, 0, 4 * d + h], QS[:, d, h, 64 * ch:64 * ch + 64], h == 0, False,
                              [bfree[4 + d]], h == 3, skip=True)
                geo[d] = geo[d] + (ta,)
            tp = []
            for d in range(2):
                ch, n, hf, p, ta = geo[d]
                i0 = 16 * d + 4 * n
                tn = P.tt(dve, VN[p, d], UV[p, i0:i0 + 4], ps[p, d].rearrange("p (h v) -> p h v", h=4), SUB, [ta])
                bfree[d] = [tn]
                tp.append(P.tt(pool, SS2[:, 1, 4 * d:4 * d + 4], SS2[:, 0, 4 * d:4 * d + 4],
                               EH[:, hf, i0:i0 + 4].rearrange("p (h a) -> p h a", a=1).to_broadcast([128, 4, 128]), MUL,
                               [tso[d]]))
                for h in range(4):
                    t = P.mm(ps[:, 2 + d, 128 * h:128 * h + 128], KG[p, i0 + h], VN[p, d, h], True, True, [tn, bfree[2 + d]], h == 3)
                geo[d] = geo[d] + (t,)
            for d in range(2):
                ch, n, hf, p, ta, t = geo[d]
                i0 = 16 * d + 4 * n
                tso[d] = P.tt(dve, SS2[:, 0, 4 * d:4 * d + 4], SS2[:, 1, 4 * d:4 * d + 4],
                              ps[:, 2 + d].rearrange("p (h v) -> p h v", h=4), ADD, [t, tp[d]])
                bfree[2 + d] = [tso[d]]
                for h in range(4):
                    t = P.mm(ps[:, 4 + d, 64 * h:64 * h + 64], VN[p, d, h], ATT[p, i0 + h], False, h == 3, inc=h == 3, skip=True)
                o = ps[:, 4 + d, 0:256].rearrange("p (h j) -> p h j", h=4)
                dst = OO[:, :, 64 * ch:64 * ch + 64]
                if ch in to:
                    to[ch] = P.tt(dve, dst, o, dst, ADD, [t, to[ch]])
                else:
                    to[ch] = P.a(dst, o, ACT.Copy, [t])
                bfree[4 + d] = [to[ch]]
        P.barrier()
        xt = []
        for k in range(4):
            xt.append(split(AT[:, k], k, None))
        todo, xs = [], []
        for h in range(4):
            i, x, free = tmp.take()
            t = P.a(x, OO[:, h], ACT.Square, [free])
            b, _, free = bank.take()
            t = P.mm(ps[:, b], ones, x, True, True, [t, free], True)
            todo.append((x, ps[:, b], [t]))
            xs.append((h, i, x, b))
        first, second = P.rsqrts(todo, prm("eps"), 1.0 / 128)
        for (h, i, x, b), t1, t in zip(xs, first, second):
            bank.free[b] = [t1]
            t = P.tt(dve, x, x, OO[:, h], MUL, [t])
            t = P.stt(x, x, prm("dng"), ZG[:, h], MUL, MUL, [t])
            xt.append(split(x, 4 + h, t))
            tmp.free[i] = xt[-1]

        def expert(name, e_):
            if name == "down":
                pat, pat1 = "(j p) n -> p j n", "a (j p) n -> p (a j) n"
            else:
                pat, pat1 = "(p k) n -> p k n", "a (p k) n -> p (a k) n"
            w = A[f"e_{name}"]
            if e_ < 64:
                return w[e_].rearrange(pat, p=128)

            def src(e):
                if e_ not in regs:
                    regs[e_] = e.value_load(OVI[0:1, e_ - 64:e_ - 63], min_val=0, max_val=63)
                return w[bass.ds(regs[e_], 1)].rearrange(pat1, p=128)
            return src

        regs = {}
        todo = []
        for i in range(65):
            todo += [("gate", i), ("up", i)] if i < 64 else []
            todo += [("down", i - 1)] if i else []
        for i in range(64, 2 * NP, 2):
            todo += [(x, i + z) for x, z in (("gate", 0), ("up", 0), ("gate", 1), ("up", 1), ("down", 0), ("down", 1))]
        E = Ring(P, "s_e", [P.place(f"ew{i}", [128, 2048], F32, base + 8192 * i)[0] for i in range(11)],
                 [(expert(*x), 2 if x[0] == "down" else KT) for x in todo], [pe.now(), dve.now(), act.now(), pool.now()], 192)
        gemm(KT, residual(ht), xt)
        E.load(11)

        P.barrier()
        XN, x = P.place("XN", [128, KT, S], F32, xs0)
        TK, x = P.place("TK", [128, 4, D], F32, x)
        HT, x = P.place("HT", [128, 4, D], F32, ring0)
        XG = []
        for i in range(3):
            y, x = P.place(f"XG{i}", [128, D], F32, x)
            XG.append(y)
        RW, x = P.place("RW", [128, KT, 72], F32, x)
        RB, x = P.place("RB", [128, 72], F32, x)
        HID2, x = P.place("HID2", [128, 2, 2, 64], F32, x)
        SIL, x = P.place("SIL", [128, 2, 2, 64], F32, x)
        GATES, x = P.place("GATES", [128, 2, 4], F32, x)
        SRC, x = P.place("SRC", [128, NP], I32, x)
        DST, x = P.place("DST", [128, NP], I32, x)
        OVI, x = P.place("OVI", [1, NOV + 1], I32, x)
        PAIR, x = P.place("PAIR", [128, 2, 4], I32, x)
        ADDR, x = P.place("ADDR", [128, 2, 4], I32, x)
        scratch0 = x
        s_r = P.sem("s_r")
        P.dma(sp, RW[:, :, :].rearrange("p k n -> p (k n)"), A["router_w"], s_r)
        t_rw = P.dma(sp, RB[:, :], A["router_b"], s_r)
        xtok = nc.dram_tensor("xtok", [S, D], F32, kind="Internal").ap()
        otok = nc.dram_tensor("otok", [2 * S, D], F32, kind="Internal").ap()
        rmap = nc.dram_tensor("rmap", [ROWS, 1], I32, kind="Internal").ap()
        t = P.memset(pool, SRC[:, :], NOWHERE)
        s_m = P.sem("s_m")
        t_m0 = P.dma(sp, rmap.rearrange("(p b) a -> p (b a)", p=128), SRC[:, :], s_m, [t], store=True)
        t_xg = [P.memset(pool, XG[i][:, :], 0.0) for i in range(3)]

        ia, acc, ta = square_sum([H[:, k] for k in range(KT)], ht)
        ir, r, tr = rstd_of(acc, D, "eps", ta)
        tmp.free[ia] = [pe.now()]
        xn = [P.stt(XN[:, k], H[:, k], prm("ln2", k), r, MUL, MUL, [tr, ht[k]]) for k in range(KT)]
        tmp.free[ir] = [xn[-1]]
        b, _, free = bank.take()
        for n in range(4):
            for k in range(KT):
                t = P.mm(ps[:, b, 72 * n:72 * n + 72], XN[:, k, 128 * n:128 * n + 128], RW[:, k], k == 0, k == KT - 1,
                         [free, xn, t_rw], n == 3 and k == KT - 1)
        y = scratch0
        sc = {}

        def small(name, *shape):
            nonlocal y
            sc[name], y = P.place("r" + name, [128] + list(shape), F32, y)
            return sc[name]

        def over(a, n):
            return a.rearrange("p (n a) -> p n a", a=1).to_broadcast([128, 4, n])

        def along(name, n):
            return cst(name, n).rearrange("p (a j) -> p a j", a=1).to_broadcast([128, 4, n])

        LGT = small("LGT", 4, 72)
        t_l = P.tt(dve, LGT[:, :, :], ps[:, b, 0:288].rearrange("p (n j) -> p n j", n=4),
                   RB[:, :].rearrange("p (a j) -> p a j", a=1).to_broadcast([128, 4, 72]), ADD, [t])
        bank.free[b] = [t_l]
        th, tx = [], []
        for n in range(4):
            for half in range(2):
                for srcs, dst, toks in ((H, HT, th), (XN, TK, tx)):
                    b, _, free = bank.take()
                    for q in range(4):
                        t = P.tr(ps[:, b, 128 * q:128 * q + 128], srcs[:, 4 * half + q, 128 * n:128 * n + 128], ident,
                                 [free, xn, ht], q == 3)
                    toks.append(P.a(dst[:, n, 512 * half:512 * half + 512], ps[:, b], ACT.Copy, [t]))
                    bank.free[b] = [toks[-1]]
        s_x = P.sem("s_x")
        t_xt = P.dma(sp, xtok.rearrange("(n p) d -> p n d", p=128), TK[:, :, :], s_x, [tx], store=True)

        def first_max(v, n, w, name):
            m, i, oh = small(name + "m", 4), small(name + "i", 4), small(name + "o", 4, n)
            t1 = P.red(m[:, :], v, MAX, [w])
            t = P.tt(dve, oh[:, :, :], v, over(m[:, :], n), ALU.is_equal, [t1])
            t = P.stt(oh[:, :, :], oh[:, :, :], -100.0, along(f"iota{n}", n), MUL, ADD, [t])
            t = P.red(i[:, :], oh[:, :, :], MIN, [t])
            t = P.ts(dve, i[:, :], i[:, :], 100.0, None, ADD, w=[t])
            t = P.tt(dve, oh[:, :, :], along(f"iota{n}", n), over(i[:, :], n), ALU.is_equal, [t])
            return m, i, oh, t

        gl = LGT[:, :, 0:8]
        gm, gi, goh, t = first_max(gl, 8, t_l, "g")
        ge, gs = small("ge", 4, 8), small("gs", 4)
        t1 = P.tt(dve, ge[:, :, :], gl, over(gm[:, :], 8), SUB, [t])
        t1 = P.a(ge[:, :, :], ge[:, :, :], ACT.Exp, [t1])
        t1 = P.red(gs[:, :], ge[:, :, :], ADD, [t1])
        t_gp = P.recip(gs[:, :], gs[:, :], [t1])
        pr, ig = small("pr", 4, 8, 8), small("ig", 4, 8)
        tr_ = []
        for n in range(4):
            tr_.append(P.tt(dve, pr[:, n], LGT[:, n, 8:72].rearrange("p (g e) -> p g e", g=8),
                            goh[:, n].rearrange("p (g a) -> p g a", a=1).to_broadcast([128, 8, 8]), MUL, [t]))
        t = P.red(ig[:, :, :], pr[:, :, :, :].rearrange("p n g e -> p n e g"), ADD, tr_)
        m1, i1, o1, t = first_max(ig[:, :, :], 8, t, "a")
        t = P.stt(ig[:, :, :], o1[:, :, :], -1e30, ig[:, :, :], MUL, ADD, [t])
        m2, i2, o2, t = first_max(ig[:, :, :], 8, t, "b")
        ex, dn = small("ex", 4), small("dn", 4)
        t1 = P.tt(dve, ex[:, :], m2[:, :], m1[:, :], SUB, [t])
        t1 = P.a(ex[:, :], ex[:, :], ACT.Exp, [t1])
        t2 = P.ts(dve, dn[:, :], ex[:, :], 1.0, None, ADD, w=[t1])
        t2 = P.recip(dn[:, :], dn[:, :], [t2])
        t2 = P.tt(dve, dn[:, :], dn[:, :], gs[:, :], MUL, [t2, t_gp])
        t2 = P.cp(dve, GATES[:, 0], dn[:, :], [t2])
        t_gate = P.tt(dve, GATES[:, 1], dn[:, :], ex[:, :], MUL, [t2])
        eid, oh = [], []
        for s, i in enumerate((i1, i2)):
            e, o = small(f"eid{s}", 4), small(f"oh{s}", 4, 64)
            t1 = P.stt(e[:, :], gi[:, :], 8.0, i[:, :], MUL, ADD, [t])
            t1 = P.tt(dve, o[:, :, :], along("iota64", 64), over(e[:, :], 64), ALU.is_equal, [t1])
            eid.append(e)
            oh.append(o)
        mm = small("mm", 4, 64)
        t_mm = P.tt(dve, mm[:, :, :], oh[0][:, :, :], oh[1][:, :, :], ADD, [t1])
        b, _, free = bank.take()
        for n in range(4):
            for m in range(n):
                P.mm(ps[:, b, 64 * n:64 * n + 64], ones, mm[:, m], m == 0, False, [t_mm, free])
            P.mm(ps[:, b, 64 * n:64 * n + 64], cst("tri", 128), mm[:, n], n == 0, True, [t_mm, free])
        for m in range(4):
            t = P.mm(ps[:, b, 256:320], ones, mm[:, m], m == 0, m == 3, inc=m == 3)
        rank, cnt, ob, cum = small("rank", 4, 64), small("cnt", 64), small("ob", 64), small("cum", 64)
        t1 = P.cp(dve, rank[:, :, :], ps[:, b, 0:256].rearrange("p (n j) -> p n j", n=4), [t])
        t2 = P.cp(dve, cnt[:, :], ps[:, b, 256:320], [t])
        bank.free[b] = [t1, t2]
        t3 = P.ts(dve, ob[:, :], cnt[:, :], 64.0, None, ALU.is_gt, w=[t2])
        for lim in range(128, S, 64):
            t3 = P.stt(ob[:, :], cnt[:, :], float(lim), ob[:, :], ALU.is_gt, ADD, [t3])
        t3 = dve.put(lambda e: e.tensor_tensor_scan(cum[:, :], cst("ones", 64), ob[:, :], 0.0, MUL, ADD), [t3])
        ovf = small("ovf", NOV, 64)
        ovs = small("ovs", NOV)
        t4 = P.tt(dve, ovf[:, :, :], cum[:, :].rearrange("p (a j) -> p a j", a=1).to_broadcast([128, NOV, 64]),
                  cst("iota16", NOV).rearrange("p (j a) -> p j a", a=1).to_broadcast([128, NOV, 64]), ALU.is_le, [t3])
        t4 = P.red(ovs[:, :], ovf[:, :, :], ADD, [t4])
        t4 = P.ts(dve, ovs[:, :], ovs[:, :], 63.0, None, MIN, w=[t4])
        t4 = P.cp(dve, OVI[:, 0:NOV], ovs[0:1, :], [t4])
        t_ov = P.cp(dve, OVI[:, NOV:NOV + 1], cum[0:1, 63:64], [t3, t4])
        t5 = P.tt(dve, ob[:, :], cum[:, :], ob[:, :], SUB, [t3])
        addr = small("addr", 2, 4)
        big, rk, xo, qq, q1 = small("big", 4, 64), small("rk", 4), small("xo", 4), small("qq", 4), small("q1", 4)
        first, later = small("first", 4), small("later", 4)
        t = None
        for s in range(2):
            t = P.tt(dve, big[:, :, :], oh[s][:, :, :], rank[:, :, :], MUL, [t1, t_mm, t])
            t = P.red(rk[:, :], big[:, :, :], ADD, [t])
            t = P.tt(dve, big[:, :, :], oh[s][:, :, :], ob[:, :].rearrange("p (a j) -> p a j", a=1).to_broadcast([128, 4, 64]), MUL, [t, t5])
            t = P.red(xo[:, :], big[:, :, :], ADD, [t])
            t = P.tt(dve, big[:, :, :], oh[s][:, :, :], along("slot64", 64), MUL, [t])
            t = P.red(first[:, :], big[:, :, :], ADD, [t])
            t = P.ts(dve, qq[:, :], rk[:, :], 64.0, None, ALU.is_ge, w=[t])
            t = P.cp(dve, q1[:, :], qq[:, :], [t])
            for lim in range(128, S, 64):
                t = P.stt(qq[:, :], rk[:, :], float(lim), qq[:, :], ALU.is_ge, ADD, [t])
            t = P.tt(dve, xo[:, :], xo[:, :], qq[:, :], ADD, [t])
            t = P.ts(dve, xo[:, :], xo[:, :], -1.0, None, ADD, w=[t])
            ohx = big[:, :, 0:NOV]
            t = P.tt(dve, ohx, along("iota16", NOV), over(xo[:, :], NOV), ALU.is_equal, [t])
            t = P.tt(dve, ohx, ohx, along("slot16", NOV), MUL, [t])
            t = P.red(later[:, :], ohx, ADD, [t])
            t = P.tt(dve, later[:, :], later[:, :], first[:, :], SUB, [t])
            t = P.tt(dve, later[:, :], later[:, :], q1[:, :], MUL, [t])
            t = P.tt(dve, first[:, :], first[:, :], later[:, :], ADD, [t])
            t = P.stt(rk[:, :], qq[:, :], -64.0, rk[:, :], MUL, ADD, [t])
            t = P.stt(addr[:, s], rk[:, :], float(NP), first[:, :], MUL, ADD, [t])
        t = P.cp(dve, ADDR[:, :, :], addr[:, :, :], [t])
        for s in range(2):
            for n in range(4):
                t2 = P.ts(dve, addr[:, s, n:n + 1], cst("gidx", 1), float(512 * s + 128 * n), None, ADD, w=[t])
        t_pair = P.cp(dve, PAIR[:, :, :], addr[:, :, :], [t2])
        s_mp = P.sem("s_mp")
        pool.wait(t_m0, t, t_pair)
        for s in range(2):
            for n in range(4):
                P.counts[s_mp.num] = P.counts.get(s_mp.num, 0) + 16
                pool.list.append(lambda e, s=s, n=n: e.indirect_dma_start(
                    out=rmap, out_offset=bass.IndirectOffsetOnAxis(ap=ADDR[:, s, n:n + 1], axis=0),
                    in_=PAIR[:, s, n:n + 1], in_offset=None).then_inc(s_mp, 16))
        t_mp = (s_mp, P.counts[s_mp.num])
        P.stores.append(t_mp)
        t = P.dma(sp, DST[:, :], rmap.rearrange("(p b) a -> p (b a)", p=128), s_m, [t_mp])
        fm, fq = small("fm", NP), small("fq", NP)
        t_dst = t
        t = P.cp(dve, fm[:, :], DST[:, :], [t])
        t = P.ts(dve, fq[:, :], fm[:, :], 512.0, -512.0, ALU.is_ge, MUL, [t])
        t = P.tt(dve, fm[:, :], fm[:, :], fq[:, :], ADD, [t])
        t_src = P.cp(dve, SRC[:, :], fm[:, :], [t])

        sent = pe.now()
        XT, y = P.place("XT", [128, 2, KT, 128], F32, PRM_END)
        OUTB, y = P.place("OUTB", [128, 2, D], F32, y)
        s_gx = [P.sem(f"s_gx{i}") for i in range(3)]
        s_ox = [P.sem(f"s_ox{i}") for i in range(2)]
        s_gy, s_oy = P.sem("s_gy"), P.sem("s_oy")
        MARK, y = P.place("MARK", [1, NP], F32, y)
        gfree = [[t_xg[i]] for i in range(3)]
        gathered = {}

        def gather(q):
            if q >= NP:
                return
            i = q % 3
            pool.wait(gfree[i], t_xt, t_src)
            sem = s_gy if q > 32 else s_gx[i]
            gathered[q] = P.counted_up(pool, sem, q > 32)
            pool.list.append(lambda e: e.indirect_dma_start(
                out=XG[i][:, :], out_offset=None, in_=xtok,
                in_offset=bass.IndirectOffsetOnAxis(ap=SRC[:, q:q + 1], axis=0),
                bounds_check=S - 1, oob_is_err=False).then_inc(sem, 16))

        xfree = [[sent, th, tx, xn], [sent, th, tx, xn]]
        turned = {}

        def turn_x(q):
            if q >= 32 and not more:
                return
            i, z = q % 3, q % 2
            got = []
            v = XG[i][:, :].rearrange("p (f k) -> p k f", k=KT)
            for half in range(2):
                b = 2 + half
                for k in range(4):
                    t = P.tr(ps[:, b, 128 * k:128 * k + 128], v[:, 4 * half + k], ident, [gathered[q], bfree[b]], k == 3)
                o, x = ps[:, b], XT[:, z, 4 * half:4 * half + 4].rearrange("p k r -> p (k r)")
                t1 = P.cp(dve, x, o, [t, xfree[z]]) if half else P.a(x, o, ACT.Copy, [t, xfree[z]])
                bfree[b] = [t1]
                got.append(t1)
            gfree[i] = [t]
            turned[q] = got

        hfree = [[], []]
        ofree = [[sent, th, tx, xn], [sent, th, tx, xn]]
        hidden = {}

        def gate_up(i):
            q, z, r = i // 2, i // 2 % 2, slice(64 * (i % 2), 64 * (i % 2) + 64)
            b = i % 2
            for part in range(2):
                wv, tw, done = E.next()
                wv = wv[:, :].rearrange("p (k n) -> p k n", k=KT)
                for m in range(2):
                    o = ps[:, b, 128 * part + 64 * m:128 * part + 64 * m + 64]
                    for k in range(KT):
                        t = P.mm(o, wv[:, k, 128 * m:128 * m + 128], XT[:, z, k, r], k == 0, k == KT - 1,
                                 [tw, bfree[b], turned[q]], m == 1 and k == KT - 1)
                done(t)
            xfree[z] = [t]
            g = ps[:, b, 0:128].rearrange("p (m r) -> p m r", m=2)
            u = ps[:, b, 128:256].rearrange("p (m r) -> p m r", m=2)
            ts = P.a(SIL[:, b], g, ACT.Silu, [t, hfree[b]])
            hidden[i] = P.tt(dve, HID2[:, b], u, SIL[:, b], MUL, [ts, t, hfree[b]])
            bfree[b] = [hidden[i]]

        def down(i):
            q, z, r = i // 2, i // 2 % 2, slice(64 * (i % 2), 64 * (i % 2) + 64)
            wv, tw, done = E.next()
            wv = wv[:, :].rearrange("p (j n) -> p j n", j=2)
            for c_ in range(2):
                b = 4 + 2 * z + c_
                for j in range(2):
                    t = P.mm(ps[r, b], HID2[:, i % 2, j], wv[:, j, 512 * c_:512 * c_ + 512], j == 0, j == 1,
                             [tw, hidden[i], bfree[b]], j == 1)
                if i % 2:
                    n = slice(512 * c_, 512 * c_ + 512)
                    to = P.cp(dve, OUTB[:, z, n], ps[:, b], [t, ofree[z]]) if c_ else P.a(OUTB[:, z, n], ps[:, b], ACT.Copy, [t, ofree[z]])
                    bfree[b] = [to]
                    pool.wait(to)
            done(t)
            hfree[i % 2] = [t]
            if i % 2:
                sem = s_oy if more else s_ox[z]
                ofree[z] = [P.counted_up(pool, sem, bool(more))]
                pool.list.append(lambda e: e.indirect_dma_start(
                    out=otok, out_offset=bass.IndirectOffsetOnAxis(ap=DST[:, q:q + 1], axis=0),
                    in_=OUTB[:, z], in_offset=None, bounds_check=2 * S - 1, oob_is_err=False).then_inc(sem, 16))
                if more:
                    ofree[z] = [P.memset(pool, MARK[:, q:q + 1], 0.0, [ofree[z]])]

        more = []
        gather(0)
        gather(1)
        turn_x(0)
        for i in range(65):
            if i < 64:
                if i % 2 == 0 and i < 62:
                    gather(i // 2 + 2)
                gate_up(i)
                if i % 2:
                    turn_x(i // 2 + 1)
            if i > 0:
                down(i - 1)
        first_sent = [ofree[0], ofree[1]]
        more.append(True)
        over_ = P.counted(OVI[0:1, NOV:NOV + 1], NOV, [t_ov])
        for q in range(32, NP):
            with P.when(over_, 2 * (q - 32)):
                E.load(6 * q + 6)
                gather(q + 1)
                turn_x(q)
                gate_up(2 * q)
                gate_up(2 * q + 1)
                down(2 * q)
                down(2 * q + 1)
                pool.wait(gathered.get(q + 1))
        P.barrier()
        OT, y = P.place("OT", [128, 2, 4, D], F32, xs0)
        s_ot = P.sem("s_ot")
        t_o = P.dma(sp, OT[:, :, :, :], otok.rearrange("(s n p) d -> p s n d", s=2, p=128), s_ot, [first_sent, ofree[0], ofree[1]])
        s_out = P.sem("s_out")
        for n in range(4):
            t = P.stt(HT[:, n], OT[:, 0, n], GATES[:, 0, n:n + 1], HT[:, n], MUL, ADD, [t_o])
            t = P.stt(HT[:, n], OT[:, 1, n], GATES[:, 1, n:n + 1], HT[:, n], MUL, ADD, [t])
            P.dma(sp, out[128 * n:128 * n + 128, :], HT[:, n], s_out, [t], store=True)
        P.stores += [first_sent[0][0], first_sent[1][0]]
        P.run()



def packed(w, mt, order=None):
    k, n = w.shape
    a = w.reshape(k // 128, 128, n // 128, 128).transpose(2, 1, 0, 3)
    if order is not None:
        a = a[order]
    return np.ascontiguousarray(a.reshape(n // 128 // mt, mt, 128, k).transpose(0, 2, 1, 3).reshape(-1, 128, mt * k))


def packed_tok(w, cols):
    k, n = w.shape
    a = w.reshape(k // 128, 128, n // cols, cols).transpose(2, 1, 0, 3)
    return np.ascontiguousarray(a.reshape(n // cols, 128, k // 128 * cols))


def column(v):
    return np.ascontiguousarray(v.reshape(-1, 128).T)


def wide(w, n, at=0):
    out = np.zeros((w.shape[0], n), w.dtype)
    out[:, at:at + w.shape[1]] = w
    return out


def layout(i):
    g = {k: np.asarray(v) for k, v in i.items()}
    a = {}
    pc = param_columns()
    prm = np.zeros((128, pc["n"]), np.float32)

    def put(name, v, at=0):
        prm[:, pc[name] + at:pc[name] + at + v.shape[1]] = v

    for l in range(2):
        put("mixg", column(g["norm_mix_g"][l]), 8 * l)
        put("ffng", column(g["norm_ffn_g"][l]), 8 * l)
        for j in range(3):
            put("cw", column(g["ffn_conv_w"][l, j]), (3 * l + j) * 44)
        put("cb", column(g["ffn_conv_b"][l]), 44 * l)
    put("fing", column(g["norm_final_g"]))
    put("ln1", column(g["ln1_g_2"][0]))
    put("ln2", column(g["ln2_g_2"][0]))
    put("bu", column(g["sgu_b_in"][0, :D]))
    for j in range(6):
        put("mu", column(g["rwkv_mu"][0, j]), 8 * j)
    for name, key in (("w0", "rwkv_w0"), ("a0", "rwkv_a0"), ("kk", "rwkv_k_k"), ("ka", "rwkv_k_a"),
                      ("lnw", "rwkv_ln_w"), ("lnb", "rwkv_ln_b")):
        put(name, column(g[key][0]))
    put("rk", column(g["rwkv_r_k"][0].reshape(-1)))
    for j in range(5):
        put("dncw", column(g["dn_conv_w_2"][0, j]), 12 * j)
    put("qg", np.concatenate([g["attn_q_norm_g_2"][0]] * 2)[:, None])
    put("kg", np.concatenate([g["attn_k_norm_g_2"][0]] * 2)[:, None])
    put("aog", column(g["attn_out_norm_g_2"][0]))
    put("dng", g["dn_out_norm_g_2"][0][:, None])
    put("eps", np.full((128, 1), 1e-6))
    put("gneps", np.full((128, 1), 64e-5))
    put("one", np.ones((128, 1)))
    a["params"] = prm
    a["consts"] = constants()
    a["sel"] = ((np.arange(D) // 64)[None] == np.arange(16)[:, None]).astype(np.float32)
    a["x"] = np.ascontiguousarray(g["x"][0].T)
    w = g["sgu_w_in"][0]
    a["sgu_u"] = packed(w[:, :D], 2)
    a["sgu_v"] = packed_tok(w[:, D:], 256)
    a["sgu_o"] = packed(g["sgu_w_out"][0], 2)
    a["sgu_ws"] = np.ascontiguousarray(g["sgu_w_s"][0].transpose(2, 0, 1))
    a["sgu_rows"] = np.ascontiguousarray(np.broadcast_to(np.stack([g["sgu_b_in"][0, D:], g["sgu_g_v"][0]])[None], (128, 2, D)))
    a["sgu_bs"] = g["sgu_b_s"][0]
    pairs = [f + h * FT for f in range(FT) for h in range(2)]
    for l in range(2):
        a[f"up{l}"] = packed(g["ffn_w_up"][l], 2, pairs)
        d = packed(g["ffn_w_down"][l], 1)
        a[f"down{l}"] = np.ascontiguousarray(d.reshape(8, 128, 2, 1408).transpose(0, 2, 1, 3).reshape(16, 128, 1408))
    g1 = g["rwkv_g1"][0]
    a["lora1"] = np.concatenate([packed(x, 1) for x in (
        wide(g["rwkv_w1"][0], 128), wide(g["rwkv_a1"][0], 128, 64), g1[:, :128], wide(g1[:, 128:], 128))])
    lora2 = np.zeros((2, 128, 2048), np.float32)
    lora2[0, :64, :D] = g["rwkv_w2"][0]
    lora2[0, 64:, :D] = g["rwkv_a2"][0]
    lora2[1, :, :D] = g["rwkv_g2"][0][:128]
    lora2[1, :32, D:] = g["rwkv_g2"][0][128:]
    a["lora2"] = lora2
    a["rwkv_rkv"] = np.concatenate([packed(g[x][0], 2) for x in ("rwkv_w_r", "rwkv_w_k", "rwkv_w_v")])
    a["rwkv_o"] = packed(g["rwkv_w_o"][0], 2)
    w = g["w_in_2"][0]
    a["in2_qk"] = packed(w[:, :1024], 2)
    a["in2_v"] = packed_tok(w[:, 1024:1536], 256)
    a["in2_dn"] = packed(w[:, 1536:3584], 2)
    a["in2_ab"] = packed_tok(w[:, 3584:], 16)
    a["out2"] = packed(g["w_out_2"][0], 2)
    pad = np.zeros((8, 15, 160), np.float32)
    pad[:, :, 48:79] = g["attn_rpb_2"][0]
    a["rpb"] = np.stack([pad[:, :, 63 - c:127 - c] for c in range(64)])
    a["rows8"] = np.ascontiguousarray(np.broadcast_to(
        np.stack([g["dn_dt_bias_2"][0].reshape(8), g["dn_a_log_2"][0].reshape(8)])[None], (128, 2, 8)))
    a["colmask"] = column_mask()
    r = np.concatenate([g["router_group_w_2"][0], g["router_expert_w_2"][0]], 1)
    a["router_w"] = np.ascontiguousarray(r.reshape(8, 128, 72).transpose(1, 0, 2).reshape(128, 576))
    a["router_b"] = np.ascontiguousarray(np.broadcast_to(
        np.concatenate([g["router_group_b_2"][0], g["router_expert_b_2"][0]])[None], (128, 72)))
    for name in ("gate", "up", "down"):
        a[f"e_{name}"] = g[f"expert_w_{name}_2"][0]
    return a


def column_mask():
    q = np.arange(128)[:, None] % 64
    k = np.arange(64)[None, :]
    lo = np.clip(q - 8, 0, 48)
    return np.where((k >= lo) & (k < lo + 16), 0.0, -1e30).astype(np.float32)


def kernel(**inputs):
    import concourse.bacc as bacc
    from concourse.bass_utils import run_bass_kernel_spmd

    arrays = layout(inputs)
    nc = bacc.Bacc("TRN2", target_bir_lowering=False, num_devices=1)
    A = {k: nc.dram_tensor(k, list(v.shape), F32, kind="ExternalInput").ap() for k, v in arrays.items()}
    out = nc.dram_tensor("out", [S, D], F32, kind="ExternalOutput").ap()
    build(nc, A, out)
    r = run_bass_kernel_spmd(nc, [arrays], core_ids=[0])
    return r.results[0]["out"].reshape(1, S, D)
```

```python
from contextlib import ExitStack, contextmanager

import numpy as np

import concourse.bass as bass
from concourse import mybir

F32 = mybir.dt.float32
F32R = mybir.dt.float32r
I32 = mybir.dt.int32
ALU = mybir.AluOpType
ACT = mybir.ActivationFunctionType
AX = mybir.AxisListType
MUL, ADD, SUB, MAX, MIN = ALU.mult, ALU.add, ALU.subtract, ALU.max, ALU.min

S = 512
D = 1024
KT = 8
FF = 2816
FT = FF // 128
NOV = 16
NP = (64 + NOV) // 2
NOWHERE = 1 << 20


class Engine:

    def __init__(self, sem):
        self.sem, self.n, self.list, self.met, self.sent = sem, 0, [], {}, []

    def wait(self, *tokens):
        for t in tokens:
            if not t:
                continue
            if isinstance(t, list):
                self.wait(*t)
                continue
            sem, value = t
            if self.met.get(sem.num, 0) < value:
                self.met[sem.num] = value
                self.list.append(lambda e, s=sem, v=value: e.wait_ge(s, v))

    def put(self, f, w=(), inc=True):
        self.wait(*w)
        if not inc:
            self.list.append(f)
            return None
        self.n += 1
        self.list.append(lambda e, f=f: f(e).then_inc(self.sem, 1))
        return (self.sem, self.n)

    def now(self):
        return (self.sem, self.n) if self.n else None


class Banks:

    def __init__(self, ids, free):
        self.ids, self.free, self.i = ids, free, -1

    def take(self):
        self.i = (self.i + 1) % len(self.ids)
        b = self.ids[self.i]
        return b, None, self.free[b]


class Slots:

    def __init__(self, bufs):
        self.bufs, self.free, self.i = bufs, [[] for _ in bufs], -1

    def take(self):
        self.i = (self.i + 1) % len(self.bufs)
        return self.i, self.bufs[self.i], self.free[self.i]


PARAMS = {}


def param_columns():
    if PARAMS:
        return PARAMS
    at = 0
    for name, n in (("mixg", 16), ("ffng", 16), ("fing", 8), ("ln1", 8), ("ln2", 8), ("bu", 8),
                    ("mu", 48), ("w0", 8), ("a0", 8), ("kk", 8), ("ka", 8), ("rk", 8), ("lnw", 8), ("lnb", 8),
                    ("cw", 2 * 3 * 44), ("cb", 2 * 44), ("dncw", 5 * 12), ("qg", 1), ("kg", 1), ("aog", 4), ("dng", 1),
                    ("eps", 1), ("gneps", 1), ("zero", 1), ("one", 1)):
        PARAMS[name] = at
        at += n
    PARAMS["n"] = at
    return PARAMS


CONSTS = {}


def const_columns():
    if CONSTS:
        return CONSTS
    at = 0
    for name, n in (("ident", 128), ("ones", 128), ("blk", 128), ("i2", 64), ("up", 128), ("lo", 128), ("eye16", 256),
                    ("incu", 64), ("stru", 64), ("incl", 64), ("strl", 64), ("cumf", 128), ("cumb", 128),
                    ("half", 256), ("tri", 128), ("iota8", 8), ("iota64", 64), ("iota16", NOV), ("iota80", 2 * NP), ("pair", 8)):
        CONSTS[name] = at
        at += n
    CONSTS["n"] = at
    return CONSTS


def constants():
    c = const_columns()
    out = np.zeros((128, c["n"]), np.float32)

    def put(name, a):
        out[:, c[name]:c[name] + a.shape[1]] = a

    p = np.arange(128)[:, None]
    j = np.arange(64)[None, :]
    q = p % 64
    t = np.arange(128)[None, :]
    put("ident", np.eye(128))
    put("ones", np.ones((128, 128)))
    put("blk", (p // 64 == t // 64) * 1.0)
    put("i2", (q == j) * 1.0)
    for l in range(2):
        b = 32 << l
        same = (q // b == j // b)
        up = same & (q % b < b // 2) & (j % b >= b // 2)
        lo = same & (q % b >= b // 2) & (j % b < b // 2)
        out[:, c["up"] + 64 * l:c["up"] + 64 * l + 64] = up
        out[:, c["lo"] + 64 * l:c["lo"] + 64 * l + 64] = lo
    put("eye16", np.repeat(np.eye(16).reshape(1, 256), 128, 0))
    put("incu", (q <= j) * 1.0)
    put("stru", (q < j) * 1.0)
    put("incl", (q >= j) * 1.0)
    put("strl", (q > j) * 1.0)
    put("cumf", ((p // 64 == t // 64) & (p <= t)) * 1.0)
    put("cumb", ((p // 64 == t // 64) & (p >= t)) * 1.0)
    put("half", np.concatenate([np.repeat(p < 64, 128, 1), np.repeat(p >= 64, 128, 1)], 1) * 1.0)
    put("tri", (p < t) * 1.0)
    put("iota8", np.repeat(np.arange(8)[None], 128, 0))
    put("iota64", np.repeat(np.arange(64)[None], 128, 0))
    put("iota16", np.repeat(np.arange(NOV)[None], 128, 0))
    put("iota80", np.repeat(np.arange(2 * NP)[None], 128, 0))
    put("pair", p + 1 + np.array([[512 * s + 128 * n for s in range(2) for n in range(4)]]))
    return out


class Program:
    def __init__(self, nc, ctx, A):
        self.nc, self.ctx, self.A = nc, ctx, A
        self.nsem = 0
        self.pe, self.dve, self.act, self.pool, self.sp = (Engine(self.sem(x)) for x in ("s_pe", "s_dve", "s_act", "s_pool", "s_sp"))
        self.counts = {}
        self.stores = []
        self.ps = ctx.enter_context(nc.psum_tensor("ps", [128, 8, 512], F32))
        self.at = 16512 - 16512 % 32 + 32
        self.end = 229344

    def sem(self, name):
        return self.ctx.enter_context(self.nc.semaphore(name))

    def place(self, name, shape, dt, offset):
        n = 4
        for x in shape[1:]:
            n *= x
        n += -n % 32
        assert offset + n <= self.end, (name, offset, n)
        return self.nc.alloc_sbuf_tensor_at(name, shape, dt, offset=offset), offset + n

    def keep(self, name, shape, dt=F32):
        t, self.at = self.place(name, shape, dt, self.at)
        return t

    def dma(self, eng, out, in_, sem, w=(), store=False):
        eng.wait(*w)
        t = self.counted_up(eng, sem)
        eng.list.append(lambda e: e.dma_start(out, in_(e) if callable(in_) else in_).then_inc(sem, 16))
        if store:
            self.stores.append(t)
        return t

    def counted_up(self, eng, sem, within=False):
        self.counts[sem.num] = self.counts.get(sem.num, 0) + 16
        if not within:
            eng.sent.append(sem)
        return (sem, self.counts[sem.num])

    def counted(self, at, most, w):
        regs = {}
        for x in (self.pe, self.dve, self.act, self.pool, self.sp):
            x.wait(*w)
            x.list.append(lambda e, x=x: regs.update({x: e.value_load(at, min_val=0, max_val=most)}))
        return regs

    @contextmanager
    def when(self, regs, n):
        engines = (self.pe, self.dve, self.act, self.pool, self.sp)
        before = [(x, x.list, x.n, dict(x.met), len(x.sent)) for x in engines]
        now = [x.now() for x in engines[:4]]
        counts = dict(self.counts)
        for x in engines:
            x.list = []
        yield
        for x, outer, first, met, sent in before:
            inner, x.list, x.met = x.list, outer, met
            owed = [(x.sem, x.n - first)] if x.n > first else []
            for sem in {s.num: s for s in x.sent[sent:]}.values():
                owed.append((sem, 16 * sum(s.num == sem.num for s in x.sent[sent:])))

            quiet = [(s, first if s is x.sem else counts.get(s.num, 0)) for s, _ in owed] + (now if len(x.sent) > sent else [])

            def both(e, x=x, inner=inner, owed=owed, quiet=quiet):
                with e.If(regs[x] > n):
                    for f in inner:
                        f(e)
                with e.Else():
                    for sem, value in quiet:
                        e.wait_ge(sem, value)
                    for sem, value in owed:
                        e.sem_inc(sem, value)

            x.list.append(both)

    def mm(self, out, l, r, start, stop, w=(), inc=False, skip=False):
        return self.pe.put(lambda e: e.matmul(out, l, r, start=start, stop=stop, skip_group_check=skip), w, inc)

    def tr(self, out, in_, ident, w=(), inc=False):
        return self.pe.put(lambda e: e.transpose(out, in_, ident), w, inc)

    def a(self, out, in_, func, w=(), bias=0.0, scale=1.0, accum=None):
        if accum is not None:
            return self.act.put(lambda e: e.activation(out, in_, func, bias=bias, scale=scale, accum_out=accum), w)
        return self.act.put(lambda e: e.activation(out, in_, func, bias=bias, scale=scale), w)

    def tt(self, eng, out, in0, in1, op, w=()):
        return eng.put(lambda e: e.tensor_tensor(out, in0, in1, op), w)

    def ts(self, eng, out, in0, s1, s2, op0, op1=None, w=()):
        if op1 is None:
            return eng.put(lambda e: e.tensor_scalar(out, in0, s1, None, op0), w)
        return eng.put(lambda e: e.tensor_scalar(out, in0, s1, s2, op0, op1), w)

    def stt(self, out, in0, s, in1, op0, op1, w=()):
        return self.dve.put(lambda e: e.scalar_tensor_tensor(out, in0, s, in1, op0, op1), w)

    def cp(self, eng, out, in_, w=()):
        return eng.put(lambda e: e.tensor_copy(out, in_), w)

    def red(self, out, in_, op, w=(), axis=AX.X):
        return self.dve.put(lambda e: e.tensor_reduce(out, in_, axis, op), w)

    def recip(self, out, in_, w=()):
        return self.dve.put(lambda e: e.reciprocal(out, in_), w)

    def rsqrt(self, out, in_, w=(), bias=0.0, scale=1.0):
        t = self.a(out, in_, ACT.Ln, w, bias=bias, scale=scale)
        return t, self.a(out, out, ACT.Exp, [t], scale=-0.5)

    def rsqrts(self, todo, bias=0.0, scale=1.0):
        first = [self.a(out, in_, ACT.Ln, w, bias=bias, scale=scale) for out, in_, w in todo]
        return first, [self.a(out, out, ACT.Exp, [t], scale=-0.5) for (out, _, _), t in zip(todo, first)]

    def memset(self, eng, out, v, w=()):
        return eng.put(lambda e: e.memset(out, v), w)

    def barrier(self):
        now = [x.now() for x in (self.pe, self.dve, self.act, self.pool)]
        for x in (self.pe, self.dve, self.act, self.pool, self.sp):
            x.wait(*now)

    def run(self):
        block = self.ctx.enter_context(self.nc.Block())

        @block.tensor
        def _(e):
            for f in self.pe.list:
                f(e)

        @block.vector
        def _(e):
            for f in self.dve.list:
                f(e)

        @block.scalar
        def _(e):
            for f in self.act.list:
                f(e)

        @block.gpsimd
        def _(e):
            for f in self.pool.list:
                f(e)

        @block.sync
        def _(e):
            for f in self.sp.list:
                f(e)
            last = {}
            for sem, v in self.stores:
                last[sem.num] = (sem, max(v, last.get(sem.num, (sem, 0))[1]))
            for sem, v in last.values():
                e.wait_ge(sem, v)


class Stream:

    def __init__(self, P, name, raws, highs, lows, items, ahead=1, share=None):
        self.P, self.items, self.ahead, self.share = P, items, ahead, share
        self.raws, self.highs, self.lows = raws, highs, lows
        self.rfree = [[] for _ in raws]
        self.sfree = [[] for _ in highs]
        self.sems = [P.sem(f"{name}{i}") for i in range(len(raws))]
        self.loaded, self.cut, self.i, self.ns = {}, {}, 0, 0
        self.nl = 0

    def load(self, upto):
        while self.nl < min(upto, len(self.items)):
            i = self.nl
            r = i % len(self.raws)
            src, n = self.items[i][:2]
            self.loaded[i] = self.P.dma(self.P.sp, self.raws[r][:, 0:n], src, self.sems[r], self.rfree[r])
            self.nl += 1

    def split(self, i):
        if i in self.cut or i >= len(self.items):
            return
        P = self.P
        n = self.items[i][1]
        r = i % len(self.raws)
        if self.items[i][2] == "raw":
            self.cut[i] = (self.raws[r], None, [self.loaded[i]], r)
            return
        s = self.ns % len(self.highs)
        self.ns += 1
        h, l, raw = self.highs[s], self.lows[s], self.raws[r]
        t1 = P.a(h[:, 0:n], raw[:, 0:n], ACT.Copy, [self.loaded[i], self.sfree[s]])
        m = self.share or n
        w = [self.loaded[i], t1, self.sfree[s]]
        t2 = [P.tt(P.dve, l[:, 0:m], raw[:, 0:m], h[:, 0:m].bitcast(F32), SUB, w)]
        if m < n:
            t2.append(P.tt(P.pool, l[:, m:n], raw[:, m:n], h[:, m:n].bitcast(F32), SUB, w))
        self.rfree[r] = [t1, t2]
        self.cut[i] = (h, l, [t1, t2], s)

    def next(self):
        i = self.i
        self.i += 1
        upto = i + 1
        while upto < min(i + len(self.raws), len(self.items)) and self.items[upto][2] != "late":
            upto += 1
        self.load(upto)
        self.split(i)
        for q in range(i + 1, min(i + 1 + self.ahead, len(self.items))):
            if self.items[q][2] != "split":
                break
            self.split(q)
        h, l, t, s = self.cut[i]

        def done(token):
            if self.items[i][2] == "raw":
                self.rfree[s] = [token]
            else:
                self.sfree[s] = [token]

        return h, l, t, done


def weaving(steps, width):
    steps, now = list(steps), []
    while steps or now:
        while steps and len(now) < width:
            now.append(steps.pop(0))
        for g in list(now):
            try:
                next(g)
            except StopIteration:
                now.remove(g)
        yield


def weave(steps, width):
    for _ in weaving(steps, width):
        pass


class Ring:

    def __init__(self, P, name, slots, items, free, alone):
        self.P, self.slots, self.items, self.alone = P, slots, items, alone
        self.free = [free for _ in slots]
        self.sems = [P.sem(f"{name}{i}") for i in range(len(slots))]
        self.loaded, self.i, self.nl = {}, 0, 0

    def load(self, upto):
        while self.nl < min(upto, len(self.items)):
            i, r = self.nl, self.nl % len(self.slots)
            src, k = self.items[i]
            self.loaded[i] = self.P.dma(self.P.sp, self.slots[r][:, :].rearrange("p (k n) -> p k n", k=k), src,
                                        self.sems[r], self.free[r])
            self.nl += 1

    def next(self):
        i = self.i
        self.i += 1
        assert i < self.nl

        def done(token):
            self.free[i % len(self.slots)] = [token]
            self.load(min(i + 1 + len(self.slots), self.alone))

        return self.slots[i % len(self.slots)], self.loaded[i], done


def build(nc, A, out):
    with ExitStack() as ctx:
        P = Program(nc, ctx, A)
        c, pc = const_columns(), param_columns()
        pe, dve, act, pool, sp = P.pe, P.dve, P.act, P.pool, P.sp
        ps = P.ps
        CST = P.keep("cst", [128, c["n"]])
        PRM = P.keep("prm", [128, pc["n"]])
        PRM_END = P.at
        H = P.keep("H", [128, KT, S])
        TMPS = [P.keep(f"tmp{i}", [128, S]) for i in range(6)]
        ring0 = P.at
        RAW = [P.keep(f"raw{i}", [128, 2048]) for i in range(2)]
        WH = [P.keep(f"wh{i}", [128, 2048], F32R) for i in range(2)]
        WL = [P.keep(f"wl{i}", [128, 2048], F32R) for i in range(2)]
        cut0 = P.at - 32768
        xs0 = P.at
        XH = P.keep("xh", [128, KT, S], F32R)
        XL = P.keep("xl", [128, KT, S], F32R)
        base = P.at

        def cst(name, n, k=0):
            return CST[:, c[name] + k:c[name] + k + n]

        def prm(name, k=0):
            return PRM[:, pc[name] + k:pc[name] + k + 1]

        ident, ones, blk = cst("ident", 128), cst("ones", 128), cst("blk", 128)
        tmp = Slots([t[:, :] for t in TMPS])
        bfree = {b: [] for b in range(8)}
        bank = Banks(list(range(8)), bfree)

        items = []

        def feed(name, n, kind="split"):
            for i in range(A[name].shape[0]):
                items.append((A[name][i], n, kind))

        feed("sgu_u", 2048)
        feed("sgu_v", 2048)
        feed("sgu_o", 2048)
        for l in range(2):
            feed(f"up{l}", 2048)
            feed(f"down{l}", 1408)
            if l == 0:
                feed("lora1", 1024)
                feed("rwkv_rkv", 2048)
                feed("lora2", 2048, "raw")
                items.append((A["rwkv_o"][0], 2048, "late"))
                for i in range(1, 4):
                    items.append((A["rwkv_o"][i], 2048, "split"))
        feed("in2_qk", 2048)
        feed("in2_v", 2048)
        feed("in2_dn", 2048)
        feed("in2_ab", 1024)
        items.append((A["out2"][0], 2048, "late"))
        for i in range(1, 4):
            items.append((A["out2"][i], 2048, "split"))
        W = Stream(P, "s_w", RAW, WH, WL, items)

        s_c = P.sem("s_c")
        t_x = []
        for i in range(4):
            t_x += [P.dma(sp, H[:, 2 * i:2 * i + 2], A["x"][256 * i:256 * i + 256].rearrange("(k p) t -> p k t", p=128),
                          P.sem(f"s_x{i}"))] * 2
        P.dma(sp, PRM[:, :], A["params"], s_c)
        t_c = P.dma(sp, CST[:, :], A["consts"], s_c)
        W.load(2)

        def split(src, k, t, XH=XH, XL=XL, w=()):
            th = P.a(XH[:, k], src, ACT.Copy, [t, w])
            tl = P.tt(dve, XL[:, k], src, XH[:, k].bitcast(F32), SUB, [t, th, w])
            return [th, tl]

        def rstd_of(total, n, eps, w):
            b, _, free = bank.take()
            t = P.mm(ps[:, b], ones, total, True, True, [w, free], True)
            i, r, free = tmp.take()
            t1, t = P.rsqrt(r, ps[:, b], [t, free], prm(eps), 1.0 / n)
            bank.free[b] = [t1]
            return i, r, t

        sums = {}

        def add_square(x, t):
            if not sums:
                i, acc, free = tmp.take()
                sums.update(i=i, acc=acc, t=P.a(acc, x, ACT.Square, [t, free]))
                return
            i, q, free = tmp.take()
            if i == sums["i"]:
                i, q, free = tmp.take()
            t = P.a(q, x, ACT.Square, [t, free])
            sums["t"] = P.tt(dve, sums["acc"], sums["acc"], q, ADD, [t, sums["t"]])
            tmp.free[i] = [sums["t"]]

        def square_sum(tiles, toks):
            if not sums:
                for x, t in zip(tiles, toks):
                    add_square(x, t)
            got = sums["i"], sums["acc"], sums["t"]
            sums.clear()
            return got

        def norm(gain, gk, toks, inplace=False, w=()):
            ia, acc, ta = square_sum([H[:, k] for k in range(KT)], toks)
            ir, r, tr = rstd_of(acc, D, "eps", ta)
            tmp.free[ia] = [pe.now()]
            got = [None] * KT
            last = []

            def one(k):
                if inplace:
                    got[k] = P.stt(H[:, k], H[:, k], prm(gain, gk + k), r, MUL, MUL, [tr, toks[k]])
                    last[:] = [got[k]]
                    return
                i, x, free = tmp.take()
                if i == ir:
                    i, x, free = tmp.take()
                t = P.stt(x, H[:, k], prm(gain, gk + k), r, MUL, MUL, [tr, toks[k], free])
                last[:] = [t]
                yield
                got[k] = split(x, k, t, w=w)
                tmp.free[i] = got[k]

            weave([one(k) for k in range(KT)], 2)
            tmp.free[ir] = last
            return got

        def products(o, h, l, X, XLo, xt, first, last, inc, w):
            P.mm(o, h, X, first, False, [w, xt])
            P.mm(o, h, XLo, False, False)
            return P.mm(o, l, X, False, last, inc=inc)

        def gemm(nm, evac, xt, mt=2, XH=XH, XL=XL):
            m = 0
            for _ in range(nm // mt):
                h, l, tw, done = W.next()
                hv = h[:, 0:mt * 1024].rearrange("p (m k j) -> p m k j", m=mt, j=128)
                lv = l[:, 0:mt * 1024].rearrange("p (m k j) -> p m k j", m=mt, j=128)
                got = [bank.take() for _ in range(mt)]
                ts = [None] * mt
                for k in range(KT):
                    for q, (b, _, free) in enumerate(got):
                        ts[q] = products(ps[:, b], hv[:, q, k], lv[:, q, k], XH[:, k], XL[:, k], xt[k],
                                         k == 0, k == KT - 1, k == KT - 1, [tw, free])
                for (b, _, _), t in zip(got, ts):
                    bank.free[b] = evac(m, ps[:, b], t)
                    m += 1
                done(t)

        def gemm_tok(chunks, cols, evac, xt):
            for ch in range(chunks):
                h, l, tw, done = W.next()
                hv = h[:, 0:KT * cols].rearrange("p (k j) -> p k j", k=KT)
                lv = l[:, 0:KT * cols].rearrange("p (k j) -> p k j", k=KT)
                for n in range(4):
                    b, _, free = bank.take()
                    o = ps[:, b, 0:cols]
                    for k in range(KT):
                        xh, xl = XH[:, k, 128 * n:128 * n + 128], XL[:, k, 128 * n:128 * n + 128]
                        P.mm(o, xh, hv[:, k], k == 0, False, [tw, free, xt[k]])
                        P.mm(o, xl, hv[:, k], False, False)
                        t = P.mm(o, xh, lv[:, k], False, k == KT - 1, inc=k == KT - 1)
                    bank.free[b] = evac(ch, n, o, t)
                done(t)

        def residual(toks):
            def evac(m, o, t):
                toks[m] = P.tt(dve, H[:, m], o, H[:, m], ADD, [t, toks[m]])
                add_square(H[:, m], toks[m])
                return [toks[m]]
            return evac

        for k in range(KT):
            add_square(H[:, k], t_x[k])
        for e in (pe, dve, act, pool):
            e.wait(t_c)
        W.split(0)
        at = base
        U, at = P.place("U", [128, KT, S], F32, at)
        V, at = P.place("V", [128, 4, D], F32, at)
        WS, at = P.place("WS", [128, 16, 128], F32, at)
        ROWB, at = P.place("ROWB", [128, 2, D], F32, at)
        BS, at = P.place("BS", [16, 128], F32, at)
        SEL, at = P.place("SEL", [16, D], F32, at)
        SS, at = P.place("SS", [128, 4, 4], F32, at)
        RS, at = P.place("RS", [128, 4], F32, at)
        s_g = P.sem("s_g")
        P.dma(sp, SEL[:, :], A["sel"], s_g)
        P.dma(sp, WS[:, :, :], A["sgu_ws"], s_g)
        P.dma(sp, ROWB[:, :, :], A["sgu_rows"], s_g)
        t_g = P.dma(sp, BS[:, :], A["sgu_bs"], s_g)
        t_ws = pool.put(lambda e: e.affine_select(out=WS[:, :, :], in_=WS[:, :, :], compare_op=ALU.is_ge, fill=0.0, base=0,
                                                  pattern=[[0, 16], [1, 128]], channel_multiplier=-1), [t_g])
        xt = norm("mixg", 0, t_x)
        ut = [None] * KT

        def evac_u(m, o, t):
            ut[m] = P.a(U[:, m], o, ACT.Gelu, [t], bias=prm("bu", m))
            return [ut[m]]

        gemm(KT, evac_u, xt)
        vt = [[None] * 4 for _ in range(4)]

        def evac_v(ch, n, o, t):
            v = V[:, n, 256 * ch:256 * ch + 256]
            t1 = P.tt(dve, v, o, ROWB[:, 0, 256 * ch:256 * ch + 256], ADD, [t, t_g])
            vt[n][ch] = P.a(v, v, ACT.Gelu, [t1])
            return [t1]

        gemm_tok(4, 256, evac_v, xt)
        st = []
        for n in range(4):
            for ch in range(4):
                i, q, free = tmp.take()
                t = P.a(q[:, 0:256], V[:, n, 256 * ch:256 * ch + 256], ACT.Square, [vt[n][ch], free], accum=SS[:, n, ch:ch + 1])
                tmp.free[i] = [t]
                st.append(t)
        t = P.red(RS[:, :], SS[:, :, :], ADD, st)
        t = P.a(RS[:, :], RS[:, :], ACT.Sqrt, [t], bias=prm("eps"), scale=1.0 / D)
        t = P.recip(RS[:, :], RS[:, :], [t])
        vn = [P.stt(V[:, n], V[:, n], RS[:, n:n + 1], ROWB[:, 1], MUL, MUL, [t, vt[n]]) for n in range(4)]
        xt2 = []
        for m in range(KT):
            b, _, free = bank.take()
            P.mm(ps[:, b].rearrange("p (n t) -> p n t", n=4), SEL[:, 128 * m:128 * m + 128],
                 BS[:, :].rearrange("p (a t) -> p a t", a=1).to_broadcast([16, 4, 128]), True, False, [free, t_g], skip=True)
            for n in range(4):
                for g in range(2):
                    f = 128 * m + 64 * g
                    t = P.mm(ps[64 * g:64 * g + 64, b, 128 * n:128 * n + 128], V[:, n, f:f + 64], WS[:, 2 * m + g, :],
                             False, n == 3, [vn[n], t_ws], inc=(n == 3 and g == 1), skip=True)
            i, y, free = tmp.take()
            t = P.tt(dve, y, ps[:, b], U[:, m], MUL, [t, ut[m], free])
            bank.free[b] = [t]
            xt2.append(split(y, m, t, w=[pe.now()]))
            tmp.free[i] = xt2[-1]
        ht = list(t_x)
        gemm(KT, residual(ht), xt2)

        def ffn(l, ht):
            xt = norm("ffng", 8 * l, ht, w=[pe.now()])
            HH, at = P.place(f"HH{l}", [128, FT, S], F32R, base)
            HL, at = P.place(f"HL{l}", [128, FT, S], F32R, at)
            hid = []
            half = {}

            def evac(m, o, t):
                f = m // 2 + (m % 2) * FT
                w = [prm("cw", (3 * l + j) * 44 + f) for j in range(3)]
                i, z, free = tmp.take()
                t1 = P.a(z, o, ACT.Identity, [t, free], bias=prm("cb", 44 * l + f), scale=w[2])
                t2 = P.stt(z[:, 1:S], o[:, 0:S - 1], w[1], z[:, 1:S], MUL, ADD, [t1])
                t3 = P.stt(z[:, 2:S], o[:, 0:S - 2], w[0], z[:, 2:S], MUL, ADD, [t2])
                if m % 2 == 0:
                    half[0] = (i, z, P.a(z, z, ACT.Silu, [t3]))
                    return [t3]
                ig, g, tg = half[0]
                t4 = P.tt(dve, z, z, g, MUL, [t3, tg])
                tmp.free[ig] = [t4]
                hid.append(split(z, m // 2, t4, HH, HL))
                tmp.free[i] = hid[-1]
                return [t3]

            gemm(2 * FT, evac, xt)
            for m in range(KT):
                b, _, free = bank.take()
                for part in range(2):
                    h, lo, tw, done = W.next()
                    for j in range(11):
                        k = 11 * part + j
                        t = products(ps[:, b], h[:, 128 * j:128 * j + 128], lo[:, 128 * j:128 * j + 128],
                                     HH[:, k], HL[:, k], hid[k], k == 0, k == FT - 1, j == 10, [tw, free])
                    done(t)
                ht[m] = P.tt(dve, H[:, m], ps[:, b], H[:, m], ADD, [t, ht[m]])
                bank.free[b] = [ht[m]]
                add_square(H[:, m], ht[m])
            return ht

        P.barrier()
        ht = ffn(0, ht)

        s_bl = [P.sem(f"s_bl{i}") for i in range(4)]

        def blocks(MT, T, TT, n0, name, lower, ready, free, place, got):
            FB, y = P.place(f"{name}FB", [128, 16, 16], F32, place)
            X, y = P.place(f"{name}X", [128, 2, 16, 16], F32, y)
            PR, y = P.place(f"{name}PR", [128, 256], F32, y)
            md = nc.dram_tensor(f"{name}md", [128, 256], F32, kind="Internal").ap()
            xd = nc.dram_tensor(f"{name}xd", [128, 512], F32, kind="Internal").ap()
            spots = [(r, slice(64 * (r // 4) + 16 * (r % 4), 64 * (r // 4) + 16 * (r % 4) + 16), slice(16 * (r % 4), 16 * (r % 4) + 16))
                     for r in range(8)]
            for r, p, c_ in spots:
                t = P.dma(sp, md[16 * r:16 * r + 16].rearrange("a (i j) -> i a j", i=16), MT[p, n0:n0 + 16, c_], s_bl[0],
                          [ready], store=True)
            tf = P.dma(sp, FB[:, :, :].rearrange("p i j -> p (i j)"), md, s_bl[1], [t, free])
            tz = [P.memset(pool, T[:, n0:n0 + 16], 0.0, [free]), P.memset(pool, TT[:, n0:n0 + 16], 0.0, [free])]
            t = P.cp(pool, X[:, 0].rearrange("p i j -> p (i j)"), cst("eye16", 256), [free])
            yield
            for i in range(1, 16) if lower else range(14, -1, -1):
                js = slice(0, i) if lower else slice(i + 1, 16)
                n = i if lower else 15 - i
                pr = PR[:, 0:n * n].rearrange("p (c j) -> p c j", j=n)
                t1 = P.tt(dve, pr, FB[:, i:i + 1, js].to_broadcast([128, n, n]), X[:, 0, js, js].rearrange("p j c -> p c j"), MUL,
                          [tf, t, free])
                t = P.red(X[:, 0, i, js], pr, ADD, [t1])
                if n % 3 == 0:
                    yield
            t = P.cp(dve, X[:, 1], X[:, 0].rearrange("p i j -> p j i"), [t])
            t = P.dma(sp, xd, X[:, :, :, :].rearrange("p z i j -> p (z i j)"), s_bl[2], [t], store=True)
            for r, p, c_ in spots:
                for z, dst in enumerate((TT, T)):
                    src = xd[16 * r:16 * r + 16, 256 * z:256 * z + 256].rearrange("a (i j) -> i a j", i=16)
                    t1 = P.dma(sp, dst[p, n0:n0 + 16, c_], src, s_bl[3], [t, tz])
            got.append(t1)
            for _ in range(2):
                yield

        def inverse(MT, T, TT, Z, n0, nb, masks, ready, banks, want, mbs, tri, by):
            sl = slice(n0, n0 + nb)
            w = nb * 64

            def level(l):
                return cst(masks, 64, 64 * (l - 4)).rearrange("p (a j) -> p a j", a=1).to_broadcast([128, nb, 64])

            def masked(l):
                im, mb, free = mbs.take()
                M = mb[:, 0:w].rearrange("p (a j) -> p a j", j=64)
                return im, M, P.tt(by, M, MT[:, sl], level(l), MUL, [ready, free])

            tT = tTT = list(tri)
            following = [masked(4), masked(5)]
            for l in (4, 5):
                im, M, tm = following[l - 4]
                b, _, free = banks.take()
                o = ps[:, b, 0:w].rearrange("p (a j) -> p a j", j=64)
                for a in range(nb):
                    for h in (0, 64):
                        t = P.mm(o[h:h + 64, a], M[h:h + 64, a], T[h:h + 64, n0 + a], True, True, [tm, tT, free],
                                 a == nb - 1 and h > 0)
                mbs.free[im] = [t]
                tz = P.a(Z[:, sl], o, ACT.Copy, [t, tri])
                banks.free[b] = [tz]
                yield
                last = l == 5
                got = {}
                for name, left, right in (("T", TT, Z), ("TT", Z, TT)):
                    if last and name != want:
                        continue
                    b, _, free = banks.take()
                    o = ps[:, b, 0:w].rearrange("p (a j) -> p a j", j=64)
                    for a in range(nb):
                        for h in (0, 64):
                            t = P.mm(o[h:h + 64, a], left[h:h + 64, n0 + a], right[h:h + 64, n0 + a], True, True,
                                     [tz, tTT, free], a == nb - 1 and h > 0)
                    got[name] = (b, o, t)
                both = [x[2] for x in got.values()]
                for name, (b, o, t) in got.items():
                    X = T if name == "T" else TT
                    t = P.tt(dve, X[:, sl], o, X[:, sl], ADD, [both, tT, tTT])
                    banks.free[b] = [t]
                    if name == "T":
                        tT = t
                    else:
                        tTT = t
                yield
            tri[:] = [tT if want == "T" else tTT]

        P.barrier()
        s_h = P.sem("s_h")
        hs = nc.dram_tensor("hs", [128, KT, S], F32, kind="Internal").ap()
        t_sp = P.dma(sp, hs, H[:, :, :], s_h, [ht], store=True)
        AR, at = P.place("AR", [128, 2, KT, S], F32, base)
        KB, at = P.place("KB", [128, KT, S], F32, at)
        LW, at = P.place("LW", [128, KT, S], F32, at)
        OMM, at = P.place("OMM", [128, 48], F32, at)
        PC, at = P.place("PC", [128, KT, 8], F32, at)
        q0 = at
        VF, at = P.place("VF", [128, KT, S], F32, at)
        HID, at = P.place("HID", [128, 4, S], F32, at)
        SM, _ = P.place("SM", [128, S], F32, ring0 + 12288)
        MORE, _ = P.place("MORE", [128, S], F32, ring0 + 14336)
        G, _ = P.place("G", [128, KT, S], F32, xs0)
        VT, _ = P.place("VT", [128, 4, D], F32, xs0 + 16384)
        B = H
        t_om = P.ts(dve, OMM[:, :], PRM[:, pc["mu"]:pc["mu"] + 48], -1.0, 1.0, MUL, ADD)
        xn = norm("mixg", 8, [[x, t_sp] for x in ht], inplace=True)

        XH2, _ = P.place("xh2", [128, KT, S], F32R, base)
        XL2, _ = P.place("xl2", [128, KT, S], F32R, base + 49152)
        pairs = [(XH, XL, [[]]), (XH2, XL2, [[]])]

        def mix(i, z):
            xh, xl, (w,) = pairs[z]
            got = [None] * KT

            def one(k):
                q, x, free = tmp.take()
                t = P.a(x, H[:, k], ACT.Copy, [xn[k], t_om, free], scale=OMM[:, 8 * i + k:8 * i + k + 1])
                t = P.stt(x[:, 1:S], H[:, k, 0:S - 1], prm("mu", 8 * i + k), x[:, 1:S], MUL, ADD, [t])
                yield
                got[k] = split(x, k, t, xh, xl, w=w)
                tmp.free[q] = got[k]

            weave([one(k) for k in range(KT)], 3)
            return got

        hid = [None] * 4

        def into(dst, toks, at=0, func=ACT.Copy):
            def evac(m, o, t):
                toks[at + m] = P.a(dst[:, at + m], o, func, [t])
                return [toks[at + m]]
            return evac

        rt, kt, vt = [None] * 8, [None] * 8, [None] * 8
        turns = [(1, 1, into(HID, hid, 0, ACT.Tanh), 1), (4, 1, into(HID, hid, 1), 1), (5, 2, into(HID, hid, 2, ACT.Sigmoid), 1),
                 (0, KT, into(AR[:, 1], rt), 2), (2, KT, into(KB, kt), 2), (3, KT, into(VF, vt), 2)]
        following = mix(turns[0][0], 0)
        for n, (_, nm, evac, mt) in enumerate(turns):
            xt = following
            if n + 1 < len(turns):
                following = mix(turns[n + 1][0], (n + 1) % 2)
            xh, xl, w = pairs[n % 2]
            gemm(nm, evac, xt, mt, xh, xl)
            w[0] = [pe.now()]
        mixed = [pe.now(), act.now(), dve.now()]
        raw0, _, t0, done0 = W.next()
        lt, at_, gt = [None] * 8, [None] * 8, [None] * 8
        for m in range(KT):
            b1, _, free = bank.take()
            P.mm(ps[:, b1], raw0[0:64, 128 * m:128 * m + 128], HID[0:64, 0], True, True, [t0, hid[0], free])
            b2, _, free = bank.take()
            t = P.mm(ps[:, b2], raw0[64:128, 128 * m:128 * m + 128], HID[64:128, 1], True, True, [hid[1], free], True)
            x = P.a(LW[:, m], ps[:, b1], ACT.Sigmoid, [t], bias=prm("w0", m))
            bank.free[b1] = [x]
            lt[m] = P.ts(dve, LW[:, m], LW[:, m], -float(np.exp(np.float64(-0.5))), None, MUL, w=[x])
            at_[m] = P.a(B[:, m], ps[:, b2], ACT.Sigmoid, [t, mixed], bias=prm("a0", m))
            bank.free[b2] = [at_[m]]
        done0(t)
        raw1, _, t1, done1 = W.next()
        for m in range(KT):
            b, _, free = bank.take()
            P.mm(ps[:, b], raw1[:, 128 * m:128 * m + 128], HID[:, 2], True, False, [t1, hid, free])
            t = P.mm(ps[:, b], raw1[0:32, D + 128 * m:D + 128 * m + 128], HID[0:32, 3], False, True, inc=True)
            gt[m] = P.cp(dve, G[:, m], ps[:, b], [t, mixed])
            bank.free[b] = [gt[m]]
        done1(t)
        vn = []
        for n in range(4):
            for half in range(2):
                b, _, free = bank.take()
                for q in range(4):
                    t = P.tr(ps[:, b, 128 * q:128 * q + 128], VF[:, 4 * half + q, 128 * n:128 * n + 128], ident,
                             [vt, free], q == 3)
                bank.free[b] = [P.cp(dve, VT[:, n, 512 * half:512 * half + 512], ps[:, b], [t, mixed])]
                vn += bank.free[b]
        t_sm = P.memset(pool, SM[:, :], 1.0, [t])
        t_sm = P.memset(pool, SM[:, :].rearrange("p (c t) -> p c t", t=64)[:, :, 0:1], 0.0, [t_sm])
        kk = [None] * 8
        for j0 in range(0, KT, 4):
            todo, xs = [], []

            def length(j):
                x = AR[:, 0, j]
                tx = P.ts(dve, x, KB[:, j], prm("kk", j), None, MUL, w=[kt[j], mixed])
                i, y, free = tmp.take()
                t = P.a(y, x, ACT.Square, [tx, free])
                yield
                b, _, free = bank.take()
                t = P.mm(ps[:, b], blk, y, True, True, [t, free], True)
                t = P.ts(dve, y, ps[:, b], 1e-24, None, MAX, w=[t])
                bank.free[b] = [t]
                todo.append((y, y, [t]))
                xs.append((j, i, x, y, tx))

            weave([length(j) for j in range(j0, j0 + 4)], 4)
            for (j, i, x, y, tx), t in zip(xs, P.rsqrts(todo, scale=float(2 ** 20))[1]):
                kk[j] = P.stt(x, x, 1024.0, y, MUL, MUL, [tx, t])
                tmp.free[i] = [kk[j]]
        ready = []
        bv = []
        few = Banks([0, 1, 2, 3], bfree)
        wide = Slots(tmp.bufs + [HID[:, 0], HID[:, 1]])
        wide.free[:] = tmp.free + [[pe.now()]] * 2

        def scaled(j, wide):
            r, k, a, lw = AR[:, 1, j], KB[:, j], B[:, j], LW[:, j]
            ic, cum, free = wide.take()
            t_cum = dve.put(lambda e, cum=cum, lw=lw: e.tensor_tensor_scan(cum, SM[:, :], lw, 0.0, MUL, ADD), [lt[j], t_sm, free])
            i1, x, free = wide.take()
            t = P.tt(dve, x, cum, lw, SUB, [t_cum, free])
            t_lw = t
            t_e1 = P.a(x, x, ACT.Exp, [t])
            i2, e2, free = wide.take()
            t_e2 = P.a(e2, cum, ACT.Exp, [t_cum, free])
            t_e3 = P.a(cum, cum, ACT.Exp, [t_e2, t_e1], scale=-1.0)
            yield
            i3, y, free = wide.take()
            t = P.ts(dve, y, a, -1.0, prm("ka", j), ADD, MUL, w=[at_[j], free])
            t_k = P.stt(k, y, 1.0, k, ADD, MUL, [t, kk[j]])
            t = P.stt(y, r, prm("rk", j), k, MUL, MUL, [rt[j], t_k])
            yield
            b, _, free = few.take()
            t = P.mm(ps[:, b], blk, y, True, True, [t, free], True)
            wide.free[i3] = [t]
            yield
            t_bv = P.tt(dve, lw, ps[:, b], VF[:, j], MUL, [t, t_lw, vt[j]])
            few.free[b] = [t_bv]
            bv.append(t_bv)
            t1 = P.tt(dve, a, AR[:, 0, j], a, MUL, [t, kk[j]])
            t2 = P.stt(AR[:, 0, j], AR[:, 0, j], -1.0, x, MUL, MUL, [t_e1, t1])
            wide.free[i1] = [t2]
            t3 = P.tt(dve, r, r, e2, MUL, [t_e2, t])
            t4 = P.cp(pool, PC[:, j], e2.rearrange("p (c t) -> p c t", t=64)[:, :, 63], [t_e2])
            wide.free[i2] = [t3, t4]
            t5 = P.tt(pool, a, a, cum, MUL, [t_e3, t1])
            t6 = P.tt(pool, k, k, cum, MUL, [t_e3, t_k, t])
            wide.free[ic] = [t5, t6]
            ready.append([t2, t3, t4, t5, t6])

        weave([scaled(j, wide) for j in range(2)], 2)
        wide = Slots(tmp.bufs[4:] + [HID[:, i] for i in range(4)] + [MORE[:, :], VF[:, 0]])
        wide.free[:] = [[pe.now(), dve.now(), act.now(), pool.now()]] * 8

        sets = []
        for q, x in enumerate((cut0, q0)):
            one = {}
            for name, shape in (("TT", [128, 16, 64]), ("RKB", [128, 16, 2, 64]), ("AKV", [128, 4, 256]), ("KBT", [128, 4, 2, 256])):
                one[name], x = P.place(f"q{name}{q}", shape, F32, x)
            sets.append(one)
        x = cut0 + 24576
        TN, x = P.place("TN", [128, 16, 64], F32, x)
        ZZ, x = P.place("ZZ", [128, 16, 64], F32, x)
        assert x <= cut0 + 32768
        MT, x = P.place("MT", [128, 16, 64], F32, ring0)
        ST, x = P.place("ST", [128, 2, 64], F32, x)
        RH, x = P.place("RH", [128, 2, 2, 64], F32, x)
        VU, x = P.place("VU", [128, 2, 2, 2, 64], F32, x)
        Y1, x = P.place("Y1", [128, 2, 64], F32, x)
        assert x <= ring0 + 8192
        mbs = Slots([TMPS[i][:, :] for i in range(4)])
        mbs.free[:] = wide.free[:4]
        free_banks = Banks([4, 5, 6, 7], bfree)

        def mask(name, n):
            return cst(name, 64).rearrange("p (a j) -> p a j", a=1).to_broadcast([128, n, 64])

        solved = {}

        def solve(q):
            z = sets[q % 2]
            w0 = [pe.now(), dve.now(), act.now(), pool.now()]
            pe.wait(ready[2 * q:2 * q + 2], vn)
            got = []
            for hl in range(4):
                j, r = 2 * q + hl // 2, 64 * (hl % 2)
                it = slice(4 * hl, 4 * hl + 4)
                for c in range(2):
                    b, _, free = free_banks.take()
                    own, across = slice(64 * c, 64 * c + 64), slice(64 - 64 * c, 128 - 64 * c)
                    for n in range(4):
                        f = 128 * n + 64 * c
                        for left, p in ((KB, own), (B, across)):
                            t = P.mm(ps[p, b, 128 * n:128 * n + 128].rearrange("p (a j) -> p a j", a=2),
                                     left[r:r + 64, j, f:f + 64], AR[r:r + 64, :, j, f:f + 64], True, True,
                                     [free], n == 3 and left is B)
                    o = ps[:, b].rearrange("p (n a j) -> p n a j", n=4, a=2)
                    x1 = P.a(MT[across, it], o[across, :, 0], ACT.Copy, [t, w0])
                    x2 = P.tt(dve, ZZ[own, it], o[own, :, 0], mask("stru", 4)[own], MUL, [x1, w0])
                    x3 = P.tt(dve, z["RKB"][:, it, c], o[:, :, 1], mask("incu", 4), MUL, [x1, w0])
                    free_banks.free[b] = [x1, x2, x3]
                    got += [x1, x2, x3]
                yield
            diag = []
            bl = blocks(MT, TN, z["TT"], 0, f"rw{q}", False, list(got), [w0, t], ring0 + 8192, diag)
            next(bl)
            for c in range(2):
                for jl in range(2):
                    b, _, free = free_banks.take()
                    for n in range(4):
                        f = 128 * n + 64 * c
                        for left, p in ((KB, 64 * c), (B, 64 - 64 * c)):
                            t = P.mm(ps[p:p + 64, b, 128 * n:128 * n + 128], left[:, 2 * q + jl, f:f + 64], ident, True, True,
                                     [free], n == 3 and left is B)
                    x = P.a(z["KBT"][:, :, c, 128 * jl:128 * jl + 128], ps[:, b].rearrange("p (n k) -> p n k", n=4), ACT.Copy, [t, w0])
                    free_banks.free[b] = [x]
                    got.append(x)
                yield
            for half in range(2):
                b, _, free = free_banks.take()
                for nl in range(2):
                    n = 2 * half + nl
                    for h in (0, 64):
                        for hl in range(4):
                            jl, par = hl // 2, hl % 2
                            f = 128 * (2 * q + jl) + 64 * par
                            c0 = 256 * nl + 128 * par + 64 * jl
                            t = P.mm(ps[64 - h:128 - h, b, c0:c0 + 64], ZZ[h:h + 64, 4 * hl + n], VT[h:h + 64, n, f:f + 64],
                                     True, True, [free, got], True)
                x = P.a(z["AKV"][:, 2 * half:2 * half + 2], ps[:, b].rearrange("p (n k) -> p n k", n=2), ACT.Copy, [t, w0])
                free_banks.free[b] = [x]
                got.append(x)
            yield
            for _ in bl:
                yield
                yield
            tris = [[diag, t], [diag, t]]
            gens = [inverse(MT, TN, z["TT"], ZZ, 8 * i, 8, "up", got, free_banks, "TT", mbs, tris[i], pool) for i in range(2)]
            while gens:
                for g in list(gens):
                    try:
                        next(g)
                        yield
                    except StopIteration:
                        gens.remove(g)
            solved[q] = [got, tris]

        yt = [[] for _ in range(KT)]

        def recur(q):
            z = sets[q % 2]
            w = solved[q]
            ts = P.memset(dve, ST[:, :, :], 0.0, [pe.now(), dve.now()])
            tyl = dve.now()

            def values(ch):
                p = slice(64 * (ch % 2), 64 * (ch % 2) + 64)
                return P.a(VU[p, ch % 2], VT[p, ch // 2, 256 * q:256 * q + 256].rearrange("p (j a v) -> p a j v", j=2, a=2),
                           ACT.Copy, [pe.now()])

            tv = values(0)
            for ch in range(8):
                n, c = ch // 2, ch % 2
                P_ = slice(64 - 64 * c, 128 - 64 * c)
                tv, t_v = values(ch + 1) if ch < 7 else None, tv
                for par in range(2):
                    r = slice(64 * par, 64 * par + 64)
                    for jl in range(2):
                        j = 2 * q + jl
                        f = 64 * ch
                        P.mm(ps[P_, par, 64 * jl:64 * jl + 64], AR[r, 0, j, f:f + 64], ST[r, jl], True, True, [ts, w, bfree[par]])
                        t = P.mm(ps[r, par, 256 + 64 * jl:256 + 64 * jl + 64], ST[r, jl], AR[r, 1, j, f:f + 64], True, True,
                                 inc=par == 1 and jl == 1)
                tr = P.tt(dve, RH[P_], ps[P_, 0:2, 0:128].rearrange("p a (j v) -> p a j v", j=2),
                          z["AKV"][P_, n].rearrange("p (a j v) -> p a j v", a=2, j=2), ADD, [t])
                ty = [P.cp(dve, Y1[64 * par:64 * par + 64], ps[64 * par:64 * par + 64, par, 256:384].rearrange("p (j v) -> p j v", j=2), [t, tyl])
                      for par in range(2)]
                bfree[0], bfree[1] = [tr, ty], [tr, ty]
                yield
                for par in range(2):
                    for jl in range(2):
                        hl = 2 * jl + par
                        t = P.mm(ps[P_, 2, 128 * par + 64 * jl:128 * par + 64 * jl + 64], z["TT"][P_, 4 * hl + n], RH[P_, par, jl],
                                 True, True, [tr, bfree[2]], par == 1 and jl == 1)
                tu = P.a(VU[P_, c], ps[P_, 2, 0:256].rearrange("p (a j v) -> p a j v", a=2, j=2), ACT.Copy, [t])
                bfree[2] = [tu]
                yield
                for part in range(2):
                    for par in range(2):
                        r = slice(64 * par, 64 * par + 64)
                        for jl in range(2):
                            it = 4 * (2 * jl + par) + n
                            vu = VU[:, c, par, jl]
                            if part == 0:
                                P.mm(ps[r, 3, 64 * jl:64 * jl + 64], z["KBT"][:, n, c, 128 * jl + 64 * par:128 * jl + 64 * par + 64], vu,
                                     True, True, [bfree[3], tu, t_v])
                            else:
                                t = P.mm(ps[r, 3, 128 + 64 * jl:192 + 64 * jl], vu, z["RKB"][:, it, c], True, True,
                                         inc=par == 1 and jl == 1)
                ts = P.tt(dve, ST[:, :, :], ST[:, :, :], ps[:, 3, 0:128].rearrange("p (j v) -> p j v", j=2), ADD, [t])
                ts = P.tt(dve, ST[:, :, :], ST[:, :, :], PC[:, 2 * q:2 * q + 2, ch:ch + 1].to_broadcast([128, 2, 64]), MUL, [ts])
                ty = P.tt(dve, AR[:, 1, 2 * q:2 * q + 2, 64 * ch:64 * ch + 64], ps[:, 3, 128:256].rearrange("p (j v) -> p j v", j=2),
                          Y1[:, :, :], ADD, [t, ty])
                bfree[3] = [ts, ty]
                tyl = ty
                yield
            yt[2 * q] = yt[2 * q + 1] = [ty]

        yx = [None] * KT

        def group(js, banks, last):
            todo, xs = [], []

            def spread(j):
                y = AR[:, 1, j]
                b, _, free = banks.take()
                t = P.mm(ps[:, b], blk, y, True, True, [free, yt[j]], True)
                tc = P.stt(y, ps[:, b], -1.0 / 64, y, MUL, ADD, [t])
                banks.free[b] = [tc]
                yield
                i, x, free = tmp.take()
                t = P.a(x, y, ACT.Square, [tc, free])
                yield
                b, _, free = banks.take()
                t = P.mm(ps[:, b], blk, x, True, True, [free, t], True)
                todo.append((x, ps[:, b], [t]))
                xs.append((j, i, x, y, b))

            def gated(j, i, x, y, b, t1, t):
                banks.free[b] = [t1]
                t = P.tt(dve, x, x, y, MUL, [t])
                yield
                t = P.ts(dve, x, x, prm("lnw", j), prm("lnb", j), MUL, ADD, [t])
                yield
                t = P.tt(dve, x, x, LW[:, j], ADD, [t])
                yield
                if last:
                    t = P.tt(dve, x, x, G[:, j], MUL, [t])
                    yield
                    yx[j] = split(x, j, t)
                    tmp.free[i] = yx[j]
                else:
                    yx[j] = [P.tt(dve, y, x, G[:, j], MUL, [t])]
                    tmp.free[i] = yx[j]

            yield from weaving([spread(j) for j in js], len(js))
            first, second = P.rsqrts(todo, prm("gneps"), 1.0 / 64)
            yield
            yield from weaving([gated(*x, t1, t) for x, t1, t in zip(xs, first, second)], 2)

        def early_groups():
            for js in (range(0, 3), range(3, 6)):
                tmp.free[:] = [[pe.now(), dve.now(), act.now(), pool.now()]] * len(tmp.free)
                yield from group(js, free_banks, False)

        weave([weaving([scaled(j, wide) for j in range(2, KT)], 2), solve(0)], 2)
        P.barrier()
        for q in range(3):
            ahead = solve(q + 1)
            for _ in range(3):
                next(ahead)
            weave([recur(q), ahead], 2)
        t_h = P.dma(sp, H[:, :, :], hs, s_h, [pe.now()])
        weave([recur(3), early_groups()], 2)
        P.barrier()
        W.load(W.i + 2)
        W.split(W.i)
        weave([group(range(6, 8), bank, True)], 1)
        for j in range(6):
            yx[j] = split(AR[:, 1, j], j, yx[j])
        ht = [t_h] * KT
        gemm(KT, residual(ht), yx)
        P.barrier()
        ht = ffn(1, ht)

        P.barrier()
        ht = norm("fing", 0, ht, inplace=True)
        xt = norm("ln1", 0, ht, w=[pe.now()])
        QK, at = P.place("QK", [128, 8, S], F32, base)
        AV, at = P.place("AV", [128, 4, S], F32, at)
        KQ, at = P.place("KQ", [128, 2, 4, S], F32, at)
        DV, at = P.place("DV", [128, 4, S], F32, at)
        ZG, at = P.place("ZG", [128, 4, S], F32, at)
        AT, at = P.place("AT", [128, 4, S], F32, at)
        AB, at = P.place("AB", [128, 4, 16], F32, at)
        R8, at = P.place("R8", [128, 2, 8], F32, at)
        tail = at
        s_b = P.sem("s_b")
        t_r8 = P.dma(sp, R8[:, :, :], A["rows8"], s_b)
        qt, av, dt_, ab = [None] * 8, [], [None] * 16, []
        gemm(8, into(QK, qt), xt)

        def evac_av(ch, n, o, t):
            av.append(P.a(AV[:, n, 256 * ch:256 * ch + 256], o, ACT.Copy, [t]))
            return [av[-1]]

        gemm_tok(2, 256, evac_av, xt)

        def evac_dn(m, o, t):
            if m >= 12:
                dt_[m] = P.a(ZG[:, m - 12], o, ACT.Silu, [t])
                return [dt_[m]]
            i, z, free = tmp.take()
            w = [prm("dncw", 12 * j + m) for j in range(5)]
            t1 = P.a(z, o, ACT.Copy, [t, free], scale=w[2])
            t1 = P.stt(z[:, 2:S], o[:, 0:S - 2], w[0], z[:, 2:S], MUL, ADD, [t1])
            t1 = P.stt(z[:, 1:S], o[:, 0:S - 1], w[1], z[:, 1:S], MUL, ADD, [t1])
            t1 = P.stt(z[:, 0:S - 1], o[:, 1:S], w[3], z[:, 0:S - 1], MUL, ADD, [t1])
            t1 = P.stt(z[:, 0:S - 2], o[:, 2:S], w[4], z[:, 0:S - 2], MUL, ADD, [t1])
            dst = KQ[:, 1, m] if m < 4 else KQ[:, 0, m - 4] if m < 8 else DV[:, m - 8]
            dt_[m] = P.a(dst, z, ACT.Silu, [t1])
            tmp.free[i] = [dt_[m]]
            return [t1]

        gemm(16, evac_dn, xt)

        i_ab, y_ab, free_ab = tmp.take()

        def evac_ab(m, o, t):
            ab.append(P.cp(dve, y_ab[0:16], o[0:16], [t, free_ab]))
            return ab[:]

        gemm(1, evac_ab, xt, 1)
        b, _, free = bank.take()
        for n in range(4):
            t = P.tr(ps[:, b, 16 * n:16 * n + 16], y_ab[0:16, 128 * n:128 * n + 128], ident[0:16, 0:16], [ab, free], n == 3)
        tmp.free[i_ab] = [t]
        ab[:] = [P.cp(dve, AB[:, :, :], ps[:, b, 0:64].rearrange("p (n j) -> p n j", n=4), [t])]
        bank.free[b] = ab[:]
        projected = pe.now()
        BT, _ = P.place("BT", [128, 8, 16, 64], F32, xs0)
        P.dma(sp, BT[0:64, :, 0:15], A["rpb"], s_b, [projected])
        tb = [P.dma(sp, BT[64:128, :, 1:16], A["rpb"], s_b)]
        def squares(todo, xs, m, v, tv, sum_):
            i, x, free = tmp.take()
            t = P.a(x, v, ACT.Square, [tv, free])
            yield
            b, _, free = bank.take()
            t = P.mm(ps[:, b], sum_, x, True, True, [t, free], True)
            todo.append((x, ps[:, b], [t]))
            xs.append((m, i, x, b))

        for m0 in (0, 4):
            todo, xs = [], []
            weave([squares(todo, xs, m, QK[:, m], qt[m], blk) for m in range(m0, m0 + 4)], 4)
            first, second = P.rsqrts(todo, prm("eps"), 1.0 / 64)
            for (m, i, x, b), t1, t in zip(xs, first, second):
                bank.free[b] = [t1]
                qt[m] = P.stt(QK[:, m], QK[:, m], prm("qg" if m < 4 else "kg"), x, MUL, MUL, [t])
                tmp.free[i] = [qt[m]]
        for m0 in (0, 4):
            todo, xs = [], []
            weave([squares(todo, xs, m, KQ[:, 1 - m // 4, m % 4], dt_[m], ones) for m in range(m0, m0 + 4)], 4)
            first, second = P.rsqrts(todo, prm("eps"))
            for (m, i, x, b), t1, t in zip(xs, first, second):
                v = KQ[:, 1 - m // 4, m % 4]
                bank.free[b] = [t1]
                dt_[m] = P.stt(v, v, float(128 ** -0.5) if m < 4 else 1.0, x, MUL, MUL, [t])
                tmp.free[i] = [dt_[m]]

        x = tail
        ATT, x = P.place("ATT", [128, 32, 64], F32, x)
        at_oo = x
        OO, x = P.place("OO", [128, 4, S], F32, x)
        names = ("GG", "GC", "EG", "ED", "BE", "NB", "BG", "GL", "SC1", "SC2")
        sc = {}
        for name in names:
            sc[name], x = P.place(f"d{name}", [128, 2, 4, 4], F32, x)
        EH, x = P.place("EH", [128, 2, 32], F32, x)
        GT, x = P.place("GT", [128, 2, 4, 128], F32, x)
        QS, x = P.place("QS", [128, 2, 4, S], F32, xs0)
        WT, x = P.place("WT", [128, 2, 32, 64], F32, x)
        UV, x = P.place("UV", [128, 32, 128], F32, base)
        KK, x = P.place("KKT", [128, 4, 4, 128], F32, x)
        assert x <= base + 24576
        MM, x = P.place("MM", [128, 32, 64], F32, cut0)
        TR, x = P.place("TR", [128, 32, 64], F32, x)
        TX, x = P.place("TX", [128, 32, 64], F32, x)
        ZX, x = P.place("ZX", [128, 32, 64], F32, x)
        KG, x = P.place("KG", [128, 32, 128], F32, ring0)
        SS2, x = P.place("SS2", [128, 2, 8, 128], F32, DVo := base + 16384 + 8192 + 16384)
        VN, x = P.place("VN", [128, 2, 4, 128], F32, cut0)

        def flat(name):
            return sc[name][:, :, :, :].rearrange("p d n h -> p (d n h)")

        def of_ab(k):
            return AB[:, :, 8 * k:8 * k + 8].rearrange("p n (d h) -> p d n h", d=2)

        def row(k):
            return R8[:, k].rearrange("p (d a h) -> p d a h", d=2, a=1).to_broadcast([128, 2, 4, 4])

        full = {k: sc[k][:, :, :, :] for k in names}
        t = P.tt(dve, full["SC1"], of_ab(0), row(0), ADD, [ab, t_r8])
        t1 = P.ts(dve, flat("SC2"), flat("SC1"), -1.0, None, MUL, w=[t])
        t1 = P.tt(dve, flat("SC2"), flat("SC2"), flat("SC1"), MAX, [t1])
        t1 = P.a(flat("SC2"), flat("SC2"), ACT.Exp, [t1], scale=-1.0)
        t1 = P.a(flat("SC2"), flat("SC2"), ACT.Ln, [t1], bias=prm("one"))
        t = P.ts(dve, flat("SC1"), flat("SC1"), 0.0, None, MAX, w=[t1])
        t = P.tt(dve, flat("SC1"), flat("SC1"), flat("SC2"), ADD, [t])
        t1 = P.a(R8[:, 1], R8[:, 1], ACT.Exp, [t_r8])
        t = P.tt(dve, full["GG"], full["SC1"], row(1), MUL, [t, t1])
        t_g = P.ts(dve, flat("GG"), flat("GG"), -1.0, None, MUL, w=[t])
        t_be = P.a(full["BE"], of_ab(1), ACT.Sigmoid, [ab])
        b, _, free = bank.take()
        P.mm(ps[:, b, 0:16], cst("cumf", 128), flat("GG")[:, 0:16], True, True, [t_g, free])
        P.mm(ps[:, b, 16:32], cst("cumb", 128), flat("GG")[:, 16:32], True, True)
        P.mm(ps[:, b, 32:64], blk, flat("GG"), True, True)
        P.mm(ps[:, b, 64:96], cst("half", 128), flat("GG"), True, True)
        t = P.mm(ps[:, b, 96:128], cst("half", 128, 128), flat("GG"), True, True, inc=True)
        t_gc = P.cp(dve, flat("GC"), ps[:, b, 0:32], [t])
        t_gl = P.tt(dve, flat("GL"), ps[:, b, 32:64], flat("GC"), SUB, [t_gc])
        t_eh = P.a(EH[:, :, :].rearrange("p a b -> p (a b)"), ps[:, b, 64:128], ACT.Exp, [t_gl])
        bank.free[b] = [t_gl, t_eh]
        t_e = P.a(flat("EG"), flat("GC"), ACT.Exp, [t_gc])
        t_ed = P.a(flat("ED"), flat("GL"), ACT.Exp, [t_gl])
        t_nb = P.ts(dve, flat("NB"), flat("BE"), -1.0, None, MUL, w=[t_be])
        t_bg = P.tt(dve, flat("BG"), flat("BE"), flat("EG"), MUL, [t_be, t_e])

        def spread(name, d, n, width):
            return sc[name][:, d, n, :].rearrange("p (h a) -> p h a", a=1).to_broadcast([128, 4, width])

        tm = {}
        early_tiles, early_banks = Banks([5], bfree), Banks([4], bfree)
        gt_slot = Slots([GT[:, i] for i in range(2)])
        within = {}

        def inside(n, d):
            if d == 0:
                bk, _, free = early_tiles.take()
                for h in range(4):
                    for p in (0, 64):
                        f = 128 * n + p
                        t = P.mm(ps[p:p + 64, bk, 128 * h:128 * h + 128].rearrange("p (a j) -> p a j", a=2), KQ[:, 0, h, f:f + 64],
                                 KQ[:, :, h, f:f + 64], True, True, [free], h == 3 and p > 0)
                within[n] = (bk, t, [])
            bk, t_kk, users = within[n]
            o = ps[:, bk].rearrange("p (h a j) -> p h a j", h=4, a=2)
            i0 = 16 * d + 4 * n
            ig, g, gfree = gt_slot.take()
            tg = P.tt(dve, g, blk.rearrange("p (a j) -> p a j", a=1).to_broadcast([128, 4, 128]), spread("GC", d, n, 128), MUL, [t_gc, gfree])
            yield
            b, _, free = early_banks.take()
            for h in range(4):
                t = P.mm(ps[:, b, 64 * h:64 * h + 64], g[:, h], cst("i2", 64), True, True, [free, tg], h == 3)
            gt_slot.free[ig] = [t]
            i1, y, free = tmp.take()
            y1 = y[:, 0:256].rearrange("p (h j) -> p h j", h=4)
            y2 = y[:, 256:512].rearrange("p (h j) -> p h j", h=4)
            t = P.tt(dve, y1, ps[:, b, 0:256].rearrange("p (h j) -> p h j", h=4), spread("GC", d, n, 64), SUB, [t, free])
            bfree[b] = [t]
            t2 = P.ts(dve, y2, y1, 0.0, None, MIN, w=[t])
            t1 = P.ts(dve, y1, y1, 0.0, None, MAX, w=[t2])
            t1 = P.a(y1, y1, ACT.Exp, [t1], scale=-1.0)
            t2 = P.a(y2, y2, ACT.Exp, [t2])
            yield
            t1 = P.tt(dve, y1, y1, o[:, :, 0], MUL, [t1, t_kk])
            t2 = P.tt(dve, y2, y2, o[:, :, 1], MUL, [t2, t_kk])
            users += [t1, t2]
            bfree[bk] = users
            tm[d, n] = P.tt(dve, MM[:, i0:i0 + 4], y1, spread("NB", d, n, 64), MUL, [t1, t_nb, projected])
            t3 = P.tt(dve, ATT[:, i0:i0 + 4], y2, mask("incl" if d else "incu", 4), MUL, [t2])
            tmp.free[i1] = [tm[d, n], t3]
            tm["a", d, n] = t3


        diag = [[], []]

        def early():
            for n in range(4):
                for d in range(2):
                    yield from inside(n, d)
            before = [tm[d, n] for n in range(4) for d in range(2)]
            both = [blocks(MM, TR, TX, 16 * d, f"dn{d}", not d, before, [before, projected],
                           at_oo + 4096 * d, diag[d]) for d in range(2)]
            while both:
                for g in list(both):
                    try:
                        next(g)
                        yield
                    except StopIteration:
                        both.remove(g)

        x = ring0
        LG, PM, PT = [], [], []
        for i in range(2):
            for lst, name in ((LG, "LG"), (PM, "PM"), (PT, "PT")):
                y, x = P.place(f"{name}{i}", [128, S], F32, x)
                lst.append(y[:, :])
        AO, x = P.place("AO", [128, S], F32, x)
        MX, x = P.place("MX", [128, 32], F32, x)
        SU, x = P.place("SU", [128, 32], F32, x)
        SQ, x = P.place("SQ", [128, 4], F32, x)
        lg, pm, pt = Slots(LG), Slots(PM), Slots(PT)
        assert x <= cut0
        for z in (lg, pm, pt):
            z.free[:] = [[projected], [projected]]
        at_banks = Banks([0, 1, 2, 3], bfree)
        out_banks = Banks([6, 7], bfree)
        work = [(r, h) for r in range(4) for h in range(8)]
        scored, turned = {}, {}

        def score(i):
            r, h = work[i]
            p = slice(64 * (h % 2), 64 * (h % 2) + 64)
            b, _, free = at_banks.take()
            t = P.mm(ps[:, b], QK[p, h // 2, 128 * r:128 * r + 128], QK[p, 4 + h // 2, :], True, True, [free, qt], True)
            il, l, free = lg.take()
            d = 7 - 2 * r
            t = P.stt(l, ps[:, b], 0.125, BT[:, h, d:d + 8].rearrange("p d j -> p (d j)"), MUL, ADD, [t, tb, free])
            at_banks.free[b] = [t]
            t2 = dve.put(lambda e, l=l, o=MX[:, i:i + 1]: e.tensor_reduce(o, l, AX.X, MAX, negate=True), [t])
            ip, e, free = pm.take()
            t = P.a(e, l, ACT.Exp, [t2, free], bias=MX[:, i:i + 1], accum=SU[:, i:i + 1])
            lg.free[il] = [t]
            scored[i] = (ip, e, t)

        def turn(i):
            ip, e, t = scored[i]
            b, _, free = at_banks.take()
            for k in range(4):
                t1 = P.tr(ps[:, b, 128 * k:128 * k + 128], e[:, 128 * k:128 * k + 128], ident, [t, free], k == 3)
            pm.free[ip] = [t1]
            it, q, free = pt.take()
            if i % 2:
                t1 = P.a(q, ps[:, b], ACT.Copy, [t1, free])
            else:
                t1 = P.cp(dve, q, ps[:, b], [t1, free])
            at_banks.free[b] = [t1]
            turned[i] = (it, q, t1)

        ob = {}
        att = []

        def value(i):
            r, h = work[i]
            if h == 0:
                b, _, free = out_banks.take()
                ob[r] = (b, free)
            b, free = ob[r]
            it, q, t = turned[i]
            for k in range(4):
                t1 = P.mm(ps[:, b, 64 * h:64 * h + 64], q[:, 128 * k:128 * k + 128], AV[:, k, 64 * h:64 * h + 64], k == 0, k == 3,
                          [t, free, av], k == 3)
            pt.free[it] = [t1]
            if h < 7:
                return
            s = SU[:, 8 * r:8 * r + 8]
            t2 = P.recip(s, s, [scored[i][2]])
            t2 = P.tt(dve, AO[:, :].rearrange("p (h d) -> p h d", h=8), ps[:, b].rearrange("p (h d) -> p h d", h=8),
                      s.rearrange("p (h a) -> p h a", a=1).to_broadcast([128, 8, 64]), MUL, [t1, t2, att])
            bfree[b] = [t2]
            i1, x, free = tmp.take()
            t = P.a(x, AO[:, :], ACT.Square, [t2, free], accum=SQ[:, r:r + 1])
            tmp.free[i1] = [t]
            t = P.a(SQ[:, r:r + 1], SQ[:, r:r + 1], ACT.Sqrt, [t], bias=prm("eps"), scale=1.0 / 512)
            t = P.recip(SQ[:, r:r + 1], SQ[:, r:r + 1], [t])
            t = P.ts(dve, AO[:, :], AO[:, :], SQ[:, r:r + 1], None, MUL, w=[t])
            b, _, free = at_banks.take()
            for k in range(4):
                t1 = P.tr(ps[:, b, 128 * k:128 * k + 128], AO[:, 128 * k:128 * k + 128], ident, [t, free], k == 3)
            new = []
            for k in range(4):
                new.append(P.a(AT[:, k, 128 * r:128 * r + 128], ps[:, b, 128 * k:128 * k + 128], ACT.Copy, [t1], scale=prm("aog", k)))
            at_banks.free[b] = new
            att.append(t1)
            atts.append(new)

        atts = []
        meanwhile = early()
        for i in range(len(work) + 2):
            if i < len(work):
                score(i)
            if 1 <= i < len(work) + 1:
                turn(i - 1)
            if i >= 2:
                value(i - 2)
            next(meanwhile, None)
        for _ in meanwhile:
            pass
        P.barrier()
        tv, tk = {}, []
        for n in range(4):
            b, _, free = bank.take()
            for h in range(4):
                t = P.tr(ps[:, b, 128 * h:128 * h + 128], DV[:, h, 128 * n:128 * n + 128], ident, [free, dt_], h == 3)
            o = ps[:, b].rearrange("p (h v) -> p h v", h=4)
            for d in range(2):
                i0 = 16 * d + 4 * n
                tv[d, n] = P.tt(dve, UV[:, i0:i0 + 4], o, spread("BE", d, n, 128), MUL, [t, t_be])
            bank.free[b] = [tv[0, n], tv[1, n]]
            b, _, free = bank.take()
            for h in range(4):
                t = P.tr(ps[:, b, 128 * h:128 * h + 128], KQ[:, 0, h, 128 * n:128 * n + 128], ident, [free, dt_], h == 3)
            tk.append(P.a(KK[:, n], ps[:, b].rearrange("p (h v) -> p h v", h=4), ACT.Copy, [t]))
            bank.free[b] = [tk[-1]]
        tkg = {}
        for d in range(2):
            for n in range(4):
                i0 = 16 * d + 4 * n
                tkg[d, n] = P.tt(pool, KG[:, i0:i0 + 4], KK[:, n], spread("BG", d, n, 128), MUL, [tk[n], t_bg])
        tq = []
        for d in range(2):
            for h in range(4):
                b, _, free = bank.take()
                for n in range(4):
                    t = P.mm(ps[:, b, 128 * n:128 * n + 128], sc["EG"][:, d, n, h:h + 1].to_broadcast([128, 128]), ident, True, True,
                             [free, t_e], n == 3)
                tq.append(P.tt(dve, QS[:, d, h], ps[:, b], KQ[:, 1, h], MUL, [t, dt_]))
                bank.free[b] = [tq[-1]]
        tris = [[] for _ in range(4)]
        more, _ = P.place("MBS", [128, 2, S], F32, xs0 + 16384)
        mbs = Slots([TMPS[i][:, :] for i in range(6)] + [more[:, 0], more[:, 1]])
        for i in range(8):
            mbs.free[i] = [tm["a", 0, 3], tm["a", 1, 3], tm[1, 3], tm[0, 3]]
        gens = []
        for i in range(4):
            d = i // 2
            tris[i].append(diag[d])
            n = 2 * (i % 2)
            gens.append(inverse(MM, TR, TX, ZX, 8 * i, 8, "up" if d else "lo", [tm[d, n], tm[d, n + 1]], bank, "T", mbs, tris[i], pool))
        weave(gens, 2)
        tu, tw = [], []
        for i0 in range(0, 32, 4):
            d, n = i0 // 16, i0 % 16 // 4
            b, _, free = bank.take()
            for q in range(4):
                for p in (0, 64):
                    t = P.mm(ps[p:p + 64, b, 128 * q:128 * q + 128], TR[p:p + 64, i0 + q], UV[p:p + 64, i0 + q], True, True,
                             [free, tris[i0 // 8], tv[d, n]], q == 3 and p > 0)
            tu.append(P.cp(dve, UV[:, i0:i0 + 4], ps[:, b].rearrange("p (q v) -> p q v", q=4), [t]))
            bank.free[b] = [tu[-1]]
        for i0 in range(0, 32, 8):
            bs = [bank.take() for _ in range(2)]
            d, n = i0 // 16, i0 % 16 // 4
            for q in range(8):
                for a, p in enumerate((0, 64)):
                    t = P.mm(ps[:, bs[a][0], 64 * q:64 * q + 64], KG[p:p + 64, i0 + q], TR[p:p + 64, i0 + q], True, True,
                             [bs[0][2], bs[1][2], tkg[d, n], tkg[d, n + 1]], q == 7 and a == 1)
            for a in range(2):
                tw.append(P.a(WT[:, a, i0:i0 + 8], ps[:, bs[a][0]].rearrange("p (q j) -> p q j", q=8), ACT.Copy, [t, projected]))
                bank.free[bs[a][0]] = [tw[-1]]
        tkd = []
        for d in range(2):
            for n in range(4):
                i0 = 16 * d + 4 * n
                tkd.append(P.tt(pool, KG[:, i0:i0 + 4], KK[:, n], spread("ED", d, n, 128), MUL, [t_ed, pe.now()]))
        P.barrier()
        st = P.memset(dve, SS2[:, 0], 0.0)
        tso = [st, st]
        to = {}
        tpool = None
        for s in range(8):
            geo = []
            for d in range(2):
                ch = s if d == 0 else 7 - s
                geo.append((ch, ch // 2, ch % 2, slice(64 * (ch % 2), 64 * (ch % 2) + 64)))
            for d in range(2):
                ch, n, hf, p = geo[d]
                for h in range(4):
                    it = 16 * d + 4 * n + h
                    P.mm(ps[p, d, 128 * h:128 * h + 128], WT[:, hf, it], SS2[:, 0, 4 * d + h], True, True, [tso[d], bfree[d]])
                for h in range(4):
                    ta = P.mm(ps[:, 4 + d, 64 * h:64 * h + 64], SS2[:, 0, 4 * d + h], QS[:, d, h, 64 * ch:64 * ch + 64], h == 0, False,
                              [bfree[4 + d]], h == 3, skip=True)
                geo[d] = geo[d] + (ta,)
            tp = []
            for d in range(2):
                ch, n, hf, p, ta = geo[d]
                i0 = 16 * d + 4 * n
                tn = P.tt(dve, VN[p, d], UV[p, i0:i0 + 4], ps[p, d].rearrange("p (h v) -> p h v", h=4), SUB, [ta])
                bfree[d] = [tn]
                tp.append(P.tt(pool, SS2[:, 1, 4 * d:4 * d + 4], SS2[:, 0, 4 * d:4 * d + 4],
                               EH[:, hf, i0:i0 + 4].rearrange("p (h a) -> p h a", a=1).to_broadcast([128, 4, 128]), MUL,
                               [tso[d]]))
                for h in range(4):
                    t = P.mm(ps[:, 2 + d, 128 * h:128 * h + 128], KG[p, i0 + h], VN[p, d, h], True, True, [tn, bfree[2 + d]], h == 3)
                geo[d] = geo[d] + (t,)
            for d in range(2):
                ch, n, hf, p, ta, t = geo[d]
                i0 = 16 * d + 4 * n
                tso[d] = P.tt(dve, SS2[:, 0, 4 * d:4 * d + 4], SS2[:, 1, 4 * d:4 * d + 4],
                              ps[:, 2 + d].rearrange("p (h v) -> p h v", h=4), ADD, [t, tp[d]])
                bfree[2 + d] = [tso[d]]
                for h in range(4):
                    t = P.mm(ps[:, 4 + d, 64 * h:64 * h + 64], VN[p, d, h], ATT[p, i0 + h], False, h == 3, inc=h == 3, skip=True)
                o = ps[:, 4 + d, 0:256].rearrange("p (h j) -> p h j", h=4)
                dst = OO[:, :, 64 * ch:64 * ch + 64]
                if ch in to:
                    to[ch] = P.tt(dve, dst, o, dst, ADD, [t, to[ch]])
                else:
                    to[ch] = P.a(dst, o, ACT.Copy, [t])
                bfree[4 + d] = [to[ch]]
        P.barrier()
        W.load(W.i + 2)
        todo, xs = [], []
        weave([squares(todo, xs, h, OO[:, h], None, ones) for h in range(4)], 4)
        xt = [split(AT[:, k], k, None) for k in range(4)]
        W.split(W.i)
        first, second = P.rsqrts(todo, prm("eps"), 1.0 / 128)
        for (h, i, x, b), t1, t in zip(xs, first, second):
            bank.free[b] = [t1]
            t = P.tt(dve, x, x, OO[:, h], MUL, [t])
            t = P.stt(x, x, prm("dng"), ZG[:, h], MUL, MUL, [t])
            xt.append(split(x, 4 + h, t))
            tmp.free[i] = xt[-1]

        def expert(name, e_):
            if name == "down":
                pat, pat1 = "(j p) n -> p j n", "a (j p) n -> p (a j) n"
            else:
                pat, pat1 = "(p k) n -> p k n", "a (p k) n -> p (a k) n"
            w = A[f"e_{name}"]
            if e_ < 64:
                return w[e_].rearrange(pat, p=128)

            def src(e):
                if e_ not in regs:
                    regs[e_] = e.value_load(OVI[0:1, e_ - 64:e_ - 63], min_val=0, max_val=63)
                return w[bass.ds(regs[e_], 1)].rearrange(pat1, p=128)
            return src

        regs = {}
        todo = []
        for i in range(65):
            todo += [("gate", i), ("up", i)] if i < 64 else []
            todo += [("down", i - 1)] if i else []
        for i in range(64, 2 * NP, 2):
            todo += [(x, i + z) for x, z in (("gate", 0), ("up", 0), ("gate", 1), ("up", 1), ("down", 0), ("down", 1))]
        E = Ring(P, "s_e", [P.place(f"ew{i}", [128, 2048], F32, base + 8192 * i)[0] for i in range(11)],
                 [(expert(*x), 2 if x[0] == "down" else KT) for x in todo], [pe.now(), dve.now(), act.now(), pool.now()], 192)
        gemm(KT, residual(ht), xt)
        E.load(11)

        P.barrier()
        XN, x = P.place("XN", [128, KT, S], F32, xs0)
        TK, x = P.place("TK", [128, 4, D], F32, x)
        HT, x = P.place("HT", [128, 4, D], F32, ring0)
        XG = []
        for i in range(3):
            y, x = P.place(f"XG{i}", [128, D], F32, x)
            XG.append(y)
        RW, x = P.place("RW", [128, KT, 72], F32, x)
        RB, x = P.place("RB", [128, 72], F32, x)
        HID2, x = P.place("HID2", [128, 2, 2, 64], F32, x)
        SIL, x = P.place("SIL", [128, 2, 2, 64], F32, x)
        GATES, x = P.place("GATES", [128, 2, 4], F32, x)
        SRC, x = P.place("SRC", [128, NP], I32, x)
        DST, x = P.place("DST", [128, NP], I32, x)
        OVI, x = P.place("OVI", [1, NOV + 1], I32, x)
        scratch0 = x
        s_r = P.sem("s_r")
        P.dma(sp, RW[:, :, :].rearrange("p k n -> p (k n)"), A["router_w"], s_r)
        t_rw = P.dma(sp, RB[:, :], A["router_b"], s_r)
        xtok = nc.dram_tensor("xtok", [S, D], F32, kind="Internal").ap()
        otok = nc.dram_tensor("otok", [2 * S, D], F32, kind="Internal").ap()
        t_xg = [P.memset(pool, XG[i][:, :], 0.0) for i in range(3)]

        ia, acc, ta = square_sum([H[:, k] for k in range(KT)], ht)
        ir, r, tr = rstd_of(acc, D, "eps", ta)
        tmp.free[ia] = [pe.now()]
        xn = [P.stt(XN[:, k], H[:, k], prm("ln2", k), r, MUL, MUL, [tr, ht[k]]) for k in range(KT)]
        tmp.free[ir] = [xn[-1]]
        b, _, free = bank.take()
        for n in range(4):
            for k in range(KT):
                t = P.mm(ps[:, b, 72 * n:72 * n + 72], XN[:, k, 128 * n:128 * n + 128], RW[:, k], k == 0, k == KT - 1,
                         [free, xn, t_rw], n == 3 and k == KT - 1)
        y = scratch0
        sc = {}

        def small(name, *shape):
            nonlocal y
            sc[name], y = P.place("r" + name, [128] + list(shape), F32, y)
            return sc[name]

        def over(a, n):
            return a.rearrange("p (n a) -> p n a", a=1).to_broadcast([128, 4, n])

        def along(name, n):
            return cst(name, n).rearrange("p (a j) -> p a j", a=1).to_broadcast([128, 4, n])

        LGT = small("LGT", 4, 72)
        t_l = P.tt(dve, LGT[:, :, :], ps[:, b, 0:288].rearrange("p (n j) -> p n j", n=4),
                   RB[:, :].rearrange("p (a j) -> p a j", a=1).to_broadcast([128, 4, 72]), ADD, [t])
        bank.free[b] = [t_l]
        th, tx = [], []
        for n in range(4):
            for half in range(2):
                for srcs, dst, toks in ((H, HT, th), (XN, TK, tx)):
                    b, _, free = bank.take()
                    for q in range(4):
                        t = P.tr(ps[:, b, 128 * q:128 * q + 128], srcs[:, 4 * half + q, 128 * n:128 * n + 128], ident,
                                 [free, xn, ht], q == 3)
                    toks.append(P.a(dst[:, n, 512 * half:512 * half + 512], ps[:, b], ACT.Copy, [t]))
                    bank.free[b] = [toks[-1]]
        s_x = P.sem("s_x")
        t_xt = P.dma(sp, xtok.rearrange("(n p) d -> p n d", p=128), TK[:, :, :], s_x, [tx], store=True)

        def first_max(v, n, w, name):
            m, i, oh = small(name + "m", 4), small(name + "i", 4), small(name + "o", 4, n)
            t1 = P.red(m[:, :], v, MAX, [w])
            t = P.tt(dve, oh[:, :, :], v, over(m[:, :], n), ALU.is_equal, [t1])
            t = P.stt(oh[:, :, :], oh[:, :, :], -100.0, along(f"iota{n}", n), MUL, ADD, [t])
            t = P.red(i[:, :], oh[:, :, :], MIN, [t])
            t = P.ts(dve, i[:, :], i[:, :], 100.0, None, ADD, w=[t])
            t = P.tt(dve, oh[:, :, :], along(f"iota{n}", n), over(i[:, :], n), ALU.is_equal, [t])
            return m, i, oh, t

        gl = LGT[:, :, 0:8]
        gm, gi, goh, t = first_max(gl, 8, t_l, "g")
        pr, ig = small("pr", 4, 8, 8), small("ig", 4, 8)
        tr_ = []
        for n in range(4):
            tr_.append(P.tt(dve, pr[:, n], LGT[:, n, 8:72].rearrange("p (g e) -> p g e", g=8),
                            goh[:, n].rearrange("p (g a) -> p g a", a=1).to_broadcast([128, 8, 8]), MUL, [t]))
        t = P.red(ig[:, :, :], pr[:, :, :, :].rearrange("p n g e -> p n e g"), ADD, tr_)
        m1, i1, o1, t = first_max(ig[:, :, :], 8, t, "a")
        t = P.stt(ig[:, :, :], o1[:, :, :], -1e30, ig[:, :, :], MUL, ADD, [t])
        m2, i2, o2, t = first_max(ig[:, :, :], 8, t, "b")
        t_m = t
        eid, oh = [], []
        for s, i in enumerate((i1, i2)):
            e, o = small(f"eid{s}", 4), small(f"oh{s}", 4, 64)
            t1 = P.stt(e[:, :], gi[:, :], 8.0, i[:, :], MUL, ADD, [t])
            t1 = P.tt(dve, o[:, :, :], along("iota64", 64), over(e[:, :], 64), ALU.is_equal, [t1])
            eid.append(e)
            oh.append(o)
        mm = small("mm", 4, 64)
        t_mm = P.tt(dve, mm[:, :, :], oh[0][:, :, :], oh[1][:, :, :], ADD, [t1])
        b, _, free = bank.take()
        for n in range(4):
            for m in range(n):
                P.mm(ps[:, b, 64 * n:64 * n + 64], ones, mm[:, m], m == 0, False, [t_mm, free])
            P.mm(ps[:, b, 64 * n:64 * n + 64], cst("tri", 128), mm[:, n], n == 0, True, [t_mm, free])
        for m in range(4):
            t = P.mm(ps[:, b, 256:320], ones, mm[:, m], m == 0, m == 3, inc=m == 3)
        rank, cnt, ob, cum = small("rank", 4, 64), small("cnt", 64), small("ob", 64), small("cum", 64)
        t1 = P.cp(dve, rank[:, :, :], ps[:, b, 0:256].rearrange("p (n j) -> p n j", n=4), [t])
        t2 = P.cp(dve, cnt[:, :], ps[:, b, 256:320], [t])
        bank.free[b] = [t1, t2]
        t3 = P.ts(dve, ob[:, :], cnt[:, :], 64.0, None, ALU.is_gt, w=[t2])
        for lim in range(128, S, 64):
            t3 = P.stt(ob[:, :], cnt[:, :], float(lim), ob[:, :], ALU.is_gt, ADD, [t3])
        t3 = dve.put(lambda e: e.tensor_tensor_scan(cum[:, :], cst("ones", 64), ob[:, :], 0.0, MUL, ADD), [t3])
        t5 = P.tt(dve, ob[:, :], cum[:, :], ob[:, :], SUB, [t3])
        big, rk, xo, qq, q1 = small("big", 4, 64), small("rk", 4), small("xo", 4), small("qq", 4), small("q1", 4)
        row, blk_of = [], []
        t = None
        for s in range(2):
            t = P.tt(dve, big[:, :, :], oh[s][:, :, :], rank[:, :, :], MUL, [t1, t_mm, t])
            t = P.red(rk[:, :], big[:, :, :], ADD, [t])
            t = P.tt(dve, big[:, :, :], oh[s][:, :, :], ob[:, :].rearrange("p (a j) -> p a j", a=1).to_broadcast([128, 4, 64]), MUL, [t, t5])
            t = P.red(xo[:, :], big[:, :, :], ADD, [t])
            t = P.ts(dve, qq[:, :], rk[:, :], 64.0, None, ALU.is_ge, w=[t])
            t = P.cp(dve, q1[:, :], qq[:, :], [t])
            for lim in range(128, S, 64):
                t = P.stt(qq[:, :], rk[:, :], float(lim), qq[:, :], ALU.is_ge, ADD, [t])
            t = P.stt(xo[:, :], xo[:, :], 63.0, qq[:, :], ADD, ADD, [t])
            t = P.tt(dve, xo[:, :], xo[:, :], eid[s][:, :], SUB, [t])
            t = P.tt(dve, xo[:, :], xo[:, :], q1[:, :], MUL, [t])
            t = P.tt(dve, xo[:, :], xo[:, :], eid[s][:, :], ADD, [t])
            t = P.stt(rk[:, :], qq[:, :], -64.0, rk[:, :], MUL, ADD, [t])
            a, x = P.place(f"row{s}", [128, 4, 64], F32, ring0 - 12288 + 4096 * s)
            o, x = P.place(f"blk{s}", [128, 4, 2 * NP], F32, x)
            t = P.tt(dve, a[:, :, :], along("iota64", 64), over(rk[:, :], 64), ALU.is_equal, [t])
            t = P.tt(dve, o[:, :, :], along("iota80", 2 * NP), over(xo[:, :], 2 * NP), ALU.is_equal, [t])
            t = P.tt(dve, o[:, :, :], o[:, :, :], over(cst("pair", 4, 4 * s), 2 * NP), MUL, [t])
            row.append(a)
            blk_of.append(o)
        b, _, free = bank.take()
        for z in range(2):
            for s in range(2):
                for n in range(4):
                    v = blk_of[s][:, n].rearrange("p (q z) -> p z q", z=2)[:, z]
                    t2 = P.mm(ps[64 * z:64 * z + 64, b, 0:NP], row[s][:, n], v, s == 0 and n == 0, s == 1 and n == 3, [t, free],
                              z == 1 and s == 1 and n == 3)
        fm, fq = small("fm", NP), small("fq", NP)
        t = P.ts(dve, fq[:, :], ps[:, b, 0:NP], 0.0, float(NOWHERE), ALU.is_equal, MUL, w=[t2])
        t = P.stt(fm[:, :], ps[:, b, 0:NP], -1.0, fq[:, :], ADD, ADD, [t])
        bank.free[b] = [t]
        t_dst = P.cp(dve, DST[:, :], fm[:, :], [t])
        t = P.ts(dve, fq[:, :], fm[:, :], 512.0, -512.0, ALU.is_ge, MUL, w=[t])
        t = P.tt(dve, fm[:, :], fm[:, :], fq[:, :], ADD, [t, t_dst])
        t_src = P.cp(dve, SRC[:, :], fm[:, :], [t])
        ovf = small("ovf", NOV, 64)
        ovs = small("ovs", NOV)
        t4 = P.tt(dve, ovf[:, :, :], cum[:, :].rearrange("p (a j) -> p a j", a=1).to_broadcast([128, NOV, 64]),
                  cst("iota16", NOV).rearrange("p (j a) -> p j a", a=1).to_broadcast([128, NOV, 64]), ALU.is_le, [t3])
        t4 = P.red(ovs[:, :], ovf[:, :, :], ADD, [t4])
        t4 = P.ts(dve, ovs[:, :], ovs[:, :], 63.0, None, MIN, w=[t4])
        t4 = P.cp(dve, OVI[:, 0:NOV], ovs[0:1, :], [t4])
        t_ov = P.cp(dve, OVI[:, NOV:NOV + 1], cum[0:1, 63:64], [t3, t4])
        ge, gs = small("ge", 4, 8), small("gs", 4)
        t1 = P.tt(dve, ge[:, :, :], gl, over(gm[:, :], 8), SUB, [t_m])
        t1 = P.a(ge[:, :, :], ge[:, :, :], ACT.Exp, [t1])
        t1 = P.red(gs[:, :], ge[:, :, :], ADD, [t1])
        t_gp = P.recip(gs[:, :], gs[:, :], [t1])
        ex, dn = small("ex", 4), small("dn", 4)
        t1 = P.tt(dve, ex[:, :], m2[:, :], m1[:, :], SUB, [t_m])
        t1 = P.a(ex[:, :], ex[:, :], ACT.Exp, [t1])
        t2 = P.ts(dve, dn[:, :], ex[:, :], 1.0, None, ADD, w=[t1])
        t2 = P.recip(dn[:, :], dn[:, :], [t2])
        t2 = P.tt(dve, dn[:, :], dn[:, :], gs[:, :], MUL, [t2, t_gp])
        t2 = P.cp(dve, GATES[:, 0], dn[:, :], [t2])
        t_gate = P.tt(dve, GATES[:, 1], dn[:, :], ex[:, :], MUL, [t2])
        assert y <= xs0

        sent = pe.now()
        XT, y = P.place("XT", [128, 2, KT, 128], F32, PRM_END)
        OUTB, y = P.place("OUTB", [128, 2, D], F32, y)
        s_gx = [P.sem(f"s_gx{i}") for i in range(3)]
        s_ox = [P.sem(f"s_ox{i}") for i in range(2)]
        s_gy, s_oy = P.sem("s_gy"), P.sem("s_oy")
        MARK, y = P.place("MARK", [1, NP], F32, y)
        gfree = [[t_xg[i]] for i in range(3)]
        gathered = {}

        def gather(q):
            if q >= NP:
                return
            i = q % 3
            pool.wait(gfree[i], t_xt, t_src)
            sem = s_gy if q > 32 else s_gx[i]
            gathered[q] = P.counted_up(pool, sem, q > 32)
            pool.list.append(lambda e: e.indirect_dma_start(
                out=XG[i][:, :], out_offset=None, in_=xtok,
                in_offset=bass.IndirectOffsetOnAxis(ap=SRC[:, q:q + 1], axis=0),
                bounds_check=S - 1, oob_is_err=False).then_inc(sem, 16))

        xfree = [[sent, th, tx, xn], [sent, th, tx, xn]]
        turned = {}

        def turn_x(q):
            if q >= 32 and not more:
                return
            i, z = q % 3, q % 2
            got = []
            v = XG[i][:, :].rearrange("p (f k) -> p k f", k=KT)
            for half in range(2):
                b = 2 + half
                for k in range(4):
                    t = P.tr(ps[:, b, 128 * k:128 * k + 128], v[:, 4 * half + k], ident, [gathered[q], bfree[b]], k == 3)
                o, x = ps[:, b], XT[:, z, 4 * half:4 * half + 4].rearrange("p k r -> p (k r)")
                t1 = P.cp(dve, x, o, [t, xfree[z]]) if half else P.a(x, o, ACT.Copy, [t, xfree[z]])
                bfree[b] = [t1]
                got.append(t1)
            gfree[i] = [t]
            turned[q] = got

        hfree = [[], []]
        ofree = [[sent, th, tx, xn], [sent, th, tx, xn]]
        hidden = {}

        def gate_up(i):
            q, z, r = i // 2, i // 2 % 2, slice(64 * (i % 2), 64 * (i % 2) + 64)
            b = i % 2
            for part in range(2):
                wv, tw, done = E.next()
                wv = wv[:, :].rearrange("p (k n) -> p k n", k=KT)
                for m in range(2):
                    o = ps[:, b, 128 * part + 64 * m:128 * part + 64 * m + 64]
                    for k in range(KT):
                        t = P.mm(o, wv[:, k, 128 * m:128 * m + 128], XT[:, z, k, r], k == 0, k == KT - 1,
                                 [tw, bfree[b], turned[q]], m == 1 and k == KT - 1)
                done(t)
            xfree[z] = [t]
            g = ps[:, b, 0:128].rearrange("p (m r) -> p m r", m=2)
            u = ps[:, b, 128:256].rearrange("p (m r) -> p m r", m=2)
            ts = P.a(SIL[:, b], g, ACT.Silu, [t, hfree[b]])
            hidden[i] = P.tt(dve, HID2[:, b], u, SIL[:, b], MUL, [ts, t, hfree[b]])
            bfree[b] = [hidden[i]]

        def down(i):
            q, z, r = i // 2, i // 2 % 2, slice(64 * (i % 2), 64 * (i % 2) + 64)
            wv, tw, done = E.next()
            wv = wv[:, :].rearrange("p (j n) -> p j n", j=2)
            for c_ in range(2):
                b = 4 + 2 * z + c_
                for j in range(2):
                    t = P.mm(ps[r, b], HID2[:, i % 2, j], wv[:, j, 512 * c_:512 * c_ + 512], j == 0, j == 1,
                             [tw, hidden[i], bfree[b]], j == 1)
                if i % 2:
                    n = slice(512 * c_, 512 * c_ + 512)
                    to = P.cp(dve, OUTB[:, z, n], ps[:, b], [t, ofree[z]]) if c_ else P.a(OUTB[:, z, n], ps[:, b], ACT.Copy, [t, ofree[z]])
                    bfree[b] = [to]
                    pool.wait(to)
            done(t)
            hfree[i % 2] = [t]
            if i % 2:
                sem = s_oy if more else s_ox[z]
                ofree[z] = [P.counted_up(pool, sem, bool(more))]
                pool.list.append(lambda e: e.indirect_dma_start(
                    out=otok, out_offset=bass.IndirectOffsetOnAxis(ap=DST[:, q:q + 1], axis=0),
                    in_=OUTB[:, z], in_offset=None, bounds_check=2 * S - 1, oob_is_err=False).then_inc(sem, 16))
                if more:
                    ofree[z] = [P.memset(pool, MARK[:, q:q + 1], 0.0, [ofree[z]])]

        more = []
        gather(0)
        gather(1)
        turn_x(0)
        for i in range(65):
            if i < 64:
                if i % 2 == 0 and i < 62:
                    gather(i // 2 + 2)
                gate_up(i)
                if i % 2:
                    turn_x(i // 2 + 1)
            if i > 0:
                down(i - 1)
        first_sent = [ofree[0], ofree[1]]
        more.append(True)
        over_ = P.counted(OVI[0:1, NOV:NOV + 1], NOV, [t_ov])
        for q in range(32, NP):
            with P.when(over_, 2 * (q - 32)):
                E.load(6 * q + 6)
                gather(q + 1)
                turn_x(q)
                gate_up(2 * q)
                gate_up(2 * q + 1)
                down(2 * q)
                down(2 * q + 1)
                pool.wait(gathered.get(q + 1))
        P.barrier()
        OT, y = P.place("OT", [128, 2, 4, D], F32, xs0)
        s_out = P.sem("s_out")
        got = [P.dma(sp, OT[:, :, n, :], otok.rearrange("(s n p) d -> n p s d", s=2, p=128)[n], P.sem(f"s_ot{n}"),
                     [first_sent, ofree[0], ofree[1]]) for n in range(4)]
        for n in range(4):
            t = P.stt(HT[:, n], OT[:, 0, n], GATES[:, 0, n:n + 1], HT[:, n], MUL, ADD, [got[n]])
            t = P.stt(HT[:, n], OT[:, 1, n], GATES[:, 1, n:n + 1], HT[:, n], MUL, ADD, [t])
            P.dma(sp, out[128 * n:128 * n + 128, :], HT[:, n], s_out, [t], store=True)
        P.stores += [first_sent[0][0], first_sent[1][0]]
        P.run()



def packed(w, mt, order=None):
    k, n = w.shape
    a = w.reshape(k // 128, 128, n // 128, 128).transpose(2, 1, 0, 3)
    if order is not None:
        a = a[order]
    return np.ascontiguousarray(a.reshape(n // 128 // mt, mt, 128, k).transpose(0, 2, 1, 3).reshape(-1, 128, mt * k))


def packed_tok(w, cols):
    k, n = w.shape
    a = w.reshape(k // 128, 128, n // cols, cols).transpose(2, 1, 0, 3)
    return np.ascontiguousarray(a.reshape(n // cols, 128, k // 128 * cols))


def column(v):
    return np.ascontiguousarray(v.reshape(-1, 128).T)


def wide(w, n, at=0):
    out = np.zeros((w.shape[0], n), w.dtype)
    out[:, at:at + w.shape[1]] = w
    return out


def layout(i):
    g = {k: np.asarray(v) for k, v in i.items()}
    a = {}
    pc = param_columns()
    prm = np.zeros((128, pc["n"]), np.float32)

    def put(name, v, at=0):
        prm[:, pc[name] + at:pc[name] + at + v.shape[1]] = v

    for l in range(2):
        put("mixg", column(g["norm_mix_g"][l]), 8 * l)
        put("ffng", column(g["norm_ffn_g"][l]), 8 * l)
        for j in range(3):
            put("cw", column(g["ffn_conv_w"][l, j]), (3 * l + j) * 44)
        put("cb", column(g["ffn_conv_b"][l]), 44 * l)
    put("fing", column(g["norm_final_g"]))
    put("ln1", column(g["ln1_g_2"][0]))
    put("ln2", column(g["ln2_g_2"][0]))
    put("bu", column(g["sgu_b_in"][0, :D]))
    for j in range(6):
        put("mu", column(g["rwkv_mu"][0, j]), 8 * j)
    for name, key in (("w0", "rwkv_w0"), ("a0", "rwkv_a0"), ("kk", "rwkv_k_k"), ("ka", "rwkv_k_a"),
                      ("lnw", "rwkv_ln_w"), ("lnb", "rwkv_ln_b")):
        put(name, column(g[key][0]))
    put("rk", column(g["rwkv_r_k"][0].reshape(-1)))
    for j in range(5):
        put("dncw", column(g["dn_conv_w_2"][0, j]), 12 * j)
    put("qg", np.concatenate([g["attn_q_norm_g_2"][0]] * 2)[:, None])
    put("kg", np.concatenate([g["attn_k_norm_g_2"][0]] * 2)[:, None])
    put("aog", column(g["attn_out_norm_g_2"][0]))
    put("dng", g["dn_out_norm_g_2"][0][:, None])
    put("eps", np.full((128, 1), 1e-6))
    put("gneps", np.full((128, 1), 64e-5))
    put("one", np.ones((128, 1)))
    a["params"] = prm
    a["consts"] = constants()
    a["sel"] = ((np.arange(D) // 64)[None] == np.arange(16)[:, None]).astype(np.float32)
    a["x"] = np.ascontiguousarray(g["x"][0].T)
    w = g["sgu_w_in"][0]
    a["sgu_u"] = packed(w[:, :D], 2)
    a["sgu_v"] = packed_tok(w[:, D:], 256)
    a["sgu_o"] = packed(g["sgu_w_out"][0], 2)
    a["sgu_ws"] = np.ascontiguousarray(g["sgu_w_s"][0].transpose(2, 0, 1))
    a["sgu_rows"] = np.ascontiguousarray(np.broadcast_to(np.stack([g["sgu_b_in"][0, D:], g["sgu_g_v"][0]])[None], (128, 2, D)))
    a["sgu_bs"] = g["sgu_b_s"][0]
    pairs = [f + h * FT for f in range(FT) for h in range(2)]
    for l in range(2):
        a[f"up{l}"] = packed(g["ffn_w_up"][l], 2, pairs)
        d = packed(g["ffn_w_down"][l], 1)
        a[f"down{l}"] = np.ascontiguousarray(d.reshape(8, 128, 2, 1408).transpose(0, 2, 1, 3).reshape(16, 128, 1408))
    g1 = g["rwkv_g1"][0]
    a["lora1"] = np.concatenate([packed(x, 1) for x in (
        wide(g["rwkv_w1"][0], 128), wide(g["rwkv_a1"][0], 128, 64), g1[:, :128], wide(g1[:, 128:], 128))])
    lora2 = np.zeros((2, 128, 2048), np.float32)
    lora2[0, :64, :D] = g["rwkv_w2"][0]
    lora2[0, 64:, :D] = g["rwkv_a2"][0]
    lora2[1, :, :D] = g["rwkv_g2"][0][:128]
    lora2[1, :32, D:] = g["rwkv_g2"][0][128:]
    a["lora2"] = lora2
    a["rwkv_rkv"] = np.concatenate([packed(g[x][0], 2) for x in ("rwkv_w_r", "rwkv_w_k", "rwkv_w_v")])
    a["rwkv_o"] = packed(g["rwkv_w_o"][0], 2)
    w = g["w_in_2"][0]
    a["in2_qk"] = packed(w[:, :1024], 2)
    a["in2_v"] = packed_tok(w[:, 1024:1536], 256)
    a["in2_dn"] = packed(w[:, 1536:3584], 2)
    a["in2_ab"] = packed(np.concatenate([w[:, 3584:], np.zeros((D, 112), np.float32)], 1), 1)
    a["out2"] = packed(g["w_out_2"][0], 2)
    rpb = np.full((64, 8, 15, 64), -1e30, np.float32)
    for c in range(64):
        lo = min(max(c - 8, 0), 48)
        rpb[c, :, :, lo:lo + 16] = g["attn_rpb_2"][0][:, :, lo - c + 15:lo - c + 31]
    a["rpb"] = rpb
    a["rows8"] = np.ascontiguousarray(np.broadcast_to(
        np.stack([g["dn_dt_bias_2"][0].reshape(8), g["dn_a_log_2"][0].reshape(8)])[None], (128, 2, 8)))
    r = np.concatenate([g["router_group_w_2"][0], g["router_expert_w_2"][0]], 1)
    a["router_w"] = np.ascontiguousarray(r.reshape(8, 128, 72).transpose(1, 0, 2).reshape(128, 576))
    a["router_b"] = np.ascontiguousarray(np.broadcast_to(
        np.concatenate([g["router_group_b_2"][0], g["router_expert_b_2"][0]])[None], (128, 72)))
    for name in ("gate", "up", "down"):
        a[f"e_{name}"] = g[f"expert_w_{name}_2"][0]
    return a


def kernel(**inputs):
    import concourse.bacc as bacc
    from concourse.bass_utils import run_bass_kernel_spmd

    arrays = layout(inputs)
    nc = bacc.Bacc("TRN2", target_bir_lowering=False, num_devices=1)
    A = {k: nc.dram_tensor(k, list(v.shape), F32, kind="ExternalInput").ap() for k, v in arrays.items()}
    out = nc.dram_tensor("out", [S, D], F32, kind="ExternalOutput").ap()
    build(nc, A, out)
    r = run_bass_kernel_spmd(nc, [arrays], core_ids=[0])
    return r.results[0]["out"].reshape(1, S, D)
```
